# Optimizing a Trainium2 kernel written in Bass

```python
import jax
import jax.numpy as jnp
from jax import lax
import numpy as np
import math
import jax, jax.numpy as jnp

D_MODEL = 1024
BATCH = 1
SEQ = 512
DEPTH = 1

GRID_W = 64
CTX_LEN = 256
CTX_CHUNK = 64
N_MOD = 6
EPS = 1e-6

HG_HEADS = 8
HG_HEAD_K = 128
HG_HEAD_V = D_MODEL // HG_HEADS
HG_KEY = HG_HEADS * HG_HEAD_K
HG_VAL = HG_HEADS * HG_HEAD_V

GLA_HEADS = 4
GLA_KEY = D_MODEL // 2
GLA_VAL = D_MODEL
GLA_HEAD_K = GLA_KEY // GLA_HEADS
GLA_HEAD_V = GLA_VAL // GLA_HEADS
GLA_GATE_RANK = 16
GLA_GATE_NORMALIZER = 16.0

IN_SIZES = (HG_KEY, HG_KEY, HG_KEY, HG_VAL, HG_VAL,
            GLA_KEY, GLA_KEY, GLA_VAL, GLA_VAL, GLA_GATE_RANK, GLA_GATE_RANK,
            D_MODEL, D_MODEL)
D_IN = 3 * HG_KEY + 2 * HG_VAL + 2 * GLA_KEY + 2 * GLA_VAL + 2 * GLA_GATE_RANK + 2 * D_MODEL

PEER_HEADS = 8
PEER_N_KEYS = 128
PEER_EXPERTS = PEER_N_KEYS * PEER_N_KEYS
PEER_QUERY_DIM = 256
PEER_SUB_DIM = PEER_QUERY_DIM // 2
PEER_TOPK = 16
PEER_BLOCK = 128


def rmsnorm(x, g):
    xf = x.astype(jnp.float32)
    xf = xf * lax.rsqrt(jnp.mean(xf * xf, axis=-1, keepdims=True) + EPS)
    return (xf * g.astype(jnp.float32)).astype(x.dtype)

def modulate(h, shift, scale):
    return h * (1.0 + scale) + shift

def to_heads(a, n_heads):
    bsz, t, _ = a.shape
    return a.reshape(bsz, t, n_heads, -1).transpose(0, 2, 1, 3)

def flip_t(a):
    return a[:, :, ::-1]

def hgrn_lower_bounds(logits):
    p = jax.nn.softmax(logits.astype(jnp.float32), axis=0)
    return jnp.cumsum(p, axis=0)[:DEPTH]

def hgrn_forget(z, lb):
    f = lb + (1.0 - lb) * jax.nn.sigmoid(z.astype(jnp.float32))
    return 1.0 - f, jnp.log(f)

def chunk_gla(q, k, v, log_g, s0, n_chunks):
    bsz, nh, t, _ = q.shape
    dv = v.shape[-1]
    chunk = t // n_chunks

    def blocks(a):
        return jnp.moveaxis(a.reshape(bsz, nh, n_chunks, chunk, a.shape[-1]), 2, 0)

    qc, kc, vc = blocks(q), blocks(k), blocks(v)
    b = jnp.cumsum(blocks(log_g).astype(jnp.float32), axis=3)
    b_last = b[:, :, :, chunk - 1:chunk]
    b_ref = b[:, :, :, chunk // 2:chunk // 2 + 1]
    scores = jnp.einsum("nbhck,nbhsk->nbhcs", qc * jnp.exp(b - b_ref), kc * jnp.exp(b_ref - b))
    causal_in_scan = jnp.tril(jnp.ones((chunk, chunk), dtype=bool))
    o_intra = jnp.einsum("nbhcs,nbhsv->nbhcv", jnp.where(causal_in_scan, scores, 0.0), vc)
    q_dec = qc * jnp.exp(b)
    k_dec = kc * jnp.exp(b_last - b)

    def step(state, inp):
        q_i, k_i, v_i, bl = inp
        o_inter = jnp.einsum("bhck,bhkv->bhcv", q_i, state)
        state = jnp.exp(bl)[:, :, 0, :, None] * state + jnp.einsum("bhsk,bhsv->bhkv", k_i, v_i)
        return state, o_inter

    _, o_inter = lax.scan(step, s0, (q_dec, k_dec, vc, b_last))
    o = o_intra + o_inter
    return jnp.moveaxis(o, 0, 2).reshape(bsz, nh, t, dv)

def final_state(k, v, log_g):
    b = jnp.cumsum(log_g.astype(jnp.float32), axis=2)
    return jnp.einsum("bhtk,bhtv->bhkv", k * jnp.exp(b[:, :, -1:] - b), v)

def mixer_inputs(h, w_in, lb, gk_w, gk_b):
    splits = [int(s) for s in np.cumsum(IN_SIZES)[:-1]]
    (hq, hf_fwd, hf_bwd, hi, hg, gq, gk, gv, gg, gr_fwd, gr_bwd, m_hg, m_gla) = jnp.split(
        h @ w_in, splits, axis=-1)
    hk_fwd, hlf_fwd = hgrn_forget(hf_fwd, lb[0])
    hk_bwd, hlf_bwd = hgrn_forget(hf_bwd, lb[1])
    glf_fwd = jax.nn.log_sigmoid((gr_fwd @ gk_w[0] + gk_b[0]).astype(jnp.float32)) / GLA_GATE_NORMALIZER
    glf_bwd = jax.nn.log_sigmoid((gr_bwd @ gk_w[1] + gk_b[1]).astype(jnp.float32)) / GLA_GATE_NORMALIZER
    gla_k = to_heads(gk, GLA_HEADS)
    return {
        "hg_q": to_heads(hq, HG_HEADS) * HG_HEAD_K ** -0.5,
        "hg_v": to_heads(hi, HG_HEADS),
        "hg_k": (to_heads(hk_fwd, HG_HEADS), to_heads(hk_bwd, HG_HEADS)),
        "hg_lg": (to_heads(hlf_fwd, HG_HEADS), to_heads(hlf_bwd, HG_HEADS)),
        "hg_gate": hg,
        "gla_q": to_heads(gq, GLA_HEADS) * GLA_HEAD_K ** -0.5,
        "gla_v": to_heads(gv, GLA_HEADS),
        "gla_k": (gla_k, gla_k),
        "gla_lg": (to_heads(glf_fwd, GLA_HEADS), to_heads(glf_bwd, GLA_HEADS)),
        "gla_gate": gg,
        "merge": (m_hg, m_gla),
    }

def context_states(t):
    def both(k_pair, v, lg_pair):
        return (final_state(k_pair[0], v, lg_pair[0]),
                final_state(flip_t(k_pair[1]), flip_t(v), flip_t(lg_pair[1])))
    return {"hg": both(t["hg_k"], t["hg_v"], t["hg_lg"]),
            "gla": both(t["gla_k"], t["gla_v"], t["gla_lg"])}

def zero_states(bsz):
    hg = jnp.zeros((bsz, HG_HEADS, HG_HEAD_K, HG_HEAD_V), jnp.float32)
    gla = jnp.zeros((bsz, GLA_HEADS, GLA_HEAD_K, GLA_HEAD_V), jnp.float32)
    return {"hg": (hg, hg), "gla": (gla, gla)}

def bidir(q, k_pair, v, lg_pair, s_pair, n_chunks):
    o_fwd = chunk_gla(q, k_pair[0], v, lg_pair[0], s_pair[0], n_chunks)
    o_bwd = chunk_gla(flip_t(q), flip_t(k_pair[1]), flip_t(v), flip_t(lg_pair[1]), s_pair[1], n_chunks)
    return o_fwd + flip_t(o_bwd)

def gated_head_norm(o, gate, g):
    bsz, nh, t, dv = o.shape
    on = rmsnorm(o.transpose(0, 2, 1, 3), g)
    y = on * jax.nn.silu(gate.astype(jnp.float32)).reshape(bsz, t, nh, dv)
    return y.reshape(bsz, t, nh * dv).astype(gate.dtype)

def mixer_output(t, states, n_chunks, hg_norm_g, gla_norm_g, w_br_hg, w_br_gla, w_o):
    o_hg = bidir(t["hg_q"], t["hg_k"], t["hg_v"], t["hg_lg"], states["hg"], n_chunks)
    o_gla = bidir(t["gla_q"], t["gla_k"], t["gla_v"], t["gla_lg"], states["gla"], n_chunks)
    y_hg = gated_head_norm(o_hg, t["hg_gate"], hg_norm_g) @ w_br_hg
    y_gla = gated_head_norm(o_gla, t["gla_gate"], gla_norm_g) @ w_br_gla
    m_hg, m_gla = t["merge"]
    y = jax.nn.sigmoid(m_hg) * y_hg + jax.nn.sigmoid(m_gla) * y_gla
    return y @ w_o

def peer(h, wq, k1, k2, u, v):
    bsz, t, d = h.shape
    tok = h.reshape(bsz * t, d)
    q = (tok @ wq).reshape(-1, PEER_HEADS, 2, PEER_SUB_DIM)
    s1 = jnp.einsum("nhd,kd->nhk", q[:, :, 0], k1).astype(jnp.float32)
    s2 = jnp.einsum("nhd,kd->nhk", q[:, :, 1], k2).astype(jnp.float32)
    v1, i1 = lax.top_k(s1, PEER_TOPK)
    v2, i2 = lax.top_k(s2, PEER_TOPK)
    cand = (v1[..., :, None] + v2[..., None, :]).reshape(-1, PEER_HEADS, PEER_TOPK * PEER_TOPK)
    top_s, top_c = lax.top_k(cand, PEER_TOPK)
    expert = (jnp.take_along_axis(i1, top_c // PEER_TOPK, axis=-1) * PEER_N_KEYS
              + jnp.take_along_axis(i2, top_c % PEER_TOPK, axis=-1))
    gate = jax.nn.softmax(top_s, axis=-1)
    n_sel = PEER_HEADS * PEER_TOPK

    def expert_block(args):
        xb, eb, gb = args
        act = jax.nn.gelu(jnp.einsum("pd,ped->pe", xb, jnp.take(u, eb, axis=0)), approximate=False)
        return jnp.einsum("pe,ped->pd", (gb * act).astype(v.dtype), jnp.take(v, eb, axis=0))

    out = lax.map(expert_block, (tok.reshape(-1, PEER_BLOCK, d),
                                 expert.reshape(-1, PEER_BLOCK, n_sel),
                                 gate.reshape(-1, PEER_BLOCK, n_sel)))
    return out.reshape(bsz, t, d).astype(h.dtype)

def first_inputs(seed: int = 0) -> dict:
    key = jax.random.key(seed)
    ks = jax.random.split(key, 24)

    def nrm(k, shape, scale):
        return jax.random.normal(k, shape, jnp.float32) * scale

    def gain(k, shape):
        return 1.0 + 0.1 * jax.random.normal(k, shape, jnp.float32)

    return {
        "x": nrm(ks[0], (BATCH, SEQ, D_MODEL), 1.0),
        "c": nrm(ks[1], (BATCH, D_MODEL), 1.0),
        "ctx": nrm(ks[2], (BATCH, CTX_LEN, D_MODEL), 1.0),
        "c_ctx": nrm(ks[3], (D_MODEL,), 1.0),
        "ada_w": nrm(ks[4], (DEPTH, D_MODEL, N_MOD * D_MODEL), 0.5 * D_MODEL ** -0.5),
        "ada_b": nrm(ks[5], (DEPTH, N_MOD * D_MODEL), 0.02),
        "norm_mix_g": gain(ks[6], (DEPTH, D_MODEL)),
        "w_in": nrm(ks[7], (DEPTH, D_MODEL, D_IN), D_MODEL ** -0.5),
        "hgrn_lb_logits": nrm(ks[8], (DEPTH + 1, 2, HG_KEY), 0.5),
        "hgrn_norm_g": gain(ks[9], (DEPTH, HG_HEAD_V)),
        "gla_gk_w": nrm(ks[10], (DEPTH, 2, GLA_GATE_RANK, GLA_KEY), GLA_GATE_RANK ** -0.5),
        "gla_gk_b": nrm(ks[11], (DEPTH, 2, GLA_KEY), 0.1),
        "gla_norm_g": gain(ks[12], (DEPTH, GLA_HEAD_V)),
        "w_branch_hgrn": nrm(ks[13], (DEPTH, HG_VAL, D_MODEL), HG_VAL ** -0.5),
        "w_branch_gla": nrm(ks[14], (DEPTH, GLA_VAL, D_MODEL), GLA_VAL ** -0.5),
        "w_out": nrm(ks[15], (DEPTH, D_MODEL, D_MODEL), D_MODEL ** -0.5),
        "norm_ffn_g": gain(ks[16], (DEPTH, D_MODEL)),
        "peer_wq": nrm(ks[17], (DEPTH, D_MODEL, PEER_HEADS * PEER_QUERY_DIM), D_MODEL ** -0.5),
        "peer_k1": nrm(ks[18], (DEPTH, PEER_N_KEYS, PEER_SUB_DIM), PEER_SUB_DIM ** -0.5),
        "peer_k2": nrm(ks[19], (DEPTH, PEER_N_KEYS, PEER_SUB_DIM), PEER_SUB_DIM ** -0.5),
        "peer_u": nrm(ks[20], (DEPTH, PEER_EXPERTS, D_MODEL), D_MODEL ** -0.5),
        "peer_v": nrm(ks[21], (DEPTH, PEER_EXPERTS, D_MODEL), (PEER_HEADS * PEER_TOPK) ** -0.5),
        "final_g": gain(ks[22], (D_MODEL,)),
    }

def first_block(x, c, ctx, c_ctx, ada_w, ada_b, norm_mix_g, w_in, hgrn_lb_logits, hgrn_norm_g,
              gla_gk_w, gla_gk_b, gla_norm_g, w_branch_hgrn, w_branch_gla, w_out, norm_ffn_g,
              peer_wq, peer_k1, peer_k2, peer_u, peer_v, final_g):
    bsz, seq, _ = x.shape
    rows = seq // GRID_W
    ctx_chunks = ctx.shape[1] // CTX_CHUNK
    lower = hgrn_lower_bounds(hgrn_lb_logits)
    silu_c = jax.nn.silu(c)
    silu_cc = jax.nn.silu(c_ctx)[None]
    xc = ctx
    for l in range(DEPTH):
        mod = jnp.split((silu_c @ ada_w[l] + ada_b[l])[:, None, :], N_MOD, axis=-1)
        mod_c = jnp.split((silu_cc @ ada_w[l] + ada_b[l])[:, None, :], N_MOD, axis=-1)
        mix_w = (hgrn_norm_g[l], gla_norm_g[l], w_branch_hgrn[l], w_branch_gla[l], w_out[l])
        peer_w = (peer_wq[l], peer_k1[l], peer_k2[l], peer_u[l], peer_v[l])
        t_ctx = mixer_inputs(modulate(rmsnorm(xc, norm_mix_g[l]), mod_c[0], mod_c[1]),
                             w_in[l], lower[l], gla_gk_w[l], gla_gk_b[l])
        t_lat = mixer_inputs(modulate(rmsnorm(x, norm_mix_g[l]), mod[0], mod[1]),
                             w_in[l], lower[l], gla_gk_w[l], gla_gk_b[l])
        x = x + mod[2] * mixer_output(t_lat, context_states(t_ctx), rows, *mix_w)
        x = x + mod[5] * peer(modulate(rmsnorm(x, norm_ffn_g[l]), mod[3], mod[4]), *peer_w)
        if l < DEPTH - 1:
            xc = xc + mod_c[2] * mixer_output(t_ctx, zero_states(bsz), ctx_chunks, *mix_w)
            xc = xc + mod_c[5] * peer(modulate(rmsnorm(xc, norm_ffn_g[l]), mod_c[3], mod_c[4]), *peer_w)
    return rmsnorm(x, final_g)


DEPTH_2 = 2

N_MIXERS = 2
N_MLA = (DEPTH_2 + 1) // 2
N_SSM = DEPTH_2 // 2
MLA_HEADS = 8
QK_NOPE = 128
QK_ROPE = 64
V_DIM = 128
Q_LORA = 256
KV_LORA = 128
ROPE_THETA = 10000.0
Q_BLOCK = 128
SSM_WIDTH = D_MODEL
GROUP_CH = 16
N_GROUPS = SSM_WIDTH // GROUP_CH
STATE = 64
DT_MIN = 0.001
DT_MAX = 0.1
D_FF = 4 * D_MODEL
ALPHA = (2 * DEPTH_2) ** 0.25
BETA = (8 * DEPTH_2) ** -0.25
LN_EPS = 1e-5
RMS_EPS = 1e-6


def layer_norm(x, g, b):
    xf = x.astype(jnp.float32)
    mu = jnp.mean(xf, axis=-1, keepdims=True)
    var = jnp.mean(jnp.square(xf - mu), axis=-1, keepdims=True)
    y = (xf - mu) * lax.rsqrt(var + LN_EPS) * g.astype(jnp.float32) + b.astype(jnp.float32)
    return y.astype(x.dtype)

def rms_norm(x, g):
    xf = x.astype(jnp.float32)
    y = xf * lax.rsqrt(jnp.mean(jnp.square(xf), axis=-1, keepdims=True) + RMS_EPS) * g.astype(jnp.float32)
    return y.astype(x.dtype)

def rope_tables(positions):
    inv_freq = ROPE_THETA ** (-jnp.arange(0, QK_ROPE, 2, dtype=jnp.float32) / QK_ROPE)
    ang = positions.astype(jnp.float32)[..., None] * inv_freq
    return jnp.cos(ang), jnp.sin(ang)

def apply_rope(x, cos, sin):
    xf = x.astype(jnp.float32)
    x1, x2 = jnp.split(xf, 2, axis=-1)
    return jnp.concatenate([x1 * cos - x2 * sin, x1 * sin + x2 * cos], axis=-1).astype(x.dtype)

def mla_mixer(h, cos, sin, w_in, q_norm, w_qb, kv_norm, w_kvb, w_o):
    B, L, _ = h.shape
    z = h @ w_in
    cq = rms_norm(z[..., :Q_LORA], q_norm)
    ckv = rms_norm(z[..., Q_LORA:Q_LORA + KV_LORA], kv_norm)
    k_pe = apply_rope(z[..., Q_LORA + KV_LORA:], cos, sin)
    q = (cq @ w_qb).reshape(B, L, MLA_HEADS, QK_NOPE + QK_ROPE)
    q_nope = q[..., :QK_NOPE]
    q_pe = apply_rope(q[..., QK_NOPE:], cos[:, :, None, :], sin[:, :, None, :])
    kv = (ckv @ w_kvb).reshape(B, L, MLA_HEADS, QK_NOPE + V_DIM)
    k_nope = kv[..., :QK_NOPE]
    v = kv[..., QK_NOPE:]
    scale = 1.0 / math.sqrt(QK_NOPE + QK_ROPE)
    nb = L // Q_BLOCK
    qn_b = q_nope.reshape(B, nb, Q_BLOCK, MLA_HEADS, QK_NOPE).transpose(1, 0, 2, 3, 4)
    qp_b = q_pe.reshape(B, nb, Q_BLOCK, MLA_HEADS, QK_ROPE).transpose(1, 0, 2, 3, 4)
    k_idx = jnp.arange(L)

    def attend(args):
        qn, qp, start = args
        s = (jnp.einsum('bqhd,bkhd->bhqk', qn, k_nope)
             + jnp.einsum('bqhr,bkr->bhqk', qp, k_pe)).astype(jnp.float32) * scale
        q_idx = start + jnp.arange(Q_BLOCK)
        causal = k_idx[None, :] <= q_idx[:, None]
        s = jnp.where(causal, s, jnp.float32(-1e30))
        p = jax.nn.softmax(s, axis=-1).astype(v.dtype)
        return jnp.einsum('bhqk,bkhd->bqhd', p, v)

    o = lax.map(attend, (qn_b, qp_b, jnp.arange(nb) * Q_BLOCK))
    o = o.transpose(1, 0, 2, 3, 4).reshape(B, L, MLA_HEADS * V_DIM)
    return o @ w_o

def s5_mixer(h, w_in, log_dt, a_re, a_im, b_re, b_im, c_re, c_im, d_skip, w_glu, b_glu, w_out):
    B, L, _ = h.shape
    u = h @ w_in
    u32 = u.astype(jnp.float32).reshape(B, L, N_GROUPS, GROUP_CH)
    lr = a_re.astype(jnp.float32)
    li = a_im.astype(jnp.float32)
    dt = jnp.exp(log_dt.astype(jnp.float32))[:, None]
    mag = jnp.exp(lr * dt)
    ab_re = mag * jnp.cos(li * dt)
    ab_im = mag * jnp.sin(li * dt)
    den = lr * lr + li * li
    nr = ab_re - 1.0
    coef_re = ((nr * lr + ab_im * li) / den)[..., None]
    coef_im = ((ab_im * lr - nr * li) / den)[..., None]
    br = b_re.astype(jnp.float32)
    bi = b_im.astype(jnp.float32)
    bb_re = coef_re * br - coef_im * bi
    bb_im = coef_re * bi + coef_im * br
    bu_re = jnp.einsum('blgc,gpc->blgp', u32, bb_re)
    bu_im = jnp.einsum('blgc,gpc->blgp', u32, bb_im)
    a_re_t = jnp.broadcast_to(ab_re, (1, L, N_GROUPS, STATE))
    a_im_t = jnp.broadcast_to(ab_im, (1, L, N_GROUPS, STATE))

    def combine(e1, e2):
        a1r, a1i, b1r, b1i = e1
        a2r, a2i, b2r, b2i = e2
        return (a2r * a1r - a2i * a1i,
                a2r * a1i + a2i * a1r,
                a2r * b1r - a2i * b1i + b2r,
                a2r * b1i + a2i * b1r + b2i)

    _, _, xr, xi = lax.associative_scan(combine, (a_re_t, a_im_t, bu_re, bu_im), axis=1)
    y = (jnp.einsum('blgp,gcp->blgc', xr, c_re.astype(jnp.float32))
         - jnp.einsum('blgp,gcp->blgc', xi, c_im.astype(jnp.float32)))
    y = y + d_skip.astype(jnp.float32).reshape(N_GROUPS, GROUP_CH) * u32
    y = y.reshape(B, L, SSM_WIDTH).astype(h.dtype)
    g = jax.nn.gelu(y)
    z = g * jax.nn.sigmoid(g @ w_glu + b_glu)
    return z @ w_out

def sq_relu_mlp(h, w1, b1, w2, b2):
    a = jax.nn.relu(h @ w1 + b1)
    return (a * a) @ w2 + b2

def modulation(cs, w, b):
    m = cs @ w + b
    shift, scale, gate = jnp.split(m, 3, axis=-1)
    return shift[:, None, :], scale[:, None, :], gate[:, None, :]

def second_inputs(seed: int = 0) -> dict:
    key = jax.random.key(seed)
    ks = iter(jax.random.split(key, 40))
    f32 = jnp.float32
    nrm = lambda shape, s: jax.random.normal(next(ks), shape, f32) * s
    D = D_MODEL
    x = jax.random.normal(next(ks), (BATCH, SEQ, D), f32)
    c = jax.random.normal(next(ks), (BATCH, D), f32)
    offs = jax.random.randint(next(ks), (BATCH, 1), 0, 1024, dtype=jnp.int32)
    positions = offs + jnp.arange(SEQ, dtype=jnp.int32)[None, :]
    mla_w_in = nrm((N_MLA, D, Q_LORA + KV_LORA + QK_ROPE), D ** -0.5)
    mla_q_norm = 1.0 + nrm((N_MLA, Q_LORA), 0.02)
    mla_w_qb = nrm((N_MLA, Q_LORA, MLA_HEADS * (QK_NOPE + QK_ROPE)), Q_LORA ** -0.5)
    mla_kv_norm = 1.0 + nrm((N_MLA, KV_LORA), 0.02)
    mla_w_kvb = nrm((N_MLA, KV_LORA, MLA_HEADS * (QK_NOPE + V_DIM)), KV_LORA ** -0.5)
    mla_w_o = nrm((N_MLA, MLA_HEADS * V_DIM, D), BETA * (MLA_HEADS * V_DIM) ** -0.5)
    ssm_w_in = nrm((N_SSM, D, SSM_WIDTH), D ** -0.5)
    ssm_log_dt = jax.random.uniform(next(ks), (N_SSM, N_GROUPS), f32,
                                    math.log(DT_MIN), math.log(DT_MAX))
    n_idx = jnp.arange(STATE, dtype=f32)
    ssm_a_re = -0.5 + nrm((N_SSM, N_GROUPS, STATE), 0.01)
    ssm_a_im = math.pi * n_idx + nrm((N_SSM, N_GROUPS, STATE), 0.01)
    ssm_b_re = nrm((N_SSM, N_GROUPS, STATE, GROUP_CH), (2 * GROUP_CH) ** -0.5)
    ssm_b_im = nrm((N_SSM, N_GROUPS, STATE, GROUP_CH), (2 * GROUP_CH) ** -0.5)
    ssm_c_re = nrm((N_SSM, N_GROUPS, GROUP_CH, STATE), (2 * STATE) ** -0.5)
    ssm_c_im = nrm((N_SSM, N_GROUPS, GROUP_CH, STATE), (2 * STATE) ** -0.5)
    ssm_d = nrm((N_SSM, SSM_WIDTH), 1.0)
    ssm_w_glu = nrm((N_SSM, SSM_WIDTH, SSM_WIDTH), SSM_WIDTH ** -0.5)
    ssm_b_glu = nrm((N_SSM, SSM_WIDTH), 0.01)
    ssm_w_out = nrm((N_SSM, SSM_WIDTH, D), BETA * SSM_WIDTH ** -0.5)
    mlp_w1 = nrm((DEPTH_2, D, D_FF), D ** -0.5)
    mlp_b1 = nrm((DEPTH_2, D_FF), 0.01)
    mlp_w2 = nrm((DEPTH_2, D_FF, D), BETA * D_FF ** -0.5)
    mlp_b2 = nrm((DEPTH_2, D), 0.01)
    mod_mix_w = nrm((DEPTH_2, D, 3 * D), 0.2 * D ** -0.5)
    mod_mix_b = nrm((DEPTH_2, 3 * D), 0.01)
    mod_ffn_w = nrm((DEPTH_2, D, 3 * D), 0.2 * D ** -0.5)
    mod_ffn_b = nrm((DEPTH_2, 3 * D), 0.01)
    ln_mix_g = 1.0 + nrm((DEPTH_2, D), 0.02)
    ln_mix_b = nrm((DEPTH_2, D), 0.01)
    ln_ffn_g = 1.0 + nrm((DEPTH_2, D), 0.02)
    ln_ffn_b = nrm((DEPTH_2, D), 0.01)
    return {"x": x, "c": c, "positions": positions,
            "mla_w_in": mla_w_in, "mla_q_norm": mla_q_norm, "mla_w_qb": mla_w_qb,
            "mla_kv_norm": mla_kv_norm, "mla_w_kvb": mla_w_kvb, "mla_w_o": mla_w_o,
            "ssm_w_in": ssm_w_in, "ssm_log_dt": ssm_log_dt, "ssm_a_re": ssm_a_re,
            "ssm_a_im": ssm_a_im, "ssm_b_re": ssm_b_re, "ssm_b_im": ssm_b_im,
            "ssm_c_re": ssm_c_re, "ssm_c_im": ssm_c_im, "ssm_d": ssm_d,
            "ssm_w_glu": ssm_w_glu, "ssm_b_glu": ssm_b_glu, "ssm_w_out": ssm_w_out,
            "mlp_w1": mlp_w1, "mlp_b1": mlp_b1, "mlp_w2": mlp_w2, "mlp_b2": mlp_b2,
            "mod_mix_w": mod_mix_w, "mod_mix_b": mod_mix_b,
            "mod_ffn_w": mod_ffn_w, "mod_ffn_b": mod_ffn_b,
            "ln_mix_g": ln_mix_g, "ln_mix_b": ln_mix_b,
            "ln_ffn_g": ln_ffn_g, "ln_ffn_b": ln_ffn_b}

def second_block(x, c, positions,
              mla_w_in, mla_q_norm, mla_w_qb, mla_kv_norm, mla_w_kvb, mla_w_o,
              ssm_w_in, ssm_log_dt, ssm_a_re, ssm_a_im, ssm_b_re, ssm_b_im,
              ssm_c_re, ssm_c_im, ssm_d, ssm_w_glu, ssm_b_glu, ssm_w_out,
              mlp_w1, mlp_b1, mlp_w2, mlp_b2,
              mod_mix_w, mod_mix_b, mod_ffn_w, mod_ffn_b,
              ln_mix_g, ln_mix_b, ln_ffn_g, ln_ffn_b):
    cs = jax.nn.silu(c)
    cos, sin = rope_tables(positions)
    for i in range(DEPTH_2):
        shift, scale, gate = modulation(cs, mod_mix_w[i], mod_mix_b[i])
        h = x * (1.0 + scale) + shift
        j = i // N_MIXERS
        if i % N_MIXERS == 0:
            y = mla_mixer(h, cos, sin, mla_w_in[j], mla_q_norm[j], mla_w_qb[j],
                          mla_kv_norm[j], mla_w_kvb[j], mla_w_o[j])
        else:
            y = s5_mixer(h, ssm_w_in[j], ssm_log_dt[j], ssm_a_re[j], ssm_a_im[j],
                         ssm_b_re[j], ssm_b_im[j], ssm_c_re[j], ssm_c_im[j], ssm_d[j],
                         ssm_w_glu[j], ssm_b_glu[j], ssm_w_out[j])
        x = layer_norm(ALPHA * x + (1.0 + gate) * y, ln_mix_g[i], ln_mix_b[i])
        shift, scale, gate = modulation(cs, mod_ffn_w[i], mod_ffn_b[i])
        h = x * (1.0 + scale) + shift
        y = sq_relu_mlp(h, mlp_w1[i], mlp_b1[i], mlp_w2[i], mlp_b2[i])
        x = layer_norm(ALPHA * x + (1.0 + gate) * y, ln_ffn_g[i], ln_ffn_b[i])
    return x


def setup_inputs(seed=0):
    out = dict(first_inputs(seed))
    for name, value in second_inputs(seed + 1).items():
        if name != "x":
            out[name + "_2"] = value
    return out


def reference(
    x, c, ctx, c_ctx, ada_w, ada_b, norm_mix_g, w_in, hgrn_lb_logits, hgrn_norm_g, gla_gk_w,
    gla_gk_b, gla_norm_g, w_branch_hgrn, w_branch_gla, w_out, norm_ffn_g, peer_wq, peer_k1,
    peer_k2, peer_u, peer_v, final_g, c_2, positions_2, mla_w_in_2, mla_q_norm_2, mla_w_qb_2,
    mla_kv_norm_2, mla_w_kvb_2, mla_w_o_2, ssm_w_in_2, ssm_log_dt_2, ssm_a_re_2, ssm_a_im_2,
    ssm_b_re_2, ssm_b_im_2, ssm_c_re_2, ssm_c_im_2, ssm_d_2, ssm_w_glu_2, ssm_b_glu_2,
    ssm_w_out_2, mlp_w1_2, mlp_b1_2, mlp_w2_2, mlp_b2_2, mod_mix_w_2, mod_mix_b_2, mod_ffn_w_2,
    mod_ffn_b_2, ln_mix_g_2, ln_mix_b_2, ln_ffn_g_2, ln_ffn_b_2,
):
    x = first_block(
        x, c, ctx, c_ctx, ada_w, ada_b, norm_mix_g, w_in, hgrn_lb_logits, hgrn_norm_g, gla_gk_w,
        gla_gk_b, gla_norm_g, w_branch_hgrn, w_branch_gla, w_out, norm_ffn_g, peer_wq, peer_k1,
        peer_k2, peer_u, peer_v, final_g,
    )
    return second_block(
        x, c_2, positions_2, mla_w_in_2, mla_q_norm_2, mla_w_qb_2, mla_kv_norm_2, mla_w_kvb_2,
        mla_w_o_2, ssm_w_in_2, ssm_log_dt_2, ssm_a_re_2, ssm_a_im_2, ssm_b_re_2, ssm_b_im_2,
        ssm_c_re_2, ssm_c_im_2, ssm_d_2, ssm_w_glu_2, ssm_b_glu_2, ssm_w_out_2, mlp_w1_2,
        mlp_b1_2, mlp_w2_2, mlp_b2_2, mod_mix_w_2, mod_mix_b_2, mod_ffn_w_2, mod_ffn_b_2,
        ln_mix_g_2, ln_mix_b_2, ln_ffn_g_2, ln_ffn_b_2,
    )


_drawn_inputs = setup_inputs


def setup_inputs(seed=0):
    import zlib

    import numpy as np

    out = dict(_drawn_inputs(seed))
    spreads = {}
    factors = {'ctx': 3.577,
     'c_ctx': 5.181,
     'ada_b': 3.529,
     'hgrn_norm_g': 4.296,
     'gla_gk_w': 3.053,
     'gla_gk_b': 8.0,
     'gla_norm_g': 5.169,
     'norm_ffn_g': 8.0,
     'peer_wq': 3.45,
     'peer_k1': 3.535,
     'peer_k2': 3.52,
     'peer_u': 3.854,
     'peer_v': 3.451,
     'mla_q_norm_2': 8.0,
     'mla_kv_norm_2': 8.0,
     'ssm_log_dt_2': 61.936,
     'ssm_a_re_2': 64.0,
     'ssm_a_im_2': 56.2,
     'ssm_b_re_2': 64.0,
     'ssm_b_im_2': 64.0,
     'ssm_c_re_2': 64.0,
     'ssm_c_im_2': 64.0,
     'ssm_b_glu_2': 64.0,
     'mlp_b1_2': 8.0,
     'mlp_b2_2': 6.099,
     'mod_mix_b_2': 8.0,
     'mod_ffn_b_2': 5.087,
     'ln_mix_b_2': 3.738,
     'ln_ffn_b_2': 3.894}
    for name, (base, spread) in spreads.items():
        noise = np.random.default_rng([zlib.crc32(name.encode()), seed]).standard_normal(out[name].shape)
        drawn = base * np.exp(spread * noise) if base else spread * noise
        out[name] = jnp.asarray(drawn.astype(out[name].dtype))
    for name, factor in factors.items():
        out[name] = (out[name] * factor).astype(out[name].dtype)
    return out
```

```python
import concourse.bass as bass
from concourse import mybir
from contextlib import ExitStack
import math
import numpy as np

F32 = mybir.dt.float32
U32 = mybir.dt.uint32
I32 = mybir.dt.int32
BF16 = mybir.dt.bfloat16
ALU = mybir.AluOpType
ACT = mybir.ActivationFunctionType
AXX = mybir.AxisListType.X

P = 128
T = 512
TC = 256
D = 1024
KT = D // P
CH = 64
NCH = T // CH
EPS = 1e-6
LN_EPS = 1e-5
ALPHA = 4 ** 0.25
HG_H, GLA_H = 8, 4
GLA_VT = 2
PEER_H, NKEY, TOPK = 8, 128, 16
TT = T // P
FF = 4096
ROUNDMAGIC = 12582912.0

VEC_SIZES = [
    ("c", 8), ("c_ctx", 8), ("c_2", 8), ("mod_b", 144), ("norm_mix_g", 8), ("lb_logits", 32),
    ("hgrn_norm_g", 1), ("gk_b", 8), ("gla_norm_g", 2), ("norm_ffn_g", 8), ("final_g", 8),
    ("q_norm", 2), ("kv_norm", 1), ("ssm_d", 8), ("b_glu", 8), ("mlp_b1", 64), ("mlp_b2", 16),
    ("ln_mix_g", 16), ("ln_mix_b", 16), ("ln_ffn_g", 16), ("ln_ffn_b", 16), ("inv_freq", 1), ("rope_sign", 1),
]
VEC = {}
_at = 0
for _n, _k in VEC_SIZES:
    VEC[_n] = (_at, _k)
    _at += _k
NVEC = _at
MOD_TILES = 48 + 4 * 24


class Steps:

    def __init__(self, eng, sem):
        self.eng, self.sem, self.n, self.turn = eng, sem, 0, 0

    def do(self, ins):
        self.n += 1
        ins.then_inc(self.sem, 1)

    def sync(self, passed=None):
        self.eng.wait_ge(self.sem, self.turn + self.n)
        if passed is not None:
            self.eng.sem_inc(passed, 1)

    def then(self, ins):
        self.do(ins)
        self.sync()

    def loop(self, n, per, body):
        at = self.n
        with self.eng.Fori(0, n) as i:
            self.turn = i * per
            body(i)
        assert self.n - at == per, (self.sem, self.n - at)
        self.n, self.turn = at + per * n, 0


SPENT = []


def recycle(nc):
    nc.all_engine_barrier()
    nc.clear_and_free_semaphores(list(SPENT))
    nc.all_engine_barrier()
    SPENT.clear()


class Phase:

    def __init__(self, nc, name):
        self.nc, self.name, self.ctx = nc, name, ExitStack()

    def __enter__(self):
        self.ctx.__enter__()
        return self

    def __exit__(self, *a):
        return self.ctx.__exit__(*a)

    def sb(self, name, shape, dt=F32):
        return self.ctx.enter_context(self.nc.sbuf_tensor(f"{self.name}_{name}", shape, dt))

    def banks(self, name, n=1):
        return self.ctx.enter_context(self.nc.psum_tensor(f"{self.name}_{name}", [P, n * 512], F32))

    def sems(self, *names):
        out = [self.nc.alloc_semaphore(f"{self.name}_{n}") for n in names]
        SPENT.extend(out)
        return out if len(out) > 1 else out[0]

    def block(self):
        return self.ctx.enter_context(self.nc.Block())


def stream(sp, slots, tiles, n, ready, used):
    r = len(slots)
    for s in range(min(r, n)):
        sp.dma_start(slots[s], tiles(s)).then_inc(ready[s], 16)
    if n > r:
        assert n % r == 0
        with sp.Fori(0, n // r - 1) as i:
            for s in range(r):
                sp.wait_ge(used, i * r + (s + 1))
                sp.dma_start(slots[s], tiles(i * r + (r + s))).then_inc(ready[s], 16)


def setup_and_modulation(nc, K, d):
    with Phase(nc, "mod") as ph:
        R = 8
        ring = ph.sb("ring", [P, R, KT * P])
        silu = ph.sb("silu", [P, KT, 4])
        sig = ph.sb("sig", [P, 24])
        small = ph.sb("small", [P, 5, 16])
        pos_i = ph.sb("pos_i", [P, T], I32)
        ps = [ph.banks(f"ps{i}")[:, 0:4 * R].rearrange("p (s v) -> p s v", v=4) for i in range(2)]
        ready = ph.sems(*[f"w_ready{i}" for i in range(R)])
        (tile_done, stored, vec_in, x_in, v, siluc, sigd, lb_in, lb_exp, consts, g_step) = ph.sems(
            "tile_done", "stored", "vec_in", "x_in", "v", "silu_ready", "sig_ready", "lb_max",
            "lb_exp", "consts", "g_step")
        block = ph.block()

        @block.sync
        def _(sp):
            stream(sp, [ring[:, s, :] for s in range(R)], lambda t: d["w_mod"][t], MOD_TILES, ready, tile_done)

        @block.scalar
        def _(act):
            act.dma_start(K.vec[:], d["vec"]).then_inc(vec_in, 16)
            act.dma_start(K.x[:], d["xT"].rearrange("(k p) t -> p k t", p=P)).then_inc(x_in, 16)
            act.dma_start(K.hc[:], d["ctxT"].rearrange("(k p) t -> p k t", p=P)).then_inc(x_in, 16)
            act.wait_ge(vec_in, 16)
            nc.scalar.activation(sig[:], K.vec[:, 0:24], ACT.Sigmoid).then_inc(sigd, 1)
            act.wait_ge(lb_in, 1)
            nc.scalar.activation(small[:, 1:3, :], small[:, 1:3, :], ACT.Exp).then_inc(lb_exp, 1)
            act.wait_ge(x_in, 32)

        @block.gpsimd
        def _(g):
            st = Steps(g, g_step)
            st.do(nc.gpsimd.memset(K.ones[:], 1.0))
            st.do(nc.gpsimd.memset(K.ident[:], 0.0))
            st.do(nc.gpsimd.memset(K.segf[:], 1.0))
            st.do(nc.gpsimd.memset(K.segb[:], 1.0))
            st.do(nc.gpsimd.memset(K.tri[:], 1.0))
            st.sync()
            st.do(nc.gpsimd.affine_select(out=K.ident[:], in_=K.ident[:], compare_op=ALU.not_equal, fill=1.0,
                                          base=0, pattern=[[-1, P]], channel_multiplier=1))
            st.do(nc.gpsimd.memset(K.segf[:, 0:T:CH], 0.0))
            st.do(nc.gpsimd.memset(K.segf[:, T:T + 1], 0.0))
            st.do(nc.gpsimd.memset(K.segb[:, CH - 1:T:CH], 0.0))
            st.do(nc.gpsimd.memset(K.segb[:, T + TC - 1:T + TC], 0.0))
            st.do(nc.gpsimd.affine_select(out=K.tri[:, 0, :], in_=K.tri[:, 0, :], compare_op=ALU.is_ge, fill=0.0,
                                          base=0, pattern=[[1, CH]], channel_multiplier=-1))
            st.do(nc.gpsimd.affine_select(out=K.tri[:, 1, :], in_=K.tri[:, 1, :], compare_op=ALU.is_ge, fill=0.0,
                                          base=0, pattern=[[-1, CH]], channel_multiplier=1))
            st.sync()
            for c in range(NCH):
                last = nc.gpsimd.tensor_copy(K.triu[:, :, c, :], K.tri[:])
            st.then(last)

        @block.vector
        def _(dve):
            st = Steps(dve, v)
            dve.sem_inc(stored, 1)
            dve.wait_ge(vec_in, 16)
            dve.wait_ge(sigd, 1)
            nc.vector.tensor_tensor(silu[:, :, 0:3].rearrange("p k v -> p v k"),
                                    K.vec[:, 0:24].rearrange("p (v k) -> p v k", v=3),
                                    sig[:].rearrange("p (v k) -> p v k", v=3), ALU.mult).then_inc(siluc, 1)
            a = VEC["lb_logits"][0]
            l0, l1 = K.vec[:, a:a + 16], K.vec[:, a + 16:a + 32]
            st.then(nc.vector.tensor_tensor(small[:, 0, :], l0, l1, ALU.max))
            st.do(nc.vector.tensor_tensor(small[:, 1, :], l0, small[:, 0, :], ALU.subtract))
            nc.vector.tensor_tensor(small[:, 2, :], l1, small[:, 0, :], ALU.subtract).then_inc(lb_in, 1)
            dve.wait_ge(lb_exp, 1)
            st.then(nc.vector.tensor_tensor(small[:, 3, :], small[:, 1, :], small[:, 2, :], ALU.add))
            st.then(nc.vector.reciprocal(small[:, 4, :], small[:, 3, :]))
            st.then(nc.vector.tensor_tensor(K.lb[:], small[:, 1, :], small[:, 4, :], ALU.mult))
            st.then(nc.vector.tensor_scalar(K.oml[:], K.lb[:], -1.0, 1.0, ALU.mult, ALU.add))

            def evac(i):
                for b in range(2):
                    dve.wait_ge(tile_done, i * (2 * R) + R * (b + 1))
                    nc.vector.tensor_copy(K.mod[:, bass.ds(i * (2 * R) + b * R, R), :],
                                          ps[b][:, :, 0:3]).then_inc(stored, 1)

            with dve.Fori(0, MOD_TILES // (2 * R)) as i:
                evac(i)
            dve.wait_ge(stored, MOD_TILES // R + 1)
            b = VEC["mod_b"][0]
            st.then(nc.vector.tensor_tensor(K.mod[:], K.mod[:],
                                            K.vec[:, b:b + MOD_TILES].unsqueeze(2).to_broadcast([P, MOD_TILES, 3]),
                                            ALU.add))
            g0 = VEC["norm_mix_g"][0]
            for dst, vecc in ((K.gs_mix, 0), (K.gs_ctx, 1)):
                st.then(nc.vector.tensor_scalar(dst[:], K.mod[:, 8:16, vecc], 1.0, None, ALU.add))
                st.then(nc.vector.tensor_tensor(dst[:], dst[:], K.vec[:, g0:g0 + KT], ALU.mult))
            g1 = VEC["norm_ffn_g"][0]
            st.then(nc.vector.tensor_scalar(K.gs_ffn[:], K.mod[:, 32:40, 0], 1.0, None, ALU.add))
            st.then(nc.vector.tensor_tensor(K.gs_ffn[:], K.gs_ffn[:], K.vec[:, g1:g1 + KT], ALU.mult))
            for s in range(4):
                st.do(nc.vector.tensor_scalar(K.ops[:, s, :], K.mod[:, 48 + 24 * s + 8:48 + 24 * s + 24, 2], 1.0, None, ALU.add))
            st.sync()

        @block.tensor
        def _(pe):
            pe.wait_ge(siluc, 1)

            def octet(i, b):
                pe.wait_ge(stored, i * 2 + 1)
                for s in range(R):
                    pe.wait_ge(ready[s], i * 32 + 16 * (b + 1))
                    for k in range(KT):
                        last = nc.tensor.matmul(ps[b][:, s, 0:3], ring[:, s, k * P:(k + 1) * P], silu[:, k, 0:3],
                                                start=k == 0, stop=k == KT - 1)
                    last.then_inc(tile_done, 1)

            with pe.Fori(0, MOD_TILES // (2 * R)) as i:
                for b in range(2):
                    octet(i, b)


def norm_phase(nc, K, name, jobs, center=False):
    with Phase(nc, name) as ph:
        sq = ph.sb("sq", [P, 2, T])
        rstd = ph.sb("rstd", [P, T])
        tmp = ph.sb("tmp", [P, 2, T])
        sums = ph.banks("sums", 2)[:].rearrange("p (s t) -> p s t", s=2)
        sq_ready, sums_done, rstd_ready, v, a, cent, mean_done = ph.sems(
            "sq_ready", "sums_done", "rstd_ready", "v", "a", "centered", "mean_done")
        block = ph.block()
        J = len(jobs)

        @block.tensor
        def _(pe):
            for j, (src, dst, n, mul, add) in enumerate(jobs):
                if center:
                    for k in range(KT):
                        last = nc.tensor.matmul(sums[:, 1, 0:n], K.ones[:], src[:, k, 0:n], start=k == 0, stop=k == KT - 1)
                    last.then_inc(mean_done, 1)
                if j:
                    pe.wait_ge(rstd_ready, j)
                for k in range(KT):
                    pe.wait_ge(sq_ready, j * KT + k + 1)
                    nc.tensor.matmul(sums[:, 0, 0:n], K.ones[:], sq[:, k % 2, 0:n], start=k == 0,
                                     stop=k == KT - 1).then_inc(sums_done, 1)

        @block.scalar
        def _(act):
            st = Steps(act, a)
            for j, (src, dst, n, mul, add) in enumerate(jobs):
                for k in range(KT):
                    if j * KT + k >= 2:
                        act.wait_ge(sums_done, j * KT + k - 1)
                    if center:
                        act.wait_ge(cent, j * KT + k + 1)
                    nc.scalar.activation(sq[:, k % 2, 0:n], (dst if center else src)[:, k, 0:n],
                                         ACT.Square).then_inc(sq_ready, 1)
                act.wait_ge(sums_done, (j + 1) * KT)
                if j:
                    act.wait_ge(cent, 100 * j)
                st.then(nc.scalar.activation(rstd[:, 0:n], sums[:, 0, 0:n], ACT.Ln, scale=1.0 / D,
                                             bias=LN_EPS if center else EPS))
                nc.scalar.activation(rstd[:, 0:n], rstd[:, 0:n], ACT.Exp, scale=-0.5).then_inc(rstd_ready, 1)

        @block.vector
        def _(dve):
            st = Steps(dve, v)
            for j, (src, dst, n, mul, add) in enumerate(jobs):
                if center:
                    dve.wait_ge(mean_done, 1)
                    for k in range(KT):
                        nc.vector.scalar_tensor_tensor(out=dst[:, k, 0:n], in0=sums[:, 1, 0:n], scalar=-1.0 / D,
                                                       in1=src[:, k, 0:n], op0=ALU.mult, op1=ALU.add).then_inc(cent, 1)
                base = dst if center else src
                dve.wait_ge(rstd_ready, j + 1)
                for k in range(KT):
                    if add is None:
                        st.do(nc.vector.scalar_tensor_tensor(out=dst[:, k, 0:n], in0=base[:, k, 0:n], scalar=mul[:, k:k + 1],
                                                             in1=rstd[:, 0:n], op0=ALU.mult, op1=ALU.mult))
                    else:
                        st.then(nc.vector.scalar_tensor_tensor(out=tmp[:, k % 2, 0:n], in0=base[:, k, 0:n], scalar=mul[:, k:k + 1],
                                                               in1=rstd[:, 0:n], op0=ALU.mult, op1=ALU.mult))
                        st.do(nc.vector.tensor_scalar(dst[:, k, 0:n], tmp[:, k % 2, 0:n], add[:, k:k + 1], None, ALU.add))
                st.sync()
                if j < J - 1:
                    dve.sem_inc(cent, 100)


def heads_phase(nc, K, d, name, w_dram, heads, vt, gate_norm, y, scan_scale, log_gates=None):
    hg = log_gates is None
    NT = 5 if hg else 6
    with_ctx = 3
    QI = 3
    VI = 2 if hg else 1
    GI = 4
    N = T + TC
    with Phase(nc, name) as ph:
        R = 5 if hg else 3
        ring = ph.sb("ring", [P, R, KT * P])
        proj_sb = ph.sb("proj", [P, 2, with_ctx * N + (NT - with_ctx) * T])
        sgate = ph.sb("sgate", [P, 2, vt, T])
        if hg:
            forget = ph.sb("forget", [P, 2, N])
            key2 = ph.sb("key2", [P, 2, N])
            lg2 = ph.sb("lg2", [P, 2, N])
        cum = ph.sb("cum", [P, N])
        dif = ph.sb("dif", [P, T])
        dif2 = ph.sb("dif2", [P, N])
        e_q = ph.sb("e_q", [P, T])
        e_k = ph.sb("e_k", [P, T])
        e_kd = ph.sb("e_kd", [P, N])
        q_dec = ph.sb("q_dec", [P, 2, T])
        e_last = ph.sb("e_last", [P, 2, NCH])
        vtok = ph.sb("vtok", [CH, NCH, vt, P])
        vtok_c = ph.sb("vtok_c", [P, 2, vt, P])
        ktok = ph.sb("ktok", [CH, NCH, P])
        ktok_c = ph.sb("ktok_c", [P, 2, P])
        score = ph.sb("score", [CH, 2, T])
        state = ph.sb("state", [P, 2, NCH, vt, P])
        osq = ph.sb("osq", [P, T])
        rstd = ph.sb("rstd", [P, T])
        pg = ph.banks("proj_ps", 3)
        ptr = ph.banks("trans_ps", 2)
        psc = ph.banks("score_ps")
        pkv = ph.banks("kv_ps", 2)
        kv = pkv[:].rearrange("p (n v) -> p n v", n=NCH)
        o_ps = [psc, ptr[:, 0:T]]
        ready = ph.sems(*[f"w_ready{i}" for i in range(R)])
        (proj_done, proj_stored, sig_done, f_done, ln_done, dif_done, exp_done, prep_done, vtr_done,
         vtok_done, b_done, ktok_done, mask_done, kv_done, state_done, o_done, osq_done, sum_done,
         rstd_done, y_done, v, a, passed) = ph.sems(
            "proj_done", "proj_stored", "sig_done", "forget_done", "log_done", "dif_done", "exp_done",
            "prep_done", "vtrans_done", "vtok_done", "scores_done", "ktok_done", "mask_done", "kv_done",
            "state_done", "o_done", "osq_done", "sum_done", "rstd_done", "y_done", "v", "a", "passed")
        block = ph.block()

        def proj(par, j):
            at = j * N if j < with_ctx else with_ctx * N + (j - with_ctx) * T
            return proj_sb[:, par, at:at + (N if j < with_ctx else T)]

        def pgl(t):
            return pg[:, (t % 2) * T:(t % 2) * T + T]

        def pgc(t):
            return pg[:, 2 * T:2 * T + TC]

        @block.sync
        def _(sp):
            stream(sp, [ring[:, s, :] for s in range(R)], lambda t: w_dram[t], heads * NT, ready, proj_done)

        @block.tensor
        def _(pe):
            def project(h, par, j):
                t = par * NT + j
                s = t % R
                pe.wait_ge(ready[s], h // 2 * (16 * (2 * NT // R)) + 16 * (t // R + 1) if isinstance(h, int)
                           else (h - par) * (8 * (2 * NT // R)) + 16 * (t // R + 1))
                pe.wait_ge(proj_stored, h * NT + (j + 1))
                for k in range(KT):
                    last = nc.tensor.matmul(pgl(t), ring[:, s, k * P:(k + 1) * P], K.h[:, k, :], start=k == 0, stop=k == KT - 1)
                if j < with_ctx:
                    pe.wait_ge(proj_stored, h * NT + (j + 2))
                    for k in range(KT):
                        last = nc.tensor.matmul(pgc(t), ring[:, s, k * P:(k + 1) * P], K.hc[:, k, :], start=k == 0, stop=k == KT - 1)
                last.then_inc(proj_done, 1)

            def transposes(src, out, ctx_out):
                for n in range(NCH):
                    nc.tensor.transpose(out[0:CH, n * P:(n + 1) * P], src[:, n * CH:(n + 1) * CH], K.ident[:])
                for n in range(2):
                    last = nc.tensor.transpose(ctx_out[:, n * P:(n + 1) * P], src[:, T + n * P:T + (n + 1) * P], K.ident[:])
                return last

            def attend(h, par, nxt):
                def between(*js):
                    if nxt is not None:
                        for j in js:
                            project(nxt[0], nxt[1], j)

                between(0)
                for u in range(vt):
                    pe.wait_ge(proj_stored, h * NT + NT + 2)
                    pe.wait_ge(y_done, h * vt + 1)
                    if u:
                        pe.wait_ge(vtok_done, h * vt + u)
                    pe.sem_inc(passed, 1)
                    transposes(proj(par, VI + u), ptr, pkv).then_inc(vtr_done, 1)
                for dr in range(2):
                    pe.wait_ge(vtok_done, h * vt + vt)
                    pe.wait_ge(prep_done, h * 2 + dr + 1)
                    if dr:
                        pe.wait_ge(ktok_done, h * 2 + 1)
                        pe.wait_ge(mask_done, h * 2 + 1)
                        pe.wait_ge(state_done, h * (2 * vt) + vt)
                    for n in range(NCH):
                        c = slice(n * CH, (n + 1) * CH)
                        nc.tensor.matmul(psc[0:CH, c], e_k[:, c], e_q[:, c], start=True, stop=True)
                    transposes(e_kd, ptr, pkv).then_inc(b_done, 1)
                    between(1 + 2 * dr)
                    pe.wait_ge(ktok_done, h * 2 + dr + 1)
                    for u in range(vt):
                        if u:
                            pe.wait_ge(state_done, h * (2 * vt) + dr * vt + u)
                        for n in range(NCH):
                            if n != (NCH - 1 if dr == 0 else 0):
                                nc.tensor.matmul(kv[:, n, :], ktok[:, n, :], vtok[:, n, u, :], start=True, stop=True)
                        s0 = NCH - 1 if dr == 0 else 0
                        for n in range(2):
                            last = nc.tensor.matmul(kv[:, s0, :], ktok_c[:, n, :], vtok_c[:, n, u, :], start=n == 0, stop=n == 1)
                        last.then_inc(kv_done, 1)
                    between(2 + 2 * dr)
                between(*range(5, NT))
                pe.wait_ge(mask_done, h * 2 + 2)
                pe.wait_ge(state_done, h * (2 * vt) + 2 * vt)
                for u in range(vt):
                    for n in range(NCH):
                        c = slice(n * CH, (n + 1) * CH)
                        for dr in range(2):
                            nc.tensor.matmul(o_ps[u][:, c], vtok[:, n, u, :], score[:, dr, c], start=dr == 0, stop=False)
                            last = nc.tensor.matmul(o_ps[u][:, c], state[:, dr, n, u, :], q_dec[:, dr, c], start=False, stop=dr == 1)
                    last.then_inc(o_done, 1)
                for u in range(vt):
                    pe.wait_ge(osq_done, h * vt + u + 1)
                    last = nc.tensor.matmul(ptr[:, T:2 * T], K.ones[:], osq[:], start=u == 0, stop=u == vt - 1)
                    last.then_inc(sum_done, 1)

            for j in range(NT):
                project(0, 0, j)
            with pe.Fori(0, heads // 2 - 1) as i:
                attend(i * 2, 0, (i * 2 + 1, 1))
                attend(i * 2 + 1, 1, (i * 2 + 2, 0))
            attend(heads - 2, 0, (heads - 1, 1))
            attend(heads - 1, 1, None)

        @block.scalar
        def _(act):
            st = Steps(act, a)

            def store(h, par, j):
                t = par * NT + j
                act.wait_ge(proj_done, h * NT + j + 1)
                scale = P ** -0.5 if j == QI else 1.0
                if j < with_ctx:
                    nc.scalar.activation(proj(par, j)[:, T:N], pgc(t), ACT.Copy)
                nc.scalar.activation(proj(par, j)[:, 0:T], pgl(t), ACT.Copy, scale=scale).then_inc(proj_stored, 1)

            def exps(h, dr):
                act.wait_ge(dif_done, h * 6 + dr * 3 + 1)
                if dr:
                    act.wait_ge(b_done, h * 2 + 1)
                nc.scalar.activation(e_q[:], dif[:], ACT.Exp, scale=scan_scale)
                nc.scalar.activation(e_k[:], dif[:], ACT.Exp, scale=-scan_scale)
                nc.scalar.activation(q_dec[:, dr, :], cum[:, 0:T], ACT.Exp, scale=scan_scale)
                last = (slice(CH - 1, T, CH), slice(0, T, CH))[dr]
                nc.scalar.activation(e_last[:, dr, :], cum[:, last], ACT.Exp, scale=scan_scale)
                act.wait_ge(dif_done, h * 6 + dr * 3 + 3)
                nc.scalar.activation(e_kd[:], dif2[:], ACT.Exp, scale=scan_scale).then_inc(exp_done, 1)

            def attend(h, par, nxt):
                def between(*js):
                    if nxt is not None:
                        for j in js:
                            store(nxt[0], nxt[1], j)

                act.wait_ge(proj_stored, h * NT + NT + 2)
                for u in range(vt):
                    nc.scalar.activation(sgate[:, par, u, :], proj(par, GI + u), ACT.Sigmoid).then_inc(sig_done, 1)
                if hg:
                    for dr in range(2):
                        nc.scalar.activation(forget[:, dr, :], proj(par, dr), ACT.Sigmoid).then_inc(sig_done, 1)
                    for dr in range(2):
                        act.wait_ge(f_done, h * 2 + dr + 1)
                        nc.scalar.activation(lg2[:, dr, :], forget[:, dr, :], ACT.Ln).then_inc(ln_done, 1)
                exps(h, 0)
                between(0)
                for u in range(vt):
                    act.wait_ge(vtr_done, h * vt + u + 1)
                    nc.scalar.activation(vtok_c[:, :, u, :], pkv[:, 0:2 * P].rearrange("p (n v) -> p n v", n=2), ACT.Copy)
                    nc.scalar.activation(vtok[:, :, u, :], ptr[0:CH, :].rearrange("p (n v) -> p n v", n=NCH), ACT.Copy).then_inc(vtok_done, 1)
                for dr in range(2):
                    act.wait_ge(b_done, h * 2 + dr + 1)
                    nc.scalar.activation(ktok_c[:], pkv[:, 0:2 * P].rearrange("p (n v) -> p n v", n=2), ACT.Copy)
                    nc.scalar.activation(ktok[:], ptr[0:CH, :].rearrange("p (n v) -> p n v", n=NCH), ACT.Copy).then_inc(ktok_done, 1)
                    if dr == 0:
                        exps(h, 1)
                    between(1 + 2 * dr)
                    between(2 + 2 * dr)
                between(*range(5, NT))
                for u in range(vt):
                    act.wait_ge(o_done, h * vt + u + 1)
                    if u:
                        act.wait_ge(sum_done, h * vt + u)
                    nc.scalar.activation(osq[:], o_ps[u][:, 0:T], ACT.Square).then_inc(osq_done, 1)
                act.wait_ge(sum_done, h * vt + vt)
                st.then(nc.scalar.activation(rstd[:], ptr[:, T:2 * T], ACT.Ln, scale=1.0 / (P * vt), bias=EPS))
                nc.scalar.activation(rstd[:], rstd[:], ACT.Exp, scale=-0.5).then_inc(rstd_done, 1)

            act.sem_inc(proj_stored, 2)
            for j in range(NT):
                store(0, 0, j)
            n0 = st.n
            with act.Fori(0, heads // 2 - 1) as i:
                st.turn = i * 2
                attend(i * 2, 0, (i * 2 + 1, 1))
                attend(i * 2 + 1, 1, (i * 2 + 2, 0))
            st.n, st.turn = n0 + 2 * (heads // 2 - 1), 0
            attend(heads - 2, 0, (heads - 1, 1))
            attend(heads - 1, 1, None)

        @block.vector
        def _(dve):
            st = Steps(dve, v)

            def differences(h, par, dr):
                seg = (K.segf, K.segb)[dr]
                lg = lg2[:, dr, :] if hg else log_gates[:, bass.ds(h * 2 + dr, 1), :].squeeze(1)
                if hg:
                    dve.wait_ge(ln_done, h * 2 + dr + 1)
                if dr:
                    dve.wait_ge(exp_done, h * 2 + 1)
                if dr == 0:
                    st.then(nc.vector.tensor_tensor_scan(cum[:], seg[:], lg, 0.0, ALU.mult, ALU.add))
                else:
                    st.then(nc.vector.tensor_tensor_scan(cum[:, ::-1], seg[:, ::-1], lg[:, ::-1], 0.0, ALU.mult, ALU.add))
                ref = (CH // 2, CH // 2 - 1)[dr]
                end = (CH - 1, 0)[dr]
                cend = (N - 1, T)[dr]
                c3 = cum[:, 0:T].rearrange("p (n c) -> p n c", c=CH)
                nc.vector.tensor_tensor(dif[:].rearrange("p (n c) -> p n c", c=CH), c3,
                                        c3[:, :, ref:ref + 1].to_broadcast([P, NCH, CH]), ALU.subtract).then_inc(dif_done, 1)
                nc.vector.tensor_tensor(dif2[:, 0:T].rearrange("p (n c) -> p n c", c=CH),
                                        c3[:, :, end:end + 1].to_broadcast([P, NCH, CH]), c3, ALU.subtract).then_inc(dif_done, 1)
                nc.vector.tensor_scalar(dif2[:, T:N], cum[:, T:N], -1.0, cum[:, cend:cend + 1], ALU.mult, ALU.add).then_inc(dif_done, 1)

            def products(h, par, dr):
                dve.wait_ge(exp_done, h * 2 + dr + 1)
                key = key2[:, dr, :] if hg else proj(par, 0)
                q = proj(par, QI)
                nc.vector.tensor_tensor(e_q[:], e_q[:], q, ALU.mult)
                nc.vector.tensor_tensor(e_k[:], e_k[:], key[:, 0:T], ALU.mult)
                nc.vector.tensor_tensor(q_dec[:, dr, :], q_dec[:, dr, :], q, ALU.mult)
                nc.vector.tensor_tensor(e_kd[:], e_kd[:], key, ALU.mult).then_inc(prep_done, 1)

            def mask(h, dr):
                dve.wait_ge(b_done, h * 2 + dr + 1)
                dve.sem_inc(passed, 1)
                nc.vector.copy_predicated(score[:, dr, :], K.triu[:, dr, :, :].rearrange("p n c -> p (n c)"), psc[0:CH, :]).then_inc(mask_done, 1)

            def states(h, dr):
                order = list(range(NCH)) if dr == 0 else list(range(NCH))[::-1]
                for u in range(vt):
                    dve.wait_ge(kv_done, h * (2 * vt) + dr * vt + u + 1)
                    st.then(nc.vector.tensor_copy(state[:, dr, order[0], u, :], kv[:, order[-1], :]))
                    for a_, b_ in zip(order[:-1], order[1:]):
                        ins = nc.vector.scalar_tensor_tensor(
                            out=state[:, dr, b_, u, :], in0=state[:, dr, a_, u, :], scalar=e_last[:, dr, a_:a_ + 1],
                            in1=kv[:, a_, :], op0=ALU.mult, op1=ALU.add)
                        if b_ == order[-1]:
                            ins.then_inc(state_done, 1)
                        else:
                            st.then(ins)

            def attend(h, par):
                ns = vt + (2 if hg else 0)
                dve.wait_ge(proj_stored, h * NT + NT + 2)
                dve.wait_ge(sig_done, h * ns + vt)
                st.do(nc.vector.tensor_tensor(sgate[:, par], sgate[:, par], proj_sb[:, par, with_ctx * N + (GI - with_ctx) * T:with_ctx * N + (GI - with_ctx + vt) * T].rearrange("p (u t) -> p u t", u=vt), ALU.mult))
                if hg:
                    for dr in range(2):
                        dve.wait_ge(sig_done, h * ns + vt + dr + 1)
                        col = bass.ds(h + dr * HG_H, 1)
                        nc.vector.tensor_scalar(forget[:, dr, :], forget[:, dr, :], K.oml[:, col], K.lb[:, col],
                                                ALU.mult, ALU.add).then_inc(f_done, 1)
                        dve.wait_ge(f_done, h * 2 + dr + 1)
                        st.do(nc.vector.tensor_scalar(key2[:, dr, :], forget[:, dr, :], -1.0, 1.0, ALU.mult, ALU.add))
                differences(h, par, 0)
                products(h, par, 0)
                differences(h, par, 1)
                mask(h, 0)
                products(h, par, 1)
                states(h, 0)
                mask(h, 1)
                states(h, 1)
                dve.wait_ge(rstd_done, h + 1)
                for u in range(vt):
                    yo = y[:, bass.ds(h * vt + u, 1), :].squeeze(1)
                    st.then(nc.vector.scalar_tensor_tensor(out=osq[:] if u == 0 else dif[:], in0=o_ps[u][:, 0:T], scalar=gate_norm[:, u:u + 1],
                                                           in1=rstd[:], op0=ALU.mult, op1=ALU.mult))
                    nc.vector.tensor_tensor(yo, osq[:] if u == 0 else dif[:], sgate[:, par, u, :], ALU.mult).then_inc(y_done, 1)

            dve.sem_inc(y_done, 1)
            st.then(nc.vector.memset(score[:], 0.0))
            per = 1 + (2 if hg else 0) + 2 + 2 * vt * (NCH - 1) + vt
            n0 = st.n
            with dve.Fori(0, heads // 2 - 1) as i:
                st.turn = i * (2 * per)
                attend(i * 2, 0)
                attend(i * 2 + 1, 1)
            assert st.n - n0 == 2 * per, (st.n - n0, per)
            st.n, st.turn = n0 + 2 * per * (heads // 2 - 1), 0
            attend(heads - 2, 0)
            attend(heads - 1, 1)


def lora_gates(nc, K, d, log_gates):
    N = T + TC
    with Phase(nc, "lora") as ph:
        w = ph.sb("w", [P, KT, 32])
        gw = ph.sb("gw", [16, 2, T])
        gr = ph.sb("gr", [16, 2, N])
        az = ph.sb("az", [P, N])
        mz = ph.sb("mz", [P, N])
        g_ps = ph.banks("g", 2)
        z_ps = ph.banks("z", 4)
        w_in, gr_done, gr_stored, z_done, abs_done, m_done, l_done, out_done, a = ph.sems(
            "w_in", "gr_done", "gr_stored", "z_done", "abs_done", "min_done", "log_done", "out_done", "a")
        block = ph.block()
        pairs = [(h, dr) for h in range(GLA_H) for dr in range(2)]
        gb = VEC["gk_b"][0]

        @block.sync
        def _(sp):
            sp.dma_start(w[:], d["w_gr"].rearrange("(k p) m -> p k m", p=P)).then_inc(w_in, 16)
            sp.dma_start(gw[:], d["gk_w"].rearrange("d r m -> r d m")).then_inc(w_in, 16)

        @block.tensor
        def _(pe):
            pe.wait_ge(w_in, 32)
            for dr in range(2):
                if dr:
                    pe.wait_ge(gr_stored, 1)
                for j, (src, n) in enumerate(((K.h, T), (K.hc, TC))):
                    for k in range(KT):
                        last = nc.tensor.matmul(g_ps[0:16, j * T:j * T + n], w[:, k, 16 * dr:16 * dr + 16], src[:, k, :],
                                                start=k == 0, stop=k == KT - 1)
                last.then_inc(gr_done, 1)
            pe.wait_ge(gr_stored, 2)
            for i, (h, dr) in enumerate(pairs):
                b = 2 * (i % 2) * T
                if i >= 2:
                    pe.wait_ge(m_done, i - 1)
                nc.tensor.matmul(z_ps[:, b:b + T], gw[:, dr, h * P:(h + 1) * P], gr[:, dr, 0:T], start=True, stop=True)
                nc.tensor.matmul(z_ps[:, b + T:b + N], gw[:, dr, h * P:(h + 1) * P], gr[:, dr, T:N], start=True,
                                 stop=True).then_inc(z_done, 1)

        @block.scalar
        def _(act):
            st = Steps(act, a)
            for i, (h, dr) in enumerate(pairs):
                b = 2 * (i % 2) * T
                act.wait_ge(z_done, i + 1)
                bias = K.vec[:, gb + dr * GLA_H + h:gb + dr * GLA_H + h + 1]
                if i:
                    act.wait_ge(out_done, i)
                nc.scalar.activation(az[:], z_ps[:, b:b + N], ACT.Abs, bias=bias).then_inc(abs_done, 1)
                act.wait_ge(abs_done, i + 1)
                st.then(nc.scalar.activation(az[:], az[:], ACT.Exp, scale=-1.0))
                nc.scalar.activation(az[:], az[:], ACT.Ln, bias=1.0).then_inc(l_done, 1)

        @block.vector
        def _(dve):
            for dr in range(2):
                dve.wait_ge(gr_done, dr + 1)
                nc.vector.tensor_copy(gr[:, dr, :], g_ps[0:16, 0:N]).then_inc(gr_stored, 1)
            for i, (h, dr) in enumerate(pairs):
                b = 2 * (i % 2) * T
                dve.wait_ge(abs_done, i + 1)
                bias = K.vec[:, gb + dr * GLA_H + h:gb + dr * GLA_H + h + 1]
                nc.vector.tensor_scalar(mz[:], z_ps[:, b:b + N], bias, 0.0, ALU.add, ALU.min).then_inc(m_done, 1)
                dve.wait_ge(m_done, i + 1)
                dve.wait_ge(l_done, i + 1)
                nc.vector.tensor_tensor(log_gates[:, h * 2 + dr, :], mz[:], az[:], ALU.subtract).then_inc(out_done, 1)


def merge_phase(nc, K, d, y_hg, y_gla, merged):
    with Phase(nc, "merge") as ph:
        ring = ph.sb("ring", [P, 4, KT * P])
        sg = ph.sb("sg", [P, 2, T])
        part = ph.sb("part", [P, T])
        ps = ph.banks("ps", 4)
        ready = ph.sems(*[f"w_ready{i}" for i in range(4)])
        done, sig, out, v = ph.sems("tile_done", "sig_done", "out_done", "v")
        block = ph.block()
        src = [K.h, y_hg, K.h, y_gla]

        @block.sync
        def _(sp):
            stream(sp, [ring[:, s, :] for s in range(4)], lambda t: d["w_merge"][t], 4 * KT, ready, done)

        @block.tensor
        def _(pe):
            with pe.Fori(0, KT) as i:
                for s in range(4):
                    pe.wait_ge(ready[s], i * 16 + 16)
                    if s in (0, 1):
                        pe.wait_ge(out, i * 2 + 1)
                    for k in range(KT):
                        last = nc.tensor.matmul(ps[:, s * T:(s + 1) * T], ring[:, s, k * P:(k + 1) * P], src[s][:, k, :],
                                                start=k == 0, stop=k == KT - 1)
                    last.then_inc(done, 1)

        @block.scalar
        def _(act):
            with act.Fori(0, KT) as i:
                for b in range(2):
                    act.wait_ge(done, i * 4 + 2 * b + 1)
                    act.wait_ge(out, i * 2 + 1)
                    nc.scalar.activation(sg[:, b, :], ps[:, 2 * b * T:(2 * b + 1) * T], ACT.Sigmoid).then_inc(sig, 1)

        @block.vector
        def _(dve):
            dve.sem_inc(out, 1)
            with dve.Fori(0, KT) as i:
                m = merged[:, bass.ds(i, 1), :].squeeze(1)
                dve.wait_ge(sig, i * 2 + 1)
                dve.wait_ge(done, i * 4 + 2)
                nc.vector.tensor_tensor(part[:], sg[:, 0, :], ps[:, T:2 * T], ALU.mult).then_inc(out, 1)
                dve.wait_ge(sig, i * 2 + 2)
                dve.wait_ge(done, i * 4 + 4)
                nc.vector.tensor_tensor(sg[:, 1, :], sg[:, 1, :], ps[:, 3 * T:4 * T], ALU.mult).then_inc(v, 1)
                dve.wait_ge(v, i + 1)
                dve.wait_ge(out, i * 2 + 2)
                nc.vector.tensor_tensor(m, part[:], sg[:, 1, :], ALU.add).then_inc(out, 1)


def linear_phase(nc, K, name, w_dram, src, kts, tiles, finish, R=4):
    with Phase(nc, name) as ph:
        ring = ph.sb("ring", [P, R, kts * P])
        ps = ph.banks("ps", R)
        bufs = ph.sb("buf", [P, R, T])
        ready = ph.sems(*[f"w_ready{i}" for i in range(R)])
        done, mid, out = ph.sems("tile_done", "act_done", "out_done")
        block = ph.block()
        act_step, dve_step = finish

        @block.sync
        def _(sp):
            stream(sp, [ring[:, s, :] for s in range(R)], lambda t: w_dram[t], tiles, ready, done)

        @block.tensor
        def _(pe):
            with pe.Fori(0, tiles // R) as i:
                for s in range(R):
                    pe.wait_ge(ready[s], i * 16 + 16)
                    pe.wait_ge(out, i * R + (s + 1))
                    for k in range(kts):
                        last = nc.tensor.matmul(ps[:, s * T:(s + 1) * T], ring[:, s, k * P:(k + 1) * P], src[:, k, :],
                                                start=k == 0, stop=k == kts - 1)
                    last.then_inc(done, 1)

        @block.scalar
        def _(act):
            if act_step is not None:
                if dve_step is None:
                    act.sem_inc(out, R)
                with act.Fori(0, tiles // R) as i:
                    for s in range(R):
                        act.wait_ge(done, i * R + s + 1)
                        act.wait_ge(out, i * R + (s + 1))
                        act_step(i * R + s, ps[:, s * T:(s + 1) * T], bufs[:, s, :]).then_inc(mid if dve_step else out, 1)

        @block.vector
        def _(dve):
            if dve_step is not None:
                dve.sem_inc(out, R)
                with dve.Fori(0, tiles // R) as i:
                    for s in range(R):
                        if act_step is not None:
                            dve.wait_ge(mid, i * R + s + 1)
                        else:
                            dve.wait_ge(done, i * R + s + 1)
                        dve_step(dve, i * R + s, ps[:, s * T:(s + 1) * T], bufs[:, s, :]).then_inc(out, 1)


def peer_route(nc, K, d, sel):
    NK = TOPK
    with Phase(nc, "route") as ph:
        R = 4
        ring = ph.sb("ring", [P, R, KT * P])
        keys = ph.sb("keys", [P, 2, NKEY])
        q_sb = ph.sb("q", [P, 2, T])
        rest = ph.sb("rest", [P, TT, 2 * P])
        val = ph.sb("val", [P, 2, TT, NK])
        idx = ph.sb("idx", [P, 2, TT, NK], U32)
        idxf = ph.sb("idxf", [P, 2, TT, NK])
        cand = ph.sb("cand", [P, TT, NK, NK])
        top = ph.sb("top", [P, TT, NK])
        topi = ph.sb("topi", [P, TT, NK], U32)
        rc_u = ph.sb("rc_u", [P, 2, TT, NK], U32)
        rc = ph.sb("rc", [P, 2, TT, NK])
        pick = ph.sb("pick", [P, TT, NK, NK])
        iota16 = ph.sb("iota16", [P, NK])
        expd = ph.sb("expd", [P, TT, NK])
        total = ph.sb("total", [P, 2, TT])
        q_ps = ph.banks("q_ps", 2)
        s_ps = ph.banks("s_ps", 2)
        ready = ph.sems(*[f"w_ready{i}" for i in range(R)])
        keys_in, proj_done, q_stored, s_done, s_read, cst, logit_done, exp_done, v, passed = ph.sems(
            "keys_in", "proj_done", "q_stored", "scores_done", "scores_read", "consts", "logit_done", "exp_done", "v", "passed")
        block = ph.block()
        tiles = 2 * PEER_H

        @block.sync
        def _(sp):
            sp.dma_start(keys[:], d["peer_keys"]).then_inc(keys_in, 16)
            stream(sp, [ring[:, s, :] for s in range(R)], lambda t: d["peer_wq"][t], tiles, ready, proj_done)

        @block.gpsimd
        def _(g):
            nc.gpsimd.iota(iota16[:], [[1, NK]], base=0, channel_multiplier=0,
                           allow_small_or_imprecise_dtypes=True).then_inc(cst, 1)

        @block.tensor
        def _(pe):
            pe.wait_ge(keys_in, 16)
            pe.sem_inc(s_done, 1)

            def project(i, s):
                pe.wait_ge(ready[s], i * 16 + 16)
                pe.wait_ge(q_stored, i * R + s + 1)
                for k in range(KT):
                    last = nc.tensor.matmul(q_ps[:, (s % 2) * T:(s % 2) * T + T], ring[:, s, k * P:(k + 1) * P], K.h[:, k, :],
                                            start=k == 0, stop=k == KT - 1)
                last.then_inc(proj_done, 1)

            def scores(i, s):
                pe.wait_ge(q_stored, i * R + s + 3)
                pe.wait_ge(s_read, i * R + s + 1)
                for t in range(TT):
                    last = nc.tensor.matmul(s_ps[:, (s % 2) * T + t * P:(s % 2) * T + (t + 1) * P],
                                            q_sb[:, s % 2, t * P:(t + 1) * P], keys[:, s % 2, :], start=True, stop=True)
                last.then_inc(s_done, 1)

            with pe.Fori(0, tiles // R) as i:
                project(i, 0)
                for s in range(1, R):
                    project(i, s)
                    scores(i, s - 1)
                scores(i, R - 1)

        @block.scalar
        def _(act):
            act.sem_inc(q_stored, 2)
            with act.Fori(0, tiles // R) as i:
                for s in range(R):
                    act.wait_ge(proj_done, i * R + s + 1)
                    act.wait_ge(s_done, i * R + (s + 1))
                    nc.scalar.activation(q_sb[:, s % 2, :], q_ps[:, (s % 2) * T:(s % 2) * T + T], ACT.Copy).then_inc(q_stored, 1)
                    if s % 2 and s > 1:
                        act.wait_ge(logit_done, i * 2 + 1)
                        nc.scalar.activation(expd[:], expd[:], ACT.Exp).then_inc(exp_done, 1)
                act.wait_ge(logit_done, i * 2 + 2)
                nc.scalar.activation(expd[:], expd[:], ACT.Exp).then_inc(exp_done, 1)

        @block.vector
        def _(dve):
            V = nc.vector
            dve.sem_inc(s_read, 2)
            dve.wait_ge(cst, 1)
            st = Steps(dve, v)

            def top16(src, values, indices, n):
                for t in range(TT):
                    st.do(V.max(values[:, t, 0:8], src(t)))
                st.sync(passed)
                for t in range(TT):
                    st.do(V.max_index(indices[:, t, 0:8], values[:, t, 0:8], src(t)))
                    st.do(V.match_replace(rest[:, t, 0:n], values[:, t, 0:8], src(t), -3.0e38))
                st.sync(passed)
                for t in range(TT):
                    st.do(V.max(values[:, t, 8:16], rest[:, t, 0:n]))
                st.sync(passed)
                for t in range(TT):
                    st.do(V.max_index(indices[:, t, 8:16], values[:, t, 8:16], rest[:, t, 0:n]))
                st.sync()

            def head(i, par):
                for s in range(2):
                    dve.wait_ge(s_done, i * R + (par * 2 + s + 2))
                    dve.sem_inc(passed, 1)
                    top16(lambda t: s_ps[:, s * T + t * P:s * T + (t + 1) * P], val[:, s], idx[:, s], P)
                    V.tensor_copy(idxf[:, s], idx[:, s]).then_inc(s_read, 1)
                st.then(V.tensor_tensor(cand[:], val[:, 0].unsqueeze(3).to_broadcast([P, TT, NK, NK]),
                                        val[:, 1].unsqueeze(2).to_broadcast([P, TT, NK, NK]), ALU.add))
                dve.sem_inc(passed, 1)
                top16(lambda t: cand[:, t].rearrange("p a b -> p (a b)"), top, topi, NK * NK)
                V.tensor_tensor(expd[:], top[:], top[:, :, 0:1].to_broadcast([P, TT, NK]), ALU.subtract).then_inc(logit_done, 1)
                st.do(V.tensor_scalar(rc_u[:, 0], topi[:], 4, None, ALU.logical_shift_right))
                st.then(V.tensor_scalar(rc_u[:, 1], topi[:], 15, None, ALU.bitwise_and))
                st.then(V.tensor_copy(rc[:], rc_u[:]))
                cols = slice(None)
                for s in range(2):
                    st.then(V.tensor_tensor(pick[:], rc[:, s].unsqueeze(3).to_broadcast([P, TT, NK, NK]),
                                            iota16[:].unsqueeze(1).unsqueeze(1).to_broadcast([P, TT, NK, NK]), ALU.is_equal))
                    st.then(V.tensor_tensor(pick[:], pick[:], idxf[:, s].unsqueeze(2).to_broadcast([P, TT, NK, NK]), ALU.mult))
                    st.then(V.tensor_reduce(sel[:, s, :, bass.ds(i * (2 * NK) + par * NK, NK)], pick[:], AXX, ALU.add))
                dve.wait_ge(exp_done, i * 2 + par + 1)
                st.then(V.tensor_reduce(total[:, 0, :], expd[:], AXX, ALU.add))
                st.then(V.reciprocal(total[:, 1, :], total[:, 0, :]))
                st.then(V.tensor_tensor(sel[:, 2, :, bass.ds(i * (2 * NK) + par * NK, NK)], expd[:],
                                        total[:, 1, :].unsqueeze(2).to_broadcast([P, TT, NK]), ALU.mult))

            per = 2 * (3 * 5 * TT + 1 + 3 + 6 + 3)

            def pair(i):
                head(i, 0)
                head(i, 1)
            st.loop(PEER_H // 2, per, pair)


def peer_gates(nc, K, d, sel, gates):
    G = 8
    with Phase(nc, "gates") as ph:
        selt = ph.sb("selt", [P, 3, T])
        iota = ph.sb("iota", [P, NKEY])
        rows = ph.sb("rows", [P, 2, G, NKEY])
        cols = ph.sb("cols", [P, 2, G, NKEY])
        slab = ph.sb("slab", [P, 2, NKEY, P])
        t_ps = ph.banks("t_ps", 3)
        g_ps = ph.banks("g_ps", 4)
        cst, tr_done, tr_stored, rows_dist, rows_done, cols_done, g_done, g_stored, v, passed = ph.sems(
            "consts", "trans_done", "trans_stored", "rows_dist", "rows_done", "cols_done", "g_done", "g_stored", "v", "passed")
        slab_out = ph.sems("slab_out0", "slab_out1")
        block = ph.block()
        groups = P // G

        @block.gpsimd
        def _(g):
            nc.gpsimd.iota(iota[:], [[1, NKEY]], base=0, channel_multiplier=0,
                           allow_small_or_imprecise_dtypes=True).then_inc(cst, 1)
            g.wait_ge(cst, 1)
            g.wait_ge(tr_stored, 3)
            with g.Fori(0, T // (2 * G)) as i:
                for b in range(2):
                    g.wait_ge(g_done, i * 2 + b + 1)
                    nc.gpsimd.tensor_tensor(rows[:, b], iota[:].unsqueeze(1).to_broadcast([P, G, NKEY]),
                                            selt[:, 0, bass.ds(i * (2 * G) + b * G, G)].unsqueeze(2).to_broadcast([P, G, NKEY]),
                                            ALU.subtract).then_inc(rows_dist, 1)
                    g.wait_ge(rows_dist, i * 2 + b + 1)
                    g.sem_inc(passed, 1)
                    nc.gpsimd.tensor_scalar(rows[:, b], rows[:, b], 0.0, None, ALU.is_equal).then_inc(rows_done, 1)

        @block.vector
        def _(dve):
            st = Steps(dve, v)
            for w in range(3):
                dve.wait_ge(tr_done, w + 1)
                nc.vector.tensor_copy(selt[:, w, :], t_ps[:, w * T:(w + 1) * T]).then_inc(tr_stored, 1)
            dve.wait_ge(cst, 1)
            dve.wait_ge(tr_stored, 3)

            def pair(i):
                for b in range(2):
                    dve.wait_ge(g_done, i * 2 + b + 1)
                    at = bass.ds(i * (2 * G) + b * G, G)
                    st.then(nc.vector.tensor_tensor(cols[:, b], iota[:].unsqueeze(1).to_broadcast([P, G, NKEY]),
                                                    selt[:, 1, at].unsqueeze(2).to_broadcast([P, G, NKEY]), ALU.is_equal))
                    nc.vector.tensor_tensor(cols[:, b], cols[:, b],
                                            selt[:, 2, at].unsqueeze(2).to_broadcast([P, G, NKEY]), ALU.mult).then_inc(cols_done, 1)
            st.loop(T // (2 * G), 2, pair)

        @block.tensor
        def _(pe):
            for w in range(3):
                for t in range(TT):
                    last = nc.tensor.transpose(t_ps[:, w * T + t * P:w * T + (t + 1) * P], sel[:, w, t, :], K.ident[:])
                last.then_inc(tr_done, 1)
            pe.sem_inc(g_done, 2)
            with pe.Fori(0, T // (2 * G)) as i:
                for b in range(2):
                    pe.wait_ge(rows_done, i * 2 + b + 1)
                    pe.wait_ge(cols_done, i * 2 + b + 1)
                    pe.wait_ge(g_stored, i * 2 + b + 1)
                    for t in range(G):
                        last = nc.tensor.matmul(g_ps[:, b * 1024 + t * P:b * 1024 + (t + 1) * P], rows[:, b, t, :], cols[:, b, t, :],
                                                start=True, stop=True)
                    last.then_inc(g_done, 1)

        @block.scalar
        def _(act):
            act.sem_inc(g_stored, 2)

            def group(i, n, par, b):
                act.wait_ge(g_done, i + 3)
                nc.scalar.activation(slab[:, par, :, bass.ds(n * G, G)].rearrange("p i t -> p t i"),
                                     g_ps[:, b * 1024:b * 1024 + G * P].rearrange("p (t i) -> p t i", t=G),
                                     ACT.Copy).then_inc(g_stored, 1)

            for tt in range(TT):
                par = tt % 2
                if tt >= 2:
                    act.wait_ge(slab_out[par], 16)
                with act.Fori(0, groups // 2) as i:
                    for b in range(2):
                        group(i * 2 + (tt * groups + b), i * 2 + b, par, b)
                act.wait_ge(g_stored, (tt + 1) * groups + 2)
                act.dma_start(gates[tt], slab[:, par].rearrange("p i t -> p (i t)")).then_inc(slab_out[par], 16)
            for s in slab_out:
                act.wait_ge(s, 32)


def peer_experts(nc, K, d, gates):
    J = 8
    with Phase(nc, "experts") as ph:
        R = 4
        ring = ph.sb("ring", [P, R, KT * P])
        slab = ph.sb("slab", [P, R, TT, P])
        vals = ph.sb("vals", [P, J, D])
        act_sb = ph.sb("gelu", [P, 2, T])
        wact = ph.sb("wact", [P, J, T])
        acc = ph.sb("acc", [P, KT, T])
        a_ps = ph.banks("a_ps", 4)
        o_ps = ph.banks("o_ps", 4)
        ready = ph.sems(*[f"u_ready{i}" for i in range(R)])
        g_ready = ph.sems(*[f"g_ready{i}" for i in range(R)])
        v_ready, a_done, gelu_done, w_done, o_done, acc_done, v = ph.sems(
            "v_ready", "a_done", "gelu_done", "weighted_done", "o_done", "acc_done", "v")
        block = ph.block()
        n = NKEY // J
        g_h = gates.rearrange("b p (i t) -> i p b t", t=P)

        @block.sync
        def _(sp):
            for s in range(R):
                sp.dma_start(ring[:, s, :], d["peer_u"][s]).then_inc(ready[s], 16)
                sp.dma_start(slab[:, s], g_h[s]).then_inc(g_ready[s], 16)
            with sp.Fori(0, NKEY // R - 1) as i:
                for s in range(R):
                    sp.wait_ge(a_done, i * R + s + 1)
                    sp.dma_start(ring[:, s, :], d["peer_u"][i * R + (s + R)]).then_inc(ready[s], 16)
                    sp.wait_ge(w_done, i * R + (s + 2))
                    sp.dma_start(slab[:, s], g_h[i * R + (s + R)]).then_inc(g_ready[s], 16)

        @block.gpsimd
        def _(g):
            g.dma_start(vals[:], d["peer_v"][:, 0]).then_inc(v_ready, 16)
            with g.Fori(0, n - 1) as i:
                g.wait_ge(o_done, i * KT + KT)
                g.dma_start(vals[:], d["peer_v"][:, i + 1]).then_inc(v_ready, 16)

        @block.tensor
        def _(pe):
            with pe.Fori(0, n) as i:
                for j in range(J):
                    b = j % 4
                    pe.wait_ge(ready[b], i * 32 + 16 * (j // 4 + 1))
                    pe.wait_ge(gelu_done, i * J + j + 1)
                    for k in range(KT):
                        last = nc.tensor.matmul(a_ps[:, b * T:(b + 1) * T], ring[:, b, k * P:(k + 1) * P], K.h[:, k, :],
                                                start=k == 0, stop=k == KT - 1)
                    last.then_inc(a_done, 1)
                pe.wait_ge(v_ready, i * 16 + 16)
                for k in range(KT):
                    b = k % 4
                    pe.wait_ge(acc_done, i * KT + k + 1)
                    for j in range(J):
                        if k == 0:
                            pe.wait_ge(w_done, i * J + (j + 2))
                        last = nc.tensor.matmul(o_ps[:, b * T:(b + 1) * T], vals[:, j, k * P:(k + 1) * P], wact[:, j, :],
                                                start=j == 0, stop=j == J - 1)
                    last.then_inc(o_done, 1)

        @block.scalar
        def _(act):
            act.sem_inc(gelu_done, 4)
            with act.Fori(0, n) as i:
                for j in range(J):
                    act.wait_ge(a_done, i * J + j + 1)
                    if j >= 2:
                        act.wait_ge(w_done, i * J + j)
                    else:
                        act.wait_ge(w_done, i * J + 1)
                    nc.scalar.activation(act_sb[:, j % 2, :], a_ps[:, (j % 4) * T:(j % 4 + 1) * T], ACT.Gelu).then_inc(gelu_done, 1)

        @block.vector
        def _(dve):
            st = Steps(dve, v)
            dve.sem_inc(acc_done, 4)
            dve.sem_inc(w_done, 1)
            st.then(nc.vector.memset(acc[:], 0.0))
            with dve.Fori(0, n) as i:
                for j in range(J):
                    dve.wait_ge(gelu_done, i * J + j + 5)
                    dve.wait_ge(g_ready[j % 4], i * 32 + 16 * (j // 4 + 1))
                    nc.vector.tensor_tensor(wact[:, j, :], act_sb[:, j % 2, :], slab[:, j % 4].rearrange("p b t -> p (b t)"),
                                            ALU.mult).then_inc(w_done, 1)
                for k in range(KT):
                    dve.wait_ge(o_done, i * KT + k + 1)
                    dve.wait_ge(acc_done, i * KT + 4)
                    nc.vector.tensor_tensor(acc[:, k, :], acc[:, k, :], o_ps[:, (k % 4) * T:(k % 4 + 1) * T],
                                            ALU.add).then_inc(acc_done, 1)
            dve.wait_ge(acc_done, NKEY // J * KT + 4)
            for k in range(KT):
                st.do(nc.vector.scalar_tensor_tensor(out=K.x[:, k, :], in0=acc[:, k, :], scalar=K.mod[:, 40 + k:41 + k, 0],
                                                     in1=K.x[:, k, :], op0=ALU.mult, op1=ALU.add))
            st.sync()


def peer(nc, K, d):
    gates = nc.dram_tensor("peer_gates", (TT, P, NKEY * P), F32, kind="Internal").ap()
    with nc.sbuf_tensor("sel", [P, 3, TT, P], F32) as sel:
        peer_route(nc, K, d, sel)
        peer_gates(nc, K, d, sel, gates)
    peer_experts(nc, K, d, gates)


def lay_out_peer(w):
    u = w["peer_u"][0].reshape(NKEY, NKEY, KT, P)
    return {
        "peer_keys": np.ascontiguousarray(np.stack([w["peer_k1"][0].T, w["peer_k2"][0].T], 1)),
        "peer_wq": _tiles(w["peer_wq"][0]),
        "peer_u": np.ascontiguousarray(u.transpose(1, 3, 2, 0)).reshape(NKEY, P, D),
        "peer_v": w["peer_v"][0].reshape(NKEY, NKEY // 8, 8, D),
    }


def modulate(nc, K, s):
    at = 48 + 24 * s
    with Phase(nc, f"modulate{s}") as ph:
        a, v = ph.sems("a", "v")
        block = ph.block()

        @block.scalar
        def _(act):
            for k in range(0, KT, 2):
                nc.scalar.activation(K.h[:, k, :], K.x[:, k, :], ACT.Identity, scale=K.ops[:, s, k:k + 1],
                                     bias=K.mod[:, at + k, 2:3]).then_inc(a, 1)
            act.wait_ge(a, KT // 2)

        @block.vector
        def _(dve):
            for k in range(1, KT, 2):
                nc.vector.tensor_scalar(K.h[:, k, :], K.x[:, k, :], K.ops[:, s, k:k + 1], K.mod[:, at + k, 2:3],
                                        ALU.mult, ALU.add).then_inc(v, 1)
            dve.wait_ge(v, KT // 2)


def residual_alpha(nc, K, s, bias=None):
    def act_step(i, bank, buf):
        xk = K.x[:, bass.ds(i, 1), :].squeeze(1)
        if bias is None:
            return nc.scalar.activation(buf, xk, ACT.Copy, scale=ALPHA)
        return nc.scalar.activation(buf, xk, ACT.Identity, scale=ALPHA, bias=bias[:, bass.ds(i, 1)])

    def dve_step(dve, i, bank, buf):
        xk = K.x[:, bass.ds(i, 1), :].squeeze(1)
        return nc.vector.scalar_tensor_tensor(out=xk, in0=bank, scalar=K.ops[:, s, bass.ds(i + 8, 1)], in1=buf,
                                              op0=ALU.mult, op1=ALU.add)
    return act_step, dve_step


def mlp(nc, K, d, l):
    s = 2 * l + 1
    b1 = VEC["mlp_b1"][0] + 32 * l
    b2 = VEC["mlp_b2"][0] + 8 * l
    modulate(nc, K, s)
    with nc.sbuf_tensor(f"hidden{l}", [P, FF // P, T], F32) as hidden, nc.sbuf_tensor(f"gb2_{l}", [P, KT], F32) as gb2:
        def relu(i, bank, buf):
            return nc.scalar.activation(buf, bank, ACT.Relu, bias=K.vec[:, bass.ds(i + b1, 1)])

        def square(dve, i, bank, buf):
            return nc.vector.tensor_tensor(hidden[:, bass.ds(i, 1), :].squeeze(1), buf, buf, ALU.mult)

        linear_phase(nc, K, f"mlp1_{l}", d[f"mlp_w1_{l}"], K.h, KT, FF // P, (relu, square))
        gated_bias(nc, K, f"gb{l}", gb2, s, b2)
        linear_phase(nc, K, f"mlp2_{l}", d[f"mlp_w2_{l}"], hidden, FF // P, KT, residual_alpha(nc, K, s, gb2), R=2)
    g, b = VEC["ln_ffn_g"][0] + 8 * l, VEC["ln_ffn_b"][0] + 8 * l
    norm_phase(nc, K, f"ln_ffn{l}", [(K.x, K.x, T, K.vec[:, g:g + KT], K.vec[:, b:b + KT])], center=True)


def gated_bias(nc, K, name, out, s, b):
    with Phase(nc, name) as ph:
        v = ph.sems("v")
        block = ph.block()

        @block.vector
        def _(dve):
            nc.vector.tensor_tensor(out[:], K.ops[:, s, 8:16], K.vec[:, b:b + KT], ALU.mult).then_inc(v, 1)
            dve.wait_ge(v, 1)


TWO_PI = 2 * math.pi
C1 = 6.28125
C2 = float(np.float32(round((TWO_PI - C1) * 2 ** 22) / 2 ** 22))
C3 = float(np.float32(TWO_PI - C1 - C2))
PI_IN = 3.1415925


def reduce_angle(V, st, ang, n):
    st.then(V.tensor_scalar(n, ang, 1.0 / TWO_PI, ROUNDMAGIC, ALU.mult, ALU.add))
    st.then(V.tensor_scalar(n, n, ROUNDMAGIC, None, ALU.subtract))
    for c in (C1, C2, C3):
        st.then(V.scalar_tensor_tensor(out=ang, in0=n, scalar=-c, in1=ang, op0=ALU.mult, op1=ALU.add))


def quarter_turn(V, st, out, ang, n):
    st.then(V.tensor_scalar(out, ang, math.pi / 2, None, ALU.add))
    st.then(V.tensor_scalar(n, out, math.pi, None, ALU.is_gt))
    st.then(V.scalar_tensor_tensor(out=out, in0=n, scalar=-TWO_PI, in1=out, op0=ALU.mult, op1=ALU.add))
    st.then(V.tensor_scalar(out, out, PI_IN, -PI_IN, ALU.min, ALU.max))


QN = 192 ** -0.5


def mla(nc, K, d):
    modulate(nc, K, 0)
    with ExitStack() as c:
        cq = c.enter_context(nc.sbuf_tensor("cq", [P, 2, T], F32))
        ckv = c.enter_context(nc.sbuf_tensor("ckv", [P, T], F32))
        kpe = c.enter_context(nc.sbuf_tensor("kpe", [P, T], F32))
        csq = c.enter_context(nc.sbuf_tensor("csq", [P, T], F32))
        mla_in(nc, K, d, cq, ckv, kpe, csq)
        mla_heads(nc, K, d, cq, ckv, kpe, csq)
    linear_phase(nc, K, "mla_out", d["mla_wo"], K.h, KT, KT, residual_alpha(nc, K, 0))
    g, b = VEC["ln_mix_g"][0], VEC["ln_mix_b"][0]
    norm_phase(nc, K, "ln_mix0", [(K.x, K.x, T, K.vec[:, g:g + KT], K.vec[:, b:b + KT])], center=True)


def mla_in(nc, K, d, cq, ckv, kpe, csq):
    with Phase(nc, "mla_in") as ph:
        ring = ph.sb("ring", [P, 5, KT * P])
        pos = ph.sb("pos", [P, T], I32)
        ang = ph.sb("ang", [P, T])
        ang2 = ph.sb("ang2", [P, T])
        n = ph.sb("n", [P, T])
        zsq = ph.sb("zsq", [P, 3, T])
        rstd = ph.sb("rstd", [P, 2, T])
        z = ph.banks("z", 5)
        sums = ph.banks("sums", 2)
        w_in = ph.sems(*[f"w_in{i}" for i in range(5)])
        pos_in, z_done, v, ang_done, trig_done, sq_done, sum_done, rstd_done, a = ph.sems(
            "pos_in", "z_done", "v", "angle_done", "trig_done", "sq_done", "sum_done", "rstd_done", "a")
        block = ph.block()
        fq, sg = VEC["inv_freq"][0], VEC["rope_sign"][0]
        qn, kvn = VEC["q_norm"][0], VEC["kv_norm"][0]

        @block.sync
        def _(sp):
            sp.dma_start(pos[:], d["positions"].partition_broadcast(P)).then_inc(pos_in, 16)
            for t in range(5):
                sp.dma_start(ring[:, t, :], d["mla_win"][t]).then_inc(w_in[t], 16)

        @block.tensor
        def _(pe):
            for t in range(5):
                pe.wait_ge(w_in[t], 16)
                for k in range(KT):
                    last = nc.tensor.matmul(z[:, t * T:(t + 1) * T], ring[:, t, k * P:(k + 1) * P], K.h[:, k, :],
                                            start=k == 0, stop=k == KT - 1)
                last.then_inc(z_done, 1)
            pe.wait_ge(sq_done, 3)
            nc.tensor.matmul(sums[:, 0:T], K.ones[:], zsq[:, 0, :], start=True, stop=False)
            nc.tensor.matmul(sums[:, 0:T], K.ones[:], zsq[:, 1, :], start=False, stop=True)
            nc.tensor.matmul(sums[:, T:2 * T], K.ones[:], zsq[:, 2, :], start=True, stop=True).then_inc(sum_done, 1)

        @block.scalar
        def _(act):
            st = Steps(act, a)
            act.wait_ge(ang_done, 2)
            nc.scalar.activation(ang[:], ang[:], ACT.Sin).then_inc(trig_done, 1)
            nc.scalar.activation(ang2[:], ang2[:], ACT.Sin).then_inc(trig_done, 1)
            for t in range(3):
                act.wait_ge(z_done, t + 1)
                nc.scalar.activation(zsq[:, t, :], z[:, t * T:(t + 1) * T], ACT.Square).then_inc(sq_done, 1)
            act.wait_ge(sum_done, 1)
            st.do(nc.scalar.activation(rstd[:, 0, :], sums[:, 0:T], ACT.Ln, scale=1.0 / 256, bias=EPS))
            st.then(nc.scalar.activation(rstd[:, 1, :], sums[:, T:2 * T], ACT.Ln, scale=1.0 / 128, bias=EPS))
            nc.scalar.activation(rstd[:], rstd[:], ACT.Exp, scale=-0.5).then_inc(rstd_done, 1)

        @block.vector
        def _(dve):
            V = nc.vector
            st = Steps(dve, v)
            dve.wait_ge(pos_in, 16)
            st.then(V.tensor_copy(ang[:], pos[:]))
            st.then(V.tensor_scalar(ang[:], ang[:], K.vec[:, fq:fq + 1], None, ALU.mult))
            reduce_angle(V, st, ang[:], n[:])
            quarter_turn(V, st, ang2[:], ang[:], n[:])
            V.tensor_scalar(ang[:], ang[:], PI_IN, -PI_IN, ALU.min, ALU.max).then_inc(ang_done, 2)
            dve.wait_ge(trig_done, 2)
            st.then(V.tensor_scalar(ang[:], ang[:], K.vec[:, sg:sg + 1], None, ALU.mult))
            st.do(V.tensor_copy(csq[0:64, :], ang2[0:64, :]))
            st.do(V.tensor_copy(csq[64:128, :], ang[64:128, :]))
            dve.wait_ge(z_done, 5)
            st.do(V.tensor_tensor(n[:], ang2[:], z[:, 3 * T:4 * T], ALU.mult))
            st.then(V.tensor_tensor(kpe[:], ang[:], z[:, 4 * T:5 * T], ALU.mult))
            st.do(V.tensor_tensor(kpe[:], kpe[:], n[:], ALU.add))
            dve.wait_ge(rstd_done, 1)
            for t in range(3):
                out = cq[:, t, :] if t < 2 else ckv[:]
                g = K.vec[:, qn + t:qn + t + 1] if t < 2 else K.vec[:, kvn:kvn + 1]
                st.do(V.scalar_tensor_tensor(out=out, in0=z[:, t * T:(t + 1) * T], scalar=g, in1=rstd[:, t // 2, :],
                                             op0=ALU.mult, op1=ALU.mult))
            st.sync()


def mla_heads(nc, K, d, cq, ckv, kpe, csq):
    W = 2 * 256 + 128 + 128
    with Phase(nc, "mla") as ph:
        wts = ph.sb("wts", [P, 2, W])
        qn = ph.sb("qn", [P, 2, T])
        qp = ph.sb("qp", [P, 2, T])
        kn = ph.sb("kn", [P, 2, T])
        vt = ph.sb("vt", [P, 2, TT, P])
        big = ph.sb("mask", [P, TT * P])
        prob = ph.sb("prob", [P, 2, T])
        probt = ph.sb("probt", [P, 2, T])
        stat = ph.sb("stat", [P, 2, 3])
        sm = ph.sb("rowsum", [P, 2, 1])
        pr = ph.banks("proj", 4)
        sc = ph.banks("score", 2)
        tr = ph.banks("trans")
        op = ph.banks("out")
        w_ready = ph.sems("w_ready0", "w_ready1")
        (p_done, q_stored, qp_stored, s_done, masked, max_done, exp_done, prob_done, t_done, t_stored, o_done, o_stored,
         cst, v) = ph.sems("proj_done", "q_stored", "qpe_stored", "score_done", "masked", "max_done", "exp_done", "prob_done",
                           "trans_done", "trans_stored", "out_done", "out_stored", "consts", "v")
        block = ph.block()
        H = 8

        @block.gpsimd
        def _(g):
            nc.gpsimd.memset(big[:], 0.0).then_inc(cst, 1)
            g.wait_ge(cst, 1)
            nc.gpsimd.affine_select(out=big[:], in_=big[:], compare_op=ALU.is_ge, fill=-1.0e30, base=(TT - 1) * P,
                                    pattern=[[-1, TT * P]], channel_multiplier=1).then_inc(cst, 1)

        @block.sync
        def _(sp):
            for b in range(2):
                sp.dma_start(wts[:, b, :], d["mla_wh"][b]).then_inc(w_ready[b], 16)
            with sp.Fori(0, H // 2 - 1) as i:
                for b in range(2):
                    sp.wait_ge(p_done, i * 4 + 2 * b + 2)
                    sp.dma_start(wts[:, b, :], d["mla_wh"][i * 2 + (b + 2)]).then_inc(w_ready[b], 16)

        @block.tensor
        def _(pe):
            def project(i, b):
                pe.wait_ge(w_ready[b], i * 16 + 16)
                if b:
                    pe.wait_ge(q_stored, i * 6 + 3)
                    pe.wait_ge(qp_stored, i * 2 + 1)
                else:
                    pe.wait_ge(q_stored, i * 6)
                    pe.wait_ge(qp_stored, i * 2)
                for o, c in ((0, 0), (1, P)):
                    for k in range(2):
                        nc.tensor.matmul(pr[:, o * T:(o + 1) * T], wts[:, b, k * 256 + c:k * 256 + c + P], cq[:, k, :],
                                         start=k == 0, stop=k == 1)
                nc.tensor.matmul(pr[:, 2 * T:3 * T], wts[:, b, 512:640], ckv[:], start=True, stop=True).then_inc(p_done, 1)
                for t in range(TT):
                    last = nc.tensor.matmul(pr[:, 3 * T + t * P:3 * T + (t + 1) * P], ckv[:, t * P:(t + 1) * P], wts[:, b, 640:768],
                                            start=True, stop=True)
                last.then_inc(p_done, 1)

            def scores(i, b, qt):
                n = i * 8 + (b * 4 + qt)
                if qt == 0:
                    pe.wait_ge(q_stored, i * 6 + 3 * b + 3)
                    pe.wait_ge(qp_stored, i * 2 + b + 1)
                pe.wait_ge(masked, n + 1)
                o = (qt % 2) * T
                w = (qt + 1) * P
                nc.tensor.matmul(sc[:, o:o + w], qn[:, b, qt * P:w], kn[:, b, 0:w], start=True, stop=False)
                nc.tensor.matmul(sc[:, o:o + w], qp[:, b, qt * P:w], kpe[:, 0:w], start=False, stop=True).then_inc(s_done, 1)

            def weigh(i, b, qt):
                n = i * 8 + (b * 4 + qt)
                pe.wait_ge(prob_done, n + 1)
                pe.wait_ge(t_stored, n + 1)
                for k in range(qt + 1):
                    last = nc.tensor.transpose(tr[:, k * P:(k + 1) * P], prob[:, qt % 2, k * P:(k + 1) * P], K.ident[:])
                last.then_inc(t_done, 1)

            def output(i, b, qt):
                n = i * 8 + (b * 4 + qt)
                pe.wait_ge(t_stored, n + 2)
                if qt == 0:
                    pe.wait_ge(o_stored, i * 2 + b + 1)
                for k in range(qt + 1):
                    last = nc.tensor.matmul(op[:, qt * P:(qt + 1) * P], vt[:, b, k, :], probt[:, qt % 2, k * P:(k + 1) * P],
                                            start=k == 0, stop=k == qt)
                last.then_inc(o_done, 1)

            pe.sem_inc(t_done, 2)
            pe.sem_inc(o_done, 1)
            project(0, 0)
            scores(0, 0, 0)

            def head(i, b, nxt):
                scores(i, b, 1)
                weigh(i, b, 0)
                if nxt:
                    project(*nxt)
                output(i, b, 0)
                scores(i, b, 2)
                weigh(i, b, 1)
                output(i, b, 1)
                scores(i, b, 3)
                weigh(i, b, 2)
                output(i, b, 2)
                if nxt:
                    scores(*nxt, 0)
                weigh(i, b, 3)
                output(i, b, 3)

            with pe.Fori(0, H // 2 - 1) as i:
                head(i, 0, (i, 1))
                head(i, 1, (i + 1, 0))
            head(H // 2 - 1, 0, (H // 2 - 1, 1))
            head(H // 2 - 1, 1, None)

        @block.scalar
        def _(act):
            def store(i, b):
                act.wait_ge(p_done, i * 4 + 2 * b + 1)
                nc.scalar.activation(qn[:, b, :], pr[:, 0:T], ACT.Copy).then_inc(q_stored, 1)
                nc.scalar.activation(kn[:, b, :], pr[:, 2 * T:3 * T], ACT.Copy).then_inc(q_stored, 1)
                act.wait_ge(p_done, i * 4 + 2 * b + 2)
                nc.scalar.activation(vt[:, b], pr[:, 3 * T:4 * T].rearrange("p (t v) -> p t v", t=TT), ACT.Copy).then_inc(q_stored, 1)

            def exp(i, b, qt):
                n = i * 8 + (b * 4 + qt)
                w = (qt + 1) * P
                act.wait_ge(max_done, n + 1)
                nc.scalar.activation(prob[:, qt % 2, 0:w], prob[:, qt % 2, 0:w], ACT.Exp, scale=QN,
                                     bias=stat[:, qt % 2, 1:2], accum_out=sm[:, qt % 2, :]).then_inc(exp_done, 1)

            def store_t(i, b, qt):
                n = i * 8 + (b * 4 + qt)
                w = (qt + 1) * P
                act.wait_ge(t_done, n + 3)
                if qt >= 2:
                    act.wait_ge(o_done, n)
                else:
                    act.wait_ge(o_done, i * 8 + b * 4 + 1)
                nc.scalar.activation(probt[:, qt % 2, 0:w], tr[:, 0:w], ACT.Copy).then_inc(t_stored, 1)

            def head(i, b, nxt):
                exp(i, b, 1)
                store_t(i, b, 0)
                if nxt:
                    store(*nxt)
                exp(i, b, 2)
                store_t(i, b, 1)
                exp(i, b, 3)
                store_t(i, b, 2)
                if nxt:
                    exp(*nxt, 0)
                store_t(i, b, 3)
                act.wait_ge(o_done, i * 8 + b * 4 + 5)
                nc.scalar.activation(K.h[:, bass.ds(i * 2 + b, 1), :].squeeze(1), op[:, 0:T], ACT.Copy).then_inc(o_stored, 1)

            act.sem_inc(t_stored, 1)
            act.sem_inc(o_stored, 1)
            store(0, 0)
            exp(0, 0, 0)
            with act.Fori(0, H // 2 - 1) as i:
                head(i, 0, (i, 1))
                head(i, 1, (i + 1, 0))
            head(H // 2 - 1, 0, (H // 2 - 1, 1))
            head(H // 2 - 1, 1, None)
            act.wait_ge(o_stored, H + 1)

        @block.vector
        def _(dve):
            V = nc.vector
            st = Steps(dve, v)
            dve.wait_ge(cst, 2)
            dve.sem_inc(masked, 2)

            def store(i, b):
                dve.wait_ge(p_done, i * 4 + 2 * b + 1)
                V.tensor_tensor(qp[:, b, :], csq[:], pr[:, T:2 * T], ALU.mult).then_inc(qp_stored, 1)

            def logits(i, b, qt):
                n = i * 8 + (b * 4 + qt)
                w = (qt + 1) * P
                dve.wait_ge(s_done, n + 1)
                dve.wait_ge(t_done, n + 1)
                V.tensor_tensor(prob[:, qt % 2, 0:w], big[:, (TT - 1 - qt) * P:TT * P], sc[:, (qt % 2) * T:(qt % 2) * T + w],
                                ALU.add).then_inc(masked, 1)
                dve.wait_ge(masked, n + 3)
                st.then(V.reduce_max(stat[:, qt % 2, 0:1], prob[:, qt % 2, 0:w], AXX))
                V.tensor_scalar(stat[:, qt % 2, 1:2], stat[:, qt % 2, 0:1], -QN, None, ALU.mult).then_inc(max_done, 1)

            def normalize(i, b, qt):
                n = i * 8 + (b * 4 + qt)
                w = (qt + 1) * P
                dve.wait_ge(exp_done, n + 1)
                st.then(V.reciprocal(stat[:, qt % 2, 2:3], sm[:, qt % 2, :]))
                V.tensor_scalar(prob[:, qt % 2, 0:w], prob[:, qt % 2, 0:w], stat[:, qt % 2, 2:3], None, ALU.mult).then_inc(prob_done, 1)

            def head(i, b, nxt):
                logits(i, b, 1)
                normalize(i, b, 0)
                if nxt:
                    store(*nxt)
                normalize(i, b, 1)
                logits(i, b, 2)
                normalize(i, b, 2)
                logits(i, b, 3)
                if nxt:
                    logits(*nxt, 0)
                normalize(i, b, 3)

            store(0, 0)
            logits(0, 0, 0)
            n0 = st.n
            with dve.Fori(0, H // 2 - 1) as i:
                st.turn = i * 16
                head(i, 0, (i, 1))
                head(i, 1, (i + 1, 0))
            assert st.n - n0 == 16, st.n - n0
            st.n, st.turn = n0 + 16 * (H // 2 - 1), 0
            head(H // 2 - 1, 0, (H // 2 - 1, 1))
            head(H // 2 - 1, 1, None)


def lay_out_mla(w):
    wi = w["mla_w_in_2"][0]
    x1, x2 = wi[:, 384:416], wi[:, 416:448]
    wi = np.concatenate([wi[:, 0:384], x1, x2, x1, x2, x2, x1, x2, x1], 1)
    qb = w["mla_w_qb_2"][0].reshape(256, 8, 192)
    qb = np.concatenate([qb, qb[:, :, 160:192], qb[:, :, 128:160]], 2)
    kvb = w["mla_w_kvb_2"][0].reshape(128, 8, 256)
    wh = np.concatenate([qb[0:128].transpose(1, 0, 2), qb[128:256].transpose(1, 0, 2), kvb.transpose(1, 0, 2)], 2)
    return {"mla_win": _tiles(wi), "mla_wh": np.ascontiguousarray(wh), "mla_wo": _tiles(w["mla_w_o_2"][0]),
            "positions": np.asarray(w["positions_2"]).reshape(T)}


def lay_out_rest(w):
    a = {}
    for l in range(2):
        a[f"mlp_w1_{l}"] = _tiles(w["mlp_w1_2"][l])
        a[f"mlp_w2_{l}"] = _tiles(w["mlp_w2_2"][l])
    return a


LB, LA = 32, 16
NST = 32


def ssm(nc, K, d):
    modulate(nc, K, 2)
    with ExitStack() as c:
        def keep(name, shape):
            return c.enter_context(nc.sbuf_tensor(name, shape, F32))

        u = keep("ssm_u", [P, KT, T])
        g = keep("ssm_g", [P, KT, T])

        def store(dve, i, bank, buf):
            return nc.vector.tensor_copy(u[:, bass.ds(i, 1), :].squeeze(1), bank)

        linear_phase(nc, K, "ssm_in", d["ssm_win"], K.h, KT, KT, (None, store))
        with ExitStack() as c2:
            S = Consts()
            S.mag = c2.enter_context(nc.sbuf_tensor("s_mag", [P, NST], F32))
            S.cb = c2.enter_context(nc.sbuf_tensor("s_cb", [P, 2, NST, LB], F32))
            S.ca = c2.enter_context(nc.sbuf_tensor("s_ca", [P, 2, NST, LA], F32))
            S.bd = c2.enter_context(nc.sbuf_tensor("s_bd", [P, 2, NST, 32], F32))
            S.cd = c2.enter_context(nc.sbuf_tensor("s_cd", [P, 2, NST, 32], F32))
            ssm_tables(nc, K, d, S)
            ssm_scan(nc, K, d, S, u, g)
        bg = VEC["b_glu"][0]

        def gate(i, bank, buf):
            return nc.scalar.activation(buf, bank, ACT.Sigmoid, bias=K.vec[:, bass.ds(i + bg, 1)])

        def times(dve, i, bank, buf):
            return nc.vector.tensor_tensor(u[:, bass.ds(i, 1), :].squeeze(1), buf, g[:, bass.ds(i, 1), :].squeeze(1), ALU.mult)

        linear_phase(nc, K, "glu", d["ssm_wglu"], g, KT, KT, (gate, times))
        linear_phase(nc, K, "ssm_out", d["ssm_wout"], u, KT, KT, residual_alpha(nc, K, 2))
    gg, bb = VEC["ln_mix_g"][0] + 8, VEC["ln_mix_b"][0] + 8
    norm_phase(nc, K, "ln_mix1", [(K.x, K.x, T, K.vec[:, gg:gg + KT], K.vec[:, bb:bb + KT])], center=True)


def ssm_tables(nc, K, d, S):
    with Phase(nc, "tables") as ph:
        prm = ph.sb("prm", [P, 3, NST])
        bc = ph.sb("bc", [P, 4, NST, 16])
        w = ph.sb("w", [P, 14, NST])
        bb = ph.sb("bb", [P, 2, NST, 16])
        t1 = ph.sb("t1", [P, NST, 16])
        steps = ph.sb("steps", [P, LB])
        ang = ph.sb("ang", [P, NST, LB])
        ang2 = ph.sb("ang2", [P, NST, LB])
        n = ph.sb("n", [P, NST, LB])
        prm_in, cst, dt_done, mag_in, mag_done, ang_done, trig_done, v = ph.sems(
            "prm_in", "consts", "dt_done", "mag_arg", "mag_done", "angle_done", "trig_done", "v")
        block = ph.block()

        @block.sync
        def _(sp):
            sp.dma_start(prm[:], d["ssm_prm"]).then_inc(prm_in, 16)
            sp.dma_start(bc[:], d["ssm_bc"]).then_inc(prm_in, 16)

        @block.gpsimd
        def _(g):
            nc.gpsimd.iota(steps[:], [[1, LB]], base=0, channel_multiplier=0,
                           allow_small_or_imprecise_dtypes=True).then_inc(cst, 1)

        @block.scalar
        def _(act):
            act.wait_ge(prm_in, 32)
            nc.scalar.activation(w[:, 0, :], prm[:, 2, :], ACT.Exp).then_inc(dt_done, 1)
            act.wait_ge(mag_in, 1)
            nc.scalar.activation(S.mag[:], w[:, 1, :], ACT.Exp).then_inc(mag_done, 1)
            act.wait_ge(ang_done, 1)
            nc.scalar.activation(w[:, 4:6, :], w[:, 4:6, :], ACT.Sin).then_inc(trig_done, 1)
            for m, (t, l) in enumerate(((S.cb, LB), (S.ca, LA))):
                act.wait_ge(ang_done, m + 2)
                nc.scalar.activation(t[:, 1], ang[:, :, 0:l], ACT.Sin)
                nc.scalar.activation(t[:, 0], ang2[:, :, 0:l], ACT.Sin).then_inc(trig_done, 1)

        @block.vector
        def _(dve):
            V = nc.vector
            st = Steps(dve, v)
            lr, li = prm[:, 0, :], prm[:, 1, :]
            dt, m, th, th32, sn, cs, are, aim, den, rden, cre, cim, ta, tb = [w[:, k, :] for k in
                                                                            (0, 1, 2, 3, 4, 5, 6, 7, 8, 9, 10, 11, 12, 13)]
            dve.wait_ge(dt_done, 1)
            V.tensor_tensor(m, lr, dt, ALU.mult).then_inc(mag_in, 1)
            st.then(V.tensor_tensor(th, li, dt, ALU.mult))
            reduce_angle(V, st, th, ta)
            st.then(V.tensor_scalar(th, th, PI_IN, -PI_IN, ALU.min, ALU.max))
            st.then(V.tensor_scalar(th32, th, float(LB), None, ALU.mult))
            reduce_angle(V, st, th32, ta)
            quarter_turn(V, st, cs, th, ta)
            V.tensor_copy(sn, th).then_inc(ang_done, 1)
            dve.wait_ge(trig_done, 1)
            dve.wait_ge(mag_done, 1)
            st.then(V.tensor_tensor(are, S.mag[:], cs, ALU.mult))
            st.then(V.tensor_tensor(aim, S.mag[:], sn, ALU.mult))
            st.then(V.tensor_scalar(are, are, -1.0, None, ALU.add))
            st.do(V.tensor_tensor(ta, lr, lr, ALU.mult))
            st.then(V.tensor_tensor(tb, li, li, ALU.mult))
            st.then(V.tensor_tensor(den, ta, tb, ALU.add))
            st.then(V.reciprocal(rden, den))
            for out, x, y, op in ((cre, (are, lr), (aim, li), ALU.add), (cim, (aim, lr), (are, li), ALU.subtract)):
                st.do(V.tensor_tensor(ta, *x, ALU.mult))
                st.then(V.tensor_tensor(tb, *y, ALU.mult))
                st.then(V.tensor_tensor(out, ta, tb, op))
                st.then(V.tensor_tensor(out, out, rden, ALU.mult))

            def wide(x):
                return x.unsqueeze(2).to_broadcast([P, NST, 16])
            br, bi = bc[:, 0], bc[:, 1]
            for k, (x, y, op) in enumerate((((br, cre), (bi, cim), ALU.subtract), ((bi, cre), (br, cim), ALU.add))):
                st.do(V.tensor_tensor(bb[:, k], x[0], wide(x[1]), ALU.mult))
                st.then(V.tensor_tensor(t1[:], y[0], wide(y[1]), ALU.mult))
                st.then(V.tensor_tensor(bb[:, k], bb[:, k], t1[:], op))
            st.do(V.memset(S.bd[:], 0.0))
            st.then(V.memset(S.cd[:], 0.0))
            for k in range(2):
                for hf in range(2):
                    r, c = slice(64 * hf, 64 * hf + 64), slice(16 * hf, 16 * hf + 16)
                    st.do(V.tensor_copy(S.bd[r, k, :, c], bb[r, k]))
                    st.do(V.tensor_scalar(S.cd[r, k, :, c], bc[r, 2 + k], (1.0, -1.0)[k], None, ALU.mult))
            dve.wait_ge(cst, 1)
            for m_, (x, l) in enumerate(((th, LB), (th32, LA))):
                if m_:
                    dve.wait_ge(trig_done, 2)
                st.then(V.tensor_tensor(ang[:, :, 0:l], x.unsqueeze(2).to_broadcast([P, NST, l]),
                                        steps[:, 0:l].unsqueeze(1).to_broadcast([P, NST, l]), ALU.mult))
                reduce_angle(V, st, ang[:, :, 0:l], n[:, :, 0:l])
                quarter_turn(V, st, ang2[:, :, 0:l], ang[:, :, 0:l], n[:, :, 0:l])
                V.tensor_scalar(ang[:, :, 0:l], ang[:, :, 0:l], PI_IN, -PI_IN, ALU.min, ALU.max).then_inc(ang_done, 1)
            st.sync()


def ssm_scan(nc, K, d, S, u, g):
    with Phase(nc, "scan") as ph:
        bst = ph.sb("bst", [P, 2, P])
        bt = ph.sb("bt", [P, 2, P])
        ust = ph.sb("ust", [P, T])
        ct = ph.sb("ct", [P, 2, 4, 32])
        rot = ph.sb("rot", [P, 2, 2, T])
        tmp = ph.sb("tmp", [P, 2, T])
        bu = ph.sb("bu", [P, 2, T])
        wv = ph.sb("wv", [P, 2, T])
        m = ph.sb("m", [P, 4, T])
        xs = ph.sb("xs", [P, 2, 2, T])
        yb = ph.sb("yb", [P, T])
        b_ps = ph.banks("b_ps")
        bu_ps = ph.banks("bu_ps", 4)
        y_ps = ph.banks("y_ps", 2)
        staged, bt_done, bt_stored, bu_done, bu_read, rot_done, rot_used, x_done, y_done, yb_done, g_done, v, gp = ph.sems(
            "staged", "bt_done", "bt_stored", "bu_done", "bu_read", "rot_done", "rot_used", "x_done", "y_done", "yb_done", "g_done", "v", "g")
        block = ph.block()
        dcol = VEC["ssm_d"][0]

        @block.gpsimd
        def _(eng):
            st = Steps(eng, gp)
            G = nc.gpsimd

            def turn(i):
                for t in range(4):
                    b = t % 2
                    eng.wait_ge(rot_used, i * 4 + (t + 1))
                    ca = [S.ca[:, k, bass.ds(i * 4 + t, 1), :].squeeze(1).unsqueeze(2).to_broadcast([P, LA, LB]) for k in range(2)]
                    cb = [S.cb[:, k, bass.ds(i * 4 + t, 1), :].squeeze(1).unsqueeze(1).to_broadcast([P, LA, LB]) for k in range(2)]
                    r = [rot[:, b, k, :].rearrange("p (a b) -> p a b", b=LB) for k in range(2)]
                    q = [tmp[:, k, :].rearrange("p (a b) -> p a b", b=LB) for k in range(2)]
                    st.do(G.tensor_tensor(r[0], ca[0], cb[0], ALU.mult))
                    st.do(G.tensor_tensor(q[0], ca[1], cb[1], ALU.mult))
                    st.do(G.tensor_tensor(r[1], ca[1], cb[0], ALU.mult))
                    st.do(G.tensor_tensor(q[1], ca[0], cb[1], ALU.mult))
                    st.sync()
                    G.tensor_tensor(r[0], r[0], q[0], ALU.subtract).then_inc(rot_done, 1)
                    G.tensor_tensor(r[1], r[1], q[1], ALU.add).then_inc(rot_done, 1)
                    eng.wait_ge(rot_done, i * 8 + (2 * t + 2))
            st.loop(KT, 16, turn)

        @block.tensor
        def _(pe):
            pe.sem_inc(y_done, 1)
            with pe.Fori(0, KT) as i:
                pe.wait_ge(staged, i * 2 + 1)
                for k in range(2):
                    last = nc.tensor.transpose(b_ps[:, k * P:(k + 1) * P], bst[:, k, :], K.ident[:])
                last.then_inc(bt_done, 1)
                pe.wait_ge(bt_stored, i + 2)

                def inputs(t):
                    pe.wait_ge(bu_read, i * 4 + (t + 1))
                    r = slice(32 * t, 32 * t + 32)
                    for k in range(2):
                        o = (2 * (t % 2) + k) * T
                        last = nc.tensor.matmul(bu_ps[:, o:o + T], bt[r, k, :], ust[r, :], start=True, stop=True)
                    last.then_inc(bu_done, 1)

                def outputs(t):
                    pe.wait_ge(x_done, i * 8 + (2 * t + 2))
                    for k in range(2):
                        last = nc.tensor.matmul(y_ps[32 * t:32 * t + 32, 0:T], ct[:, k, t, :], xs[:, t % 2, k, :], start=k == 0, stop=k == 1)
                    last.then_inc(y_done, 1)

                inputs(0)
                inputs(1)
                pe.wait_ge(yb_done, i + 1)
                for t in range(4):
                    outputs(t)
                    if t < 2:
                        inputs(t + 2)

        @block.scalar
        def _(act):
            act.sem_inc(bt_stored, 1)
            act.sem_inc(g_done, 1)
            with act.Fori(0, KT) as i:
                act.wait_ge(bt_done, i + 1)
                act.wait_ge(yb_done, i + 1)
                nc.scalar.activation(ust[:], u[:, bass.ds(i, 1), :].squeeze(1), ACT.Copy)
                nc.scalar.activation(bt[:], b_ps[:, 0:2 * P].rearrange("p (k s) -> p k s", k=2), ACT.Copy).then_inc(bt_stored, 1)
                act.wait_ge(yb_done, i + 2)
                nc.scalar.activation(g[:, bass.ds(i, 1), :].squeeze(1), yb[:], ACT.Gelu_apprx_tanh).then_inc(g_done, 1)
            act.wait_ge(g_done, KT + 1)

        @block.vector
        def _(dve):
            V = nc.vector
            st = Steps(dve, v)
            dve.sem_inc(rot_used, 2)
            dve.sem_inc(yb_done, 1)
            dve.sem_inc(bu_read, 2)

            def turn(i):
                dve.wait_ge(bt_stored, i + 1)
                V.tensor_copy(bst[:].rearrange("p k (t c) -> p k t c", c=32), S.bd[:, :, bass.ds(i * 4, 4), :]).then_inc(staged, 1)
                dve.wait_ge(y_done, i * 4 + 1)
                V.tensor_copy(ct[:], S.cd[:, :, bass.ds(i * 4, 4), :]).then_inc(staged, 1)
                for t in range(4):
                    b = t % 2
                    dve.wait_ge(bu_done, i * 4 + (t + 1))
                    dve.wait_ge(rot_done, i * 8 + (2 * t + 2))
                    co, si = rot[:, b, 0, :], rot[:, b, 1, :]
                    br = bu_ps[:, 2 * b * T:(2 * b + 1) * T]
                    bi = bu_ps[:, (2 * b + 1) * T:(2 * b + 2) * T]
                    st.do(V.tensor_tensor(m[:, 0, :], co, br, ALU.mult))
                    st.do(V.tensor_tensor(m[:, 1, :], si, bi, ALU.mult))
                    st.do(V.tensor_tensor(m[:, 2, :], co, bi, ALU.mult))
                    V.tensor_tensor(m[:, 3, :], si, br, ALU.mult).then_inc(bu_read, 1)
                    st.sync()
                    dve.wait_ge(bu_read, i * 4 + (t + 3))
                    st.do(V.tensor_tensor(bu[:, 0, :], m[:, 0, :], m[:, 1, :], ALU.add))
                    st.then(V.tensor_tensor(bu[:, 1, :], m[:, 2, :], m[:, 3, :], ALU.subtract))
                    mg = S.mag[:, bass.ds(i * 4 + t, 1)].to_broadcast([P, T])
                    for k in range(2):
                        st.do(V.tensor_tensor_scan(wv[:, k, :], mg, bu[:, k, :], 0.0, ALU.mult, ALU.add))
                    st.sync()
                    dve.wait_ge(y_done, i * 4 + (t if t >= 2 else 1))
                    st.do(V.tensor_tensor(m[:, 0, :], co, wv[:, 0, :], ALU.mult))
                    st.do(V.tensor_tensor(m[:, 1, :], si, wv[:, 1, :], ALU.mult))
                    st.do(V.tensor_tensor(m[:, 2, :], co, wv[:, 1, :], ALU.mult))
                    V.tensor_tensor(m[:, 3, :], si, wv[:, 0, :], ALU.mult).then_inc(rot_used, 1)
                    st.sync()
                    dve.wait_ge(rot_used, i * 4 + (t + 3))
                    V.tensor_tensor(xs[:, b, 0, :], m[:, 0, :], m[:, 1, :], ALU.subtract).then_inc(x_done, 1)
                    V.tensor_tensor(xs[:, b, 1, :], m[:, 2, :], m[:, 3, :], ALU.add).then_inc(x_done, 1)
                    dve.wait_ge(x_done, i * 8 + (2 * t + 2))
                dve.wait_ge(y_done, i * 4 + 5)
                dve.wait_ge(g_done, i + 1)
                V.scalar_tensor_tensor(out=yb[:], in0=ust[:], scalar=K.vec[:, bass.ds(i + dcol, 1)],
                                       in1=y_ps[:, 0:T], op0=ALU.mult, op1=ALU.add).then_inc(yb_done, 1)
            st.loop(KT, 40, turn)


def lay_out_ssm(w):
    def states(v):
        v = np.asarray(v)
        return np.moveaxis(v.reshape((NST, P) + v.shape[2:]), 0, 1)
    ldt = np.broadcast_to(w["ssm_log_dt_2"][0][:, None], (64, 64))
    prm = np.stack([states(w["ssm_a_re_2"][0]), states(w["ssm_a_im_2"][0]), states(ldt)], 1)
    bc = np.stack([states(w["ssm_b_re_2"][0]), states(w["ssm_b_im_2"][0]),
                   states(w["ssm_c_re_2"][0].transpose(0, 2, 1)), states(w["ssm_c_im_2"][0].transpose(0, 2, 1))], 1)
    return {"ssm_prm": np.ascontiguousarray(prm), "ssm_bc": np.ascontiguousarray(bc), "ssm_win": _tiles(w["ssm_w_in_2"][0]),
            "ssm_wglu": _tiles(w["ssm_w_glu_2"][0]), "ssm_wout": _tiles(w["ssm_w_out_2"][0])}


class Consts:
    pass


def residual(K, gate):
    def step(dve, i, bank, buf):
        xk = K.x[:, bass.ds(i, 1), :].squeeze(1)
        return dve.bass.vector.scalar_tensor_tensor(out=xk, in0=bank, scalar=gate[:, bass.ds(i, 1)],
                                                    in1=xk, op0=ALU.mult, op1=ALU.add)
    return step


def build(nc, d, out, upto=99):
    SPENT.clear()
    ctx = ExitStack()
    with ctx:
        K = Consts()


        K.x = ctx.enter_context(nc.sbuf_tensor("x", [P, KT, T], F32))
        K.h = ctx.enter_context(nc.sbuf_tensor("h", [P, KT, T], F32))
        K.vec = ctx.enter_context(nc.sbuf_tensor("vec", [P, NVEC], F32))
        K.mod = ctx.enter_context(nc.sbuf_tensor("modv", [P, MOD_TILES, 3], F32))
        K.ops = ctx.enter_context(nc.sbuf_tensor("ops", [P, 4, 16], F32))
        K.gs_mix = ctx.enter_context(nc.sbuf_tensor("gs_mix", [P, KT], F32))
        K.gs_ctx = ctx.enter_context(nc.sbuf_tensor("gs_ctx", [P, KT], F32))
        K.gs_ffn = ctx.enter_context(nc.sbuf_tensor("gs_ffn", [P, KT], F32))
        K.ones = ctx.enter_context(nc.sbuf_tensor("ones", [P, P], F32))
        K.ident = ctx.enter_context(nc.sbuf_tensor("ident", [P, P], F32))
        K.lb = ctx.enter_context(nc.sbuf_tensor("lb", [P, 16], F32))
        K.oml = ctx.enter_context(nc.sbuf_tensor("oml", [P, 16], F32))

        with ExitStack() as mix:
            K.hc = mix.enter_context(nc.sbuf_tensor("hc", [P, KT, TC], F32))
            K.segf = mix.enter_context(nc.sbuf_tensor("segf", [P, T + TC], F32))
            K.segb = mix.enter_context(nc.sbuf_tensor("segb", [P, T + TC], F32))
            K.tri = mix.enter_context(nc.sbuf_tensor("tri", [CH, 2, CH], F32))
            K.triu = mix.enter_context(nc.sbuf_tensor("triu", [CH, 2, NCH, CH], U32))
            setup_and_modulation(nc, K, d)
            if upto >= 1:
                norm_phase(nc, K, "norm1", [(K.x, K.h, T, K.gs_mix, K.mod[:, 0:8, 0]),
                                            (K.hc, K.hc, TC, K.gs_ctx, K.mod[:, 0:8, 1])])
            y_hg = mix.enter_context(nc.sbuf_tensor("y_hg", [P, HG_H, T], F32))
            g0 = VEC["hgrn_norm_g"][0]
            if upto >= 2:
                heads_phase(nc, K, d, "hgrn", d["w_hg"], HG_H, 1, K.vec[:, g0:g0 + 1], y_hg, 1.0)
            y_gla = K.x
            if upto >= 3:
                with nc.sbuf_tensor("log_gates", [P, 2 * GLA_H, T + TC], F32) as lg:
                    lora_gates(nc, K, d, lg)
                    g1 = VEC["gla_norm_g"][0]
                    if upto >= 4:
                        heads_phase(nc, K, d, "gla", d["w_gla"], GLA_H, GLA_VT, K.vec[:, g1:g1 + 2], y_gla, 1.0 / 16.0, lg)
            if upto >= 5:
                with nc.sbuf_tensor("merged", [P, KT, T], F32) as merged:
                    merge_phase(nc, K, d, y_hg, y_gla, merged)
                    load_x(nc, K, d)
                    linear_phase(nc, K, "wo", d["w_out"], merged, KT, KT, (None, residual(K, K.mod[:, 16:24, 0])))
            dump = {1: K.h, 2: y_hg, 3: lg if upto == 3 else None, 4: y_gla}.get(upto, K.x)
            if 0 <= upto < 6:
                store_out(nc, dump, out)
                return
        if upto < 0:
            load_x(nc, K, d)
            [lambda: mla(nc, K, d), lambda: mlp(nc, K, d, 0), lambda: ssm(nc, K, d), lambda: mlp(nc, K, d, 1)][-upto - 7]()
        if upto >= 6:
            recycle(nc)
            norm_phase(nc, K, "norm2", [(K.x, K.h, T, K.gs_ffn, K.mod[:, 24:32, 0])])
            peer(nc, K, d)
            f = VEC["final_g"][0]
            norm_phase(nc, K, "normf", [(K.x, K.x, T, K.vec[:, f:f + KT], None)])
        if upto >= 7:
            recycle(nc)
            mla(nc, K, d)
        if upto >= 8:
            mlp(nc, K, d, 0)
        if upto >= 9:
            recycle(nc)
            ssm(nc, K, d)
        if upto >= 10:
            mlp(nc, K, d, 1)
        store_out(nc, K.x, out)


def load_x(nc, K, d):
    with Phase(nc, "load_x") as ph:
        loaded = ph.sems("loaded")
        block = ph.block()

        @block.sync
        def _(sp):
            sp.dma_start(K.x[:], d["xT"].rearrange("(k p) t -> p k t", p=P)).then_inc(loaded, 16)
            sp.wait_ge(loaded, 16)


def store_out(nc, x, out):
    with Phase(nc, "out") as ph:
        stored = ph.sems("stored")
        block = ph.block()

        @block.sync
        def _(sp):
            sp.dma_start(out.rearrange("(k p) t -> p k t", p=P), x[:, 0:KT, 0:T]).then_inc(stored, 16)
            sp.wait_ge(stored, 16)


def _tiles(w):
    k, m = w.shape
    return np.ascontiguousarray(w.reshape(k // P, P, m // P, P).transpose(2, 1, 0, 3).reshape(m // P, P, k))


def _cols(v):
    return np.asarray(v).reshape(-1, P).T


def lay_out(inp):
    w = {k: np.asarray(v) for k, v in inp.items()}
    a = {}
    a["xT"] = np.ascontiguousarray(w["x"][0].T)
    a["ctxT"] = np.ascontiguousarray(w["ctx"][0].T)
    inv = (np.float32(10000.0) ** (-np.arange(0, 64, 2, dtype=np.float32) / np.float32(64))).astype(np.float32)
    order = {
        "c": _cols(w["c"][0]), "c_ctx": _cols(w["c_ctx"]), "c_2": _cols(w["c_2"][0]),
        "mod_b": np.concatenate([_cols(w["ada_b"][0]), _cols(w["mod_mix_b_2"][0]), _cols(w["mod_ffn_b_2"][0]),
                                 _cols(w["mod_mix_b_2"][1]), _cols(w["mod_ffn_b_2"][1])], 1),
        "norm_mix_g": _cols(w["norm_mix_g"][0]), "lb_logits": _cols(w["hgrn_lb_logits"].reshape(-1)),
        "hgrn_norm_g": _cols(w["hgrn_norm_g"][0]), "gk_b": _cols(w["gla_gk_b"][0].reshape(-1)),
        "gla_norm_g": _cols(w["gla_norm_g"][0]), "norm_ffn_g": _cols(w["norm_ffn_g"][0]), "final_g": _cols(w["final_g"]),
        "q_norm": _cols(w["mla_q_norm_2"][0]), "kv_norm": _cols(w["mla_kv_norm_2"][0]), "ssm_d": _cols(w["ssm_d_2"][0]),
        "b_glu": _cols(w["ssm_b_glu_2"][0]), "mlp_b1": _cols(w["mlp_b1_2"].reshape(-1)), "mlp_b2": _cols(w["mlp_b2_2"].reshape(-1)),
        "ln_mix_g": _cols(w["ln_mix_g_2"].reshape(-1)), "ln_mix_b": _cols(w["ln_mix_b_2"].reshape(-1)),
        "ln_ffn_g": _cols(w["ln_ffn_g_2"].reshape(-1)), "ln_ffn_b": _cols(w["ln_ffn_b_2"].reshape(-1)),
        "inv_freq": np.tile(inv, 4).reshape(P, 1),
        "rope_sign": np.where(np.arange(P) % 64 < 32, -1.0, 1.0).astype(np.float32).reshape(P, 1),
    }
    a["vec"] = np.ascontiguousarray(np.concatenate([order[n] for n, _ in VEC_SIZES], 1))
    a["w_mod"] = np.concatenate([_tiles(w["ada_w"][0]), _tiles(w["mod_mix_w_2"][0]), _tiles(w["mod_ffn_w_2"][0]),
                                 _tiles(w["mod_mix_w_2"][1]), _tiles(w["mod_ffn_w_2"][1])])
    wi = w["w_in"][0]
    at = np.cumsum([0, 1024, 1024, 1024, 1024, 1024, 512, 512, 1024, 1024, 16, 16, 1024, 1024])
    hq, ff, fb, hi, hg, gq, gk, gv, gg, _, _, mh, mg = [wi[:, at[i]:at[i + 1]] for i in range(13)]
    t = {n: _tiles(x) for n, x in dict(hq=hq, ff=ff, fb=fb, hi=hi, hg=hg, gq=gq, gk=gk, gv=gv, gg=gg, mh=mh, mg=mg).items()}
    a["w_hg"] = np.stack([t["ff"], t["fb"], t["hi"], t["hq"], t["hg"]], 1).reshape(-1, P, D)
    a["w_gla"] = np.stack([t["gk"], t["gv"][0::2], t["gv"][1::2], t["gq"], t["gg"][0::2], t["gg"][1::2]], 1).reshape(-1, P, D)
    a["w_gr"] = np.ascontiguousarray(wi[:, at[9]:at[11]])
    a["gk_w"] = w["gla_gk_w"][0]
    a["w_merge"] = np.stack([t["mh"], _tiles(w["w_branch_hgrn"][0]), t["mg"], _tiles(w["w_branch_gla"][0])], 1).reshape(-1, P, D)
    a["w_out"] = _tiles(w["w_out"][0])
    a.update(lay_out_peer(w))
    a.update(lay_out_mla(w))
    a.update(lay_out_rest(w))
    a.update(lay_out_ssm(w))
    return a


def kernel(**inputs):
    import concourse.bacc as _bacc
    from concourse.bass_utils import run_bass_kernel_spmd as _run

    nc = _bacc.Bacc("TRN2", target_bir_lowering=False, num_devices=1)
    arrays = lay_out(inputs)
    d = {n: nc.dram_tensor(f"in_{n}", a.shape, mybir.dt.from_np(a.dtype), kind="ExternalInput").ap() for n, a in arrays.items()}
    out = nc.dram_tensor("out_0", (D, T), F32, kind="ExternalOutput").ap()
    build(nc, d, out)
    r = _run(nc, [{f"in_{n}": a for n, a in arrays.items()}], core_ids=[0])
    return np.ascontiguousarray(r.results[0]["out_0"].T)[None]
```

```python
import concourse.bass as bass
from concourse import mybir
from contextlib import ExitStack
import math
import numpy as np

F32 = mybir.dt.float32
U32 = mybir.dt.uint32
I32 = mybir.dt.int32
F32R = mybir.dt.float32r
ALU = mybir.AluOpType
ACT = mybir.ActivationFunctionType
AXX = mybir.AxisListType.X

P = 128
T = 512
TC = 256
D = 1024
KT = D // P
CH = 64
NCH = T // CH
EPS = 1e-6
LN_EPS = 1e-5
ALPHA = 4 ** 0.25
HG_H, GLA_H = 8, 4
GLA_VT = 2
PEER_H, NKEY, TOPK = 8, 128, 16
TT = T // P
FF = 4096
ROUNDMAGIC = 12582912.0

VEC_SIZES = [
    ("mod_b", 144), ("norm_mix_g", 8), ("lb_logits", 32),
    ("hgrn_norm_g", 1), ("gk_b", 8), ("gla_norm_g", 2), ("norm_ffn_g", 8), ("final_g", 8),
    ("q_norm", 2), ("kv_norm", 1), ("ssm_d", 8), ("b_glu", 8), ("mlp_b1", 64), ("mlp_b2", 16),
    ("ln_mix_g", 16), ("ln_mix_b", 16), ("ln_ffn_g", 16), ("ln_ffn_b", 16), ("inv_freq", 1), ("rope_sign", 1),
]
VEC = {}
_at = 0
for _n, _k in VEC_SIZES:
    VEC[_n] = (_at, _k)
    _at += _k
NVEC = _at
MOD_TILES = 48 + 4 * 24


class Steps:

    def __init__(self, eng, sem):
        self.eng, self.sem, self.n, self.turn = eng, sem, 0, 0

    def do(self, ins):
        self.n += 1
        ins.then_inc(self.sem, 1)

    def sync(self, passed=None):
        self.eng.wait_ge(self.sem, self.turn + self.n)
        if passed is not None:
            self.eng.sem_inc(passed, 1)

    def then(self, ins):
        self.do(ins)
        self.sync()

    def loop(self, n, per, body):
        at = self.n
        with self.eng.Fori(0, n) as i:
            self.turn = i * per if per else 0
            body(i)
        assert self.n - at == per, (self.sem, self.n - at)
        self.n, self.turn = at + per * n, 0


SPENT = []


def recycle(nc):
    nc.all_engine_barrier()
    nc.clear_and_free_semaphores(list(SPENT))
    nc.all_engine_barrier()
    SPENT.clear()


class Phase:

    def __init__(self, nc, name):
        self.nc, self.name, self.ctx = nc, name, ExitStack()

    def __enter__(self):
        self.ctx.__enter__()
        return self

    def __exit__(self, *a):
        return self.ctx.__exit__(*a)

    def sb(self, name, shape, dt=F32):
        return self.ctx.enter_context(self.nc.sbuf_tensor(f"{self.name}_{name}", shape, dt))

    def banks(self, name, n=1):
        return self.ctx.enter_context(self.nc.psum_tensor(f"{self.name}_{name}", [P, n * 512], F32))

    def sems(self, *names):
        out = [self.nc.alloc_semaphore(f"{self.name}_{n}") for n in names]
        SPENT.extend(out)
        return out if len(out) > 1 else out[0]

    def block(self):
        return self.ctx.enter_context(self.nc.Block())


def stream(sp, slots, tiles, n, ready, used):
    r = len(slots)
    for s in range(min(r, n)):
        sp.dma_start(slots[s], tiles(s)).then_inc(ready[s], 16)
    if n > r:
        assert n % r == 0
        with sp.Fori(0, n // r - 1) as i:
            for s in range(r):
                sp.wait_ge(used, i * r + (s + 1))
                sp.dma_start(slots[s], tiles(i * r + (r + s))).then_inc(ready[s], 16)


class Modulation:

    def __init__(self, nc, K, ph, d, first, tiles, R, vecs):
        self.nc, self.K, self.d, self.first, self.tiles, self.vecs = nc, K, d, first, tiles, vecs
        V = len(vecs)
        self.ring = ph.sb("mod_ring", [P, R, D])
        self.rows = ph.sb("c_rows", [P, V, D])
        self.prod = ph.sb("mod_prod", [P, V, D])
        self.ready = ph.sems(*[f"mod_in{i}" for i in range(R)])
        self.rows_in, self.sig, self.silu, self.multiplied, self.summed, self.v = ph.sems(
            "c_rows_in", "c_sigmoid", "c_silu", "mod_multiplied", "mod_summed", "mod_biased")

    def load(self, eng):
        for n, (row, _) in enumerate(self.vecs):
            eng.dma_start(self.rows[:, n, :], self.d["c_rows"][row].partition_broadcast(P)).then_inc(self.rows_in, 16)
        stream(eng, [self.ring[:, s, :] for s in range(self.ring.shape[1])], lambda t: self.d["w_mod"][t + self.first],
               self.tiles, self.ready, self.multiplied)

    def start_act(self, act):
        V = len(self.vecs)
        act.sem_inc(self.summed, V)
        act.wait_ge(self.rows_in, 16 * V)
        self.nc.scalar.activation(self.prod[:], self.rows[:], ACT.Sigmoid).then_inc(self.sig, 1)

    def start_mul(self, eng, V_):
        eng.wait_ge(self.sig, 1)
        V_.tensor_tensor(self.rows[:], self.rows[:], self.prod[:], ALU.mult).then_inc(self.silu, 1)
        eng.wait_ge(self.silu, 1)

    def multiply(self, eng, V_, n, slot, at):
        V = len(self.vecs)
        eng.wait_ge(self.ready[slot], at + 16)
        for u in range(V):
            eng.wait_ge(self.summed, n * V + (u + 1))
            ins = V_.tensor_tensor(self.prod[:, u, :], self.ring[:, slot, :], self.rows[:, u, :], ALU.mult)
            ins.then_inc(self.multiplied if u == V - 1 else self.silu, 1)

    def sum(self, act, n):
        for u, (_, at) in enumerate(self.vecs):
            V = len(self.vecs)
            act.wait_ge(*((self.multiplied, n + 1) if u == V - 1 else (self.silu, n + 2)))
            self.nc.scalar.activation(self.prod[:, u, :], self.prod[:, u, :], ACT.Copy,
                                      accum_out=self.K.mod[:, bass.ds(n + at, 1)]).then_inc(self.summed, 1)

    def finish(self, eng, V_):
        V, n = len(self.vecs), self.tiles
        st = Steps(eng, self.v)
        b = VEC["mod_b"][0] + self.first
        eng.wait_ge(self.summed, V * (n + 1))
        for _, at in self.vecs:
            m = self.K.mod[:, at:at + n]
            st.do(V_.tensor_tensor(m, m, self.K.vec[:, b:b + n], ALU.add))
        st.sync()
        return st


def setup_and_modulation(nc, K, d):
    with Phase(nc, "mod") as ph:
        small = ph.sb("small", [P, 5, 16])
        M = Modulation(nc, K, ph, d, 0, 16, 8, [(0, 0), (1, MOD_TILES)])
        (vec_in, x_in, v, lb_in, lb_exp, g_step) = ph.sems(
            "vec_in", "x_in", "v", "lb_max", "lb_exp", "g_step")
        block = ph.block()

        @block.sync
        def _(sp):
            M.load(sp)

        @block.scalar
        def _(act):
            act.dma_start(K.vec[:], d["vec"]).then_inc(vec_in, 16)
            act.dma_start(K.x[:], d["xT"].rearrange("(k p) t -> p k t", p=P)).then_inc(x_in, 16)
            act.dma_start(K.hc[:], d["ctxT"].rearrange("(k p) t -> p k t", p=P)).then_inc(x_in, 16)
            M.start_act(act)
            act.wait_ge(lb_in, 1)
            nc.scalar.activation(small[:, 1:3, :], small[:, 1:3, :], ACT.Exp).then_inc(lb_exp, 1)
            for n in range(16):
                M.sum(act, n)
            act.wait_ge(x_in, 32)

        @block.gpsimd
        def _(g):
            st = Steps(g, g_step)
            st.do(nc.gpsimd.memset(K.ones[:], 1.0))
            st.do(nc.gpsimd.memset(K.ident[:], 0.0))
            st.do(nc.gpsimd.memset(K.segf[:], 1.0))
            st.do(nc.gpsimd.memset(K.segb[:], 1.0))
            st.do(nc.gpsimd.memset(K.tri[:], 1.0))
            st.sync()
            st.do(nc.gpsimd.affine_select(out=K.ident[:], in_=K.ident[:], compare_op=ALU.not_equal, fill=1.0,
                                          base=0, pattern=[[-1, P]], channel_multiplier=1))
            st.do(nc.gpsimd.memset(K.segf[:, 0:T:CH], 0.0))
            st.do(nc.gpsimd.memset(K.segf[:, T:T + 1], 0.0))
            st.do(nc.gpsimd.memset(K.segb[:, CH - 1:T:CH], 0.0))
            st.do(nc.gpsimd.memset(K.segb[:, T + TC - 1:T + TC], 0.0))
            st.do(nc.gpsimd.affine_select(out=K.tri[:, 0, :], in_=K.tri[:, 0, :], compare_op=ALU.is_ge, fill=0.0,
                                          base=0, pattern=[[1, CH]], channel_multiplier=-1))
            st.do(nc.gpsimd.affine_select(out=K.tri[:, 1, :], in_=K.tri[:, 1, :], compare_op=ALU.is_ge, fill=0.0,
                                          base=0, pattern=[[-1, CH]], channel_multiplier=1))
            st.sync()
            for c in range(NCH):
                last = nc.gpsimd.tensor_copy(K.triu[:, :, c, :], K.tri[:])
            st.then(last)

        @block.vector
        def _(dve):
            st = Steps(dve, v)
            dve.wait_ge(vec_in, 16)
            a = VEC["lb_logits"][0]
            l0, l1 = K.vec[:, a:a + 16], K.vec[:, a + 16:a + 32]
            st.then(nc.vector.tensor_tensor(small[:, 0, :], l0, l1, ALU.max))
            st.do(nc.vector.tensor_tensor(small[:, 1, :], l0, small[:, 0, :], ALU.subtract))
            nc.vector.tensor_tensor(small[:, 2, :], l1, small[:, 0, :], ALU.subtract).then_inc(lb_in, 1)
            dve.wait_ge(lb_exp, 1)
            st.then(nc.vector.tensor_tensor(small[:, 3, :], small[:, 1, :], small[:, 2, :], ALU.add))
            st.then(nc.vector.reciprocal(small[:, 4, :], small[:, 3, :]))
            st.then(nc.vector.tensor_tensor(K.lb[:], small[:, 1, :], small[:, 4, :], ALU.mult))
            st.then(nc.vector.tensor_scalar(K.oml[:], K.lb[:], -1.0, 1.0, ALU.mult, ALU.add))

            M.start_mul(dve, nc.vector)
            for n in range(16):
                M.multiply(dve, nc.vector, n, n % 8, n // 8 * 16)
            st = M.finish(dve, nc.vector)
            g0 = VEC["norm_mix_g"][0]
            for dst, at in ((K.gs_mix, 8), (K.gs_ctx, MOD_TILES + 8)):
                st.then(nc.vector.tensor_scalar(dst[:], K.mod[:, at:at + 8], 1.0, None, ALU.add))
                st.then(nc.vector.tensor_tensor(dst[:], dst[:], K.vec[:, g0:g0 + KT], ALU.mult))


def norm_phase(nc, K, name, jobs, center=False):
    with Phase(nc, name) as ph:
        sq = ph.sb("sq", [P, 2, T])
        rstd = ph.sb("rstd", [P, T])
        tmp = ph.sb("tmp", [P, 2, T])
        sums = ph.banks("sums", 2)[:].rearrange("p (s t) -> p s t", s=2)
        sq_ready, sums_done, rstd_ready, v, a, cent, mean_done = ph.sems(
            "sq_ready", "sums_done", "rstd_ready", "v", "a", "centered", "mean_done")
        block = ph.block()
        J = len(jobs)

        @block.tensor
        def _(pe):
            for j, (src, dst, n, mul, add) in enumerate(jobs):
                if center:
                    for k in range(KT):
                        last = nc.tensor.matmul(sums[:, 1, 0:n], K.ones[:], src[:, k, 0:n], start=k == 0, stop=k == KT - 1)
                    last.then_inc(mean_done, 1)
                if j:
                    pe.wait_ge(rstd_ready, j)
                for k in range(KT):
                    pe.wait_ge(sq_ready, j * KT + k + 1)
                    nc.tensor.matmul(sums[:, 0, 0:n], K.ones[:], sq[:, k % 2, 0:n], start=k == 0,
                                     stop=k == KT - 1).then_inc(sums_done, 1)

        @block.scalar
        def _(act):
            st = Steps(act, a)
            for j, (src, dst, n, mul, add) in enumerate(jobs):
                for k in range(KT):
                    if j * KT + k >= 2:
                        act.wait_ge(sums_done, j * KT + k - 1)
                    if center:
                        act.wait_ge(cent, j * KT + k + 1)
                    nc.scalar.activation(sq[:, k % 2, 0:n], (dst if center else src)[:, k, 0:n],
                                         ACT.Square).then_inc(sq_ready, 1)
                act.wait_ge(sums_done, (j + 1) * KT)
                if j:
                    act.wait_ge(cent, 100 * j)
                st.then(nc.scalar.activation(rstd[:, 0:n], sums[:, 0, 0:n], ACT.Ln, scale=1.0 / D,
                                             bias=LN_EPS if center else EPS))
                nc.scalar.activation(rstd[:, 0:n], rstd[:, 0:n], ACT.Exp, scale=-0.5).then_inc(rstd_ready, 1)

        @block.vector
        def _(dve):
            st = Steps(dve, v)
            for j, (src, dst, n, mul, add) in enumerate(jobs):
                if center:
                    dve.wait_ge(mean_done, 1)
                    for k in range(KT):
                        nc.vector.scalar_tensor_tensor(out=dst[:, k, 0:n], in0=sums[:, 1, 0:n], scalar=-1.0 / D,
                                                       in1=src[:, k, 0:n], op0=ALU.mult, op1=ALU.add).then_inc(cent, 1)
                base = dst if center else src
                dve.wait_ge(rstd_ready, j + 1)
                for k in range(KT):
                    if add is None:
                        st.do(nc.vector.scalar_tensor_tensor(out=dst[:, k, 0:n], in0=base[:, k, 0:n], scalar=mul[:, k:k + 1],
                                                             in1=rstd[:, 0:n], op0=ALU.mult, op1=ALU.mult))
                    else:
                        st.then(nc.vector.scalar_tensor_tensor(out=tmp[:, k % 2, 0:n], in0=base[:, k, 0:n], scalar=mul[:, k:k + 1],
                                                               in1=rstd[:, 0:n], op0=ALU.mult, op1=ALU.mult))
                        st.do(nc.vector.tensor_scalar(dst[:, k, 0:n], tmp[:, k % 2, 0:n], add[:, k:k + 1], None, ALU.add))
                st.sync()
                if j < J - 1:
                    dve.sem_inc(cent, 100)


def heads_phase(nc, K, d, name, w_dram, heads, vt, gate_norm, y, scan_scale, log_gates=None):
    hg = log_gates is None
    NT = 5 if hg else 6
    with_ctx = 3
    QI = 3
    VI = 2 if hg else 1
    GI = 4
    N = T + TC
    with Phase(nc, name) as ph:
        R = 5 if hg else 3
        ring = ph.sb("ring", [P, R, KT * P])
        proj_sb = ph.sb("proj", [P, 2, with_ctx * N + (NT - with_ctx) * T])
        sgate = ph.sb("sgate", [P, 2, vt, T])
        if hg:
            forget = ph.sb("forget", [P, 2, N])
            key2 = ph.sb("key2", [P, 2, N])
            lg2 = ph.sb("lg2", [P, 2, N])
        cum = ph.sb("cum", [P, N])
        dif = ph.sb("dif", [P, T])
        dif2 = ph.sb("dif2", [P, N])
        e_q = ph.sb("e_q", [P, T])
        e_k = ph.sb("e_k", [P, T])
        e_kd = ph.sb("e_kd", [P, N])
        q_dec = ph.sb("q_dec", [P, 2, T])
        e_last = ph.sb("e_last", [P, 2, NCH])
        vtok = ph.sb("vtok", [CH, NCH, vt, P])
        vtok_c = ph.sb("vtok_c", [P, 2, vt, P])
        ktok = ph.sb("ktok", [CH, NCH, P])
        ktok_c = ph.sb("ktok_c", [P, 2, P])
        score = ph.sb("score", [CH, 2, T])
        state = ph.sb("state", [P, 2, NCH, vt, P])
        osq = ph.sb("osq", [P, T])
        rstd = ph.sb("rstd", [P, T])
        pg = ph.banks("proj_ps", 3)
        ptr = ph.banks("trans_ps", 2)
        psc = ph.banks("score_ps")
        pkv = ph.banks("kv_ps", 2)
        kv = pkv[:].rearrange("p (n v) -> p n v", n=NCH)
        o_ps = [psc, ptr[:, 0:T]]
        ready = ph.sems(*[f"w_ready{i}" for i in range(R)])
        (proj_done, proj_stored, sig_done, f_done, ln_done, dif_done, exp_done, prep_done, vtr_done,
         vtok_done, b_done, ktok_done, mask_done, kv_done, state_done, o_done, osq_done, sum_done,
         rstd_done, y_done, v, a, passed) = ph.sems(
            "proj_done", "proj_stored", "sig_done", "forget_done", "log_done", "dif_done", "exp_done",
            "prep_done", "vtrans_done", "vtok_done", "scores_done", "ktok_done", "mask_done", "kv_done",
            "state_done", "o_done", "osq_done", "sum_done", "rstd_done", "y_done", "v", "a", "passed")
        block = ph.block()

        def proj(par, j):
            at = j * N if j < with_ctx else with_ctx * N + (j - with_ctx) * T
            return proj_sb[:, par, at:at + (N if j < with_ctx else T)]

        def pgl(t):
            return pg[:, (t % 2) * T:(t % 2) * T + T]

        def pgc(t):
            return pg[:, 2 * T:2 * T + TC]

        @block.sync
        def _(sp):
            stream(sp, [ring[:, s, :] for s in range(R)], lambda t: w_dram[t], heads * NT, ready, proj_done)

        @block.tensor
        def _(pe):
            def project(h, par, j):
                t = par * NT + j
                s = t % R
                pe.wait_ge(ready[s], h // 2 * (16 * (2 * NT // R)) + 16 * (t // R + 1) if isinstance(h, int)
                           else (h - par) * (8 * (2 * NT // R)) + 16 * (t // R + 1))
                pe.wait_ge(proj_stored, h * NT + (j + 1))
                for k in range(KT):
                    last = nc.tensor.matmul(pgl(t), ring[:, s, k * P:(k + 1) * P], K.h[:, k, :], start=k == 0, stop=k == KT - 1)
                if j < with_ctx:
                    pe.wait_ge(proj_stored, h * NT + (j + 2))
                    for k in range(KT):
                        last = nc.tensor.matmul(pgc(t), ring[:, s, k * P:(k + 1) * P], K.hc[:, k, :], start=k == 0, stop=k == KT - 1)
                last.then_inc(proj_done, 1)

            def transposes(src, out, ctx_out):
                for n in range(NCH):
                    nc.tensor.transpose(out[0:CH, n * P:(n + 1) * P], src[:, n * CH:(n + 1) * CH], K.ident[:])
                for n in range(2):
                    last = nc.tensor.transpose(ctx_out[:, n * P:(n + 1) * P], src[:, T + n * P:T + (n + 1) * P], K.ident[:])
                return last

            def attend(h, par, nxt):
                def between(*js):
                    if nxt is not None:
                        for j in js:
                            project(nxt[0], nxt[1], j)

                between(0)
                for u in range(vt):
                    pe.wait_ge(proj_stored, h * NT + NT + 2)
                    pe.wait_ge(y_done, h * vt + 1)
                    if u:
                        pe.wait_ge(vtok_done, h * vt + u)
                    pe.sem_inc(passed, 1)
                    transposes(proj(par, VI + u), ptr, pkv).then_inc(vtr_done, 1)
                for dr in range(2):
                    pe.wait_ge(vtok_done, h * vt + vt)
                    pe.wait_ge(prep_done, h * 2 + dr + 1)
                    if dr:
                        pe.wait_ge(ktok_done, h * 2 + 1)
                        pe.wait_ge(mask_done, h * 2 + 1)
                        pe.wait_ge(state_done, h * (2 * vt) + vt)
                    for n in range(NCH):
                        c = slice(n * CH, (n + 1) * CH)
                        nc.tensor.matmul(psc[0:CH, c], e_k[:, c], e_q[:, c], start=True, stop=True)
                    transposes(e_kd, ptr, pkv).then_inc(b_done, 1)
                    between(1 + 2 * dr)
                    pe.wait_ge(ktok_done, h * 2 + dr + 1)
                    for u in range(vt):
                        if u:
                            pe.wait_ge(state_done, h * (2 * vt) + dr * vt + u)
                        for n in range(NCH):
                            if n != (NCH - 1 if dr == 0 else 0):
                                nc.tensor.matmul(kv[:, n, :], ktok[:, n, :], vtok[:, n, u, :], start=True, stop=True)
                        s0 = NCH - 1 if dr == 0 else 0
                        for n in range(2):
                            last = nc.tensor.matmul(kv[:, s0, :], ktok_c[:, n, :], vtok_c[:, n, u, :], start=n == 0, stop=n == 1)
                        last.then_inc(kv_done, 1)
                    between(2 + 2 * dr)
                between(*range(5, NT))
                pe.wait_ge(mask_done, h * 2 + 2)
                pe.wait_ge(state_done, h * (2 * vt) + 2 * vt)
                for u in range(vt):
                    for n in range(NCH):
                        c = slice(n * CH, (n + 1) * CH)
                        for dr in range(2):
                            nc.tensor.matmul(o_ps[u][:, c], vtok[:, n, u, :], score[:, dr, c], start=dr == 0, stop=False)
                            last = nc.tensor.matmul(o_ps[u][:, c], state[:, dr, n, u, :], q_dec[:, dr, c], start=False, stop=dr == 1)
                    last.then_inc(o_done, 1)
                for u in range(vt):
                    pe.wait_ge(osq_done, h * vt + u + 1)
                    last = nc.tensor.matmul(ptr[:, T:2 * T], K.ones[:], osq[:], start=u == 0, stop=u == vt - 1)
                    last.then_inc(sum_done, 1)

            for j in range(NT):
                project(0, 0, j)
            with pe.Fori(0, heads // 2 - 1) as i:
                attend(i * 2, 0, (i * 2 + 1, 1))
                attend(i * 2 + 1, 1, (i * 2 + 2, 0))
            attend(heads - 2, 0, (heads - 1, 1))
            attend(heads - 1, 1, None)

        @block.scalar
        def _(act):
            st = Steps(act, a)

            def store(h, par, j):
                t = par * NT + j
                act.wait_ge(proj_done, h * NT + j + 1)
                scale = P ** -0.5 if j == QI else 1.0
                if j < with_ctx:
                    nc.scalar.activation(proj(par, j)[:, T:N], pgc(t), ACT.Copy)
                nc.scalar.activation(proj(par, j)[:, 0:T], pgl(t), ACT.Copy, scale=scale).then_inc(proj_stored, 1)

            def exps(h, dr):
                act.wait_ge(dif_done, h * 6 + dr * 3 + 1)
                if dr:
                    act.wait_ge(b_done, h * 2 + 1)
                nc.scalar.activation(e_q[:], dif[:], ACT.Exp, scale=scan_scale)
                nc.scalar.activation(e_k[:], dif[:], ACT.Exp, scale=-scan_scale)
                nc.scalar.activation(q_dec[:, dr, :], cum[:, 0:T], ACT.Exp, scale=scan_scale)
                last = (slice(CH - 1, T, CH), slice(0, T, CH))[dr]
                nc.scalar.activation(e_last[:, dr, :], cum[:, last], ACT.Exp, scale=scan_scale)
                act.wait_ge(dif_done, h * 6 + dr * 3 + 3)
                nc.scalar.activation(e_kd[:], dif2[:], ACT.Exp, scale=scan_scale).then_inc(exp_done, 1)

            def attend(h, par, nxt):
                def between(*js):
                    if nxt is not None:
                        for j in js:
                            store(nxt[0], nxt[1], j)

                act.wait_ge(proj_stored, h * NT + NT + 2)
                for u in range(vt):
                    nc.scalar.activation(sgate[:, par, u, :], proj(par, GI + u), ACT.Sigmoid).then_inc(sig_done, 1)
                if hg:
                    for dr in range(2):
                        nc.scalar.activation(forget[:, dr, :], proj(par, dr), ACT.Sigmoid).then_inc(sig_done, 1)
                    for dr in range(2):
                        act.wait_ge(f_done, h * 2 + dr + 1)
                        nc.scalar.activation(lg2[:, dr, :], forget[:, dr, :], ACT.Ln).then_inc(ln_done, 1)
                exps(h, 0)
                between(0)
                for u in range(vt):
                    act.wait_ge(vtr_done, h * vt + u + 1)
                    nc.scalar.activation(vtok_c[:, :, u, :], pkv[:, 0:2 * P].rearrange("p (n v) -> p n v", n=2), ACT.Copy)
                    nc.scalar.activation(vtok[:, :, u, :], ptr[0:CH, :].rearrange("p (n v) -> p n v", n=NCH), ACT.Copy).then_inc(vtok_done, 1)
                for dr in range(2):
                    act.wait_ge(b_done, h * 2 + dr + 1)
                    nc.scalar.activation(ktok_c[:], pkv[:, 0:2 * P].rearrange("p (n v) -> p n v", n=2), ACT.Copy)
                    nc.scalar.activation(ktok[:], ptr[0:CH, :].rearrange("p (n v) -> p n v", n=NCH), ACT.Copy).then_inc(ktok_done, 1)
                    if dr == 0:
                        exps(h, 1)
                    between(1 + 2 * dr)
                    between(2 + 2 * dr)
                between(*range(5, NT))
                for u in range(vt):
                    act.wait_ge(o_done, h * vt + u + 1)
                    if u:
                        act.wait_ge(sum_done, h * vt + u)
                    nc.scalar.activation(osq[:], o_ps[u][:, 0:T], ACT.Square).then_inc(osq_done, 1)
                act.wait_ge(sum_done, h * vt + vt)
                st.then(nc.scalar.activation(rstd[:], ptr[:, T:2 * T], ACT.Ln, scale=1.0 / (P * vt), bias=EPS))
                nc.scalar.activation(rstd[:], rstd[:], ACT.Exp, scale=-0.5).then_inc(rstd_done, 1)

            act.sem_inc(proj_stored, 2)
            for j in range(NT):
                store(0, 0, j)
            n0 = st.n
            with act.Fori(0, heads // 2 - 1) as i:
                st.turn = i * 2
                attend(i * 2, 0, (i * 2 + 1, 1))
                attend(i * 2 + 1, 1, (i * 2 + 2, 0))
            st.n, st.turn = n0 + 2 * (heads // 2 - 1), 0
            attend(heads - 2, 0, (heads - 1, 1))
            attend(heads - 1, 1, None)

        @block.vector
        def _(dve):
            st = Steps(dve, v)

            def differences(h, par, dr):
                seg = (K.segf, K.segb)[dr]
                lg = lg2[:, dr, :] if hg else log_gates[:, bass.ds(h * 2 + dr, 1), :].squeeze(1)
                if hg:
                    dve.wait_ge(ln_done, h * 2 + dr + 1)
                if dr:
                    dve.wait_ge(exp_done, h * 2 + 1)
                if dr == 0:
                    st.then(nc.vector.tensor_tensor_scan(cum[:], seg[:], lg, 0.0, ALU.mult, ALU.add))
                else:
                    st.then(nc.vector.tensor_tensor_scan(cum[:, ::-1], seg[:, ::-1], lg[:, ::-1], 0.0, ALU.mult, ALU.add))
                ref = (CH // 2, CH // 2 - 1)[dr]
                end = (CH - 1, 0)[dr]
                cend = (N - 1, T)[dr]
                c3 = cum[:, 0:T].rearrange("p (n c) -> p n c", c=CH)
                nc.vector.tensor_tensor(dif[:].rearrange("p (n c) -> p n c", c=CH), c3,
                                        c3[:, :, ref:ref + 1].to_broadcast([P, NCH, CH]), ALU.subtract).then_inc(dif_done, 1)
                nc.vector.tensor_tensor(dif2[:, 0:T].rearrange("p (n c) -> p n c", c=CH),
                                        c3[:, :, end:end + 1].to_broadcast([P, NCH, CH]), c3, ALU.subtract).then_inc(dif_done, 1)
                nc.vector.tensor_scalar(dif2[:, T:N], cum[:, T:N], -1.0, cum[:, cend:cend + 1], ALU.mult, ALU.add).then_inc(dif_done, 1)

            def products(h, par, dr):
                dve.wait_ge(exp_done, h * 2 + dr + 1)
                key = key2[:, dr, :] if hg else proj(par, 0)
                q = proj(par, QI)
                nc.vector.tensor_tensor(e_q[:], e_q[:], q, ALU.mult)
                nc.vector.tensor_tensor(e_k[:], e_k[:], key[:, 0:T], ALU.mult)
                nc.vector.tensor_tensor(q_dec[:, dr, :], q_dec[:, dr, :], q, ALU.mult)
                nc.vector.tensor_tensor(e_kd[:], e_kd[:], key, ALU.mult).then_inc(prep_done, 1)

            def mask(h, dr):
                dve.wait_ge(b_done, h * 2 + dr + 1)
                dve.sem_inc(passed, 1)
                nc.vector.copy_predicated(score[:, dr, :], K.triu[:, dr, :, :].rearrange("p n c -> p (n c)"), psc[0:CH, :]).then_inc(mask_done, 1)

            def states(h, dr):
                order = list(range(NCH)) if dr == 0 else list(range(NCH))[::-1]
                for u in range(vt):
                    dve.wait_ge(kv_done, h * (2 * vt) + dr * vt + u + 1)
                    st.then(nc.vector.tensor_copy(state[:, dr, order[0], u, :], kv[:, order[-1], :]))
                    for a_, b_ in zip(order[:-1], order[1:]):
                        ins = nc.vector.scalar_tensor_tensor(
                            out=state[:, dr, b_, u, :], in0=state[:, dr, a_, u, :], scalar=e_last[:, dr, a_:a_ + 1],
                            in1=kv[:, a_, :], op0=ALU.mult, op1=ALU.add)
                        if b_ == order[-1]:
                            ins.then_inc(state_done, 1)
                        else:
                            st.then(ins)

            def attend(h, par):
                ns = vt + (2 if hg else 0)
                dve.wait_ge(proj_stored, h * NT + NT + 2)
                dve.wait_ge(sig_done, h * ns + vt)
                st.do(nc.vector.tensor_tensor(sgate[:, par], sgate[:, par], proj_sb[:, par, with_ctx * N + (GI - with_ctx) * T:with_ctx * N + (GI - with_ctx + vt) * T].rearrange("p (u t) -> p u t", u=vt), ALU.mult))
                if hg:
                    for dr in range(2):
                        dve.wait_ge(sig_done, h * ns + vt + dr + 1)
                        col = bass.ds(h + dr * HG_H, 1)
                        nc.vector.tensor_scalar(forget[:, dr, :], forget[:, dr, :], K.oml[:, col], K.lb[:, col],
                                                ALU.mult, ALU.add).then_inc(f_done, 1)
                        dve.wait_ge(f_done, h * 2 + dr + 1)
                        st.do(nc.vector.tensor_scalar(key2[:, dr, :], forget[:, dr, :], -1.0, 1.0, ALU.mult, ALU.add))
                differences(h, par, 0)
                products(h, par, 0)
                differences(h, par, 1)
                mask(h, 0)
                products(h, par, 1)
                states(h, 0)
                mask(h, 1)
                states(h, 1)
                dve.wait_ge(rstd_done, h + 1)
                for u in range(vt):
                    yo = y[:, bass.ds(h * vt + u, 1), :].squeeze(1)
                    st.then(nc.vector.scalar_tensor_tensor(out=osq[:] if u == 0 else dif[:], in0=o_ps[u][:, 0:T], scalar=gate_norm[:, u:u + 1],
                                                           in1=rstd[:], op0=ALU.mult, op1=ALU.mult))
                    nc.vector.tensor_tensor(yo, osq[:] if u == 0 else dif[:], sgate[:, par, u, :], ALU.mult).then_inc(y_done, 1)

            dve.sem_inc(y_done, 1)
            st.then(nc.vector.memset(score[:], 0.0))
            per = 1 + (2 if hg else 0) + 2 + 2 * vt * (NCH - 1) + vt
            n0 = st.n
            with dve.Fori(0, heads // 2 - 1) as i:
                st.turn = i * (2 * per)
                attend(i * 2, 0)
                attend(i * 2 + 1, 1)
            assert st.n - n0 == 2 * per, (st.n - n0, per)
            st.n, st.turn = n0 + 2 * per * (heads // 2 - 1), 0
            attend(heads - 2, 0)
            attend(heads - 1, 1)


def lora_gates(nc, K, d, log_gates):
    N = T + TC
    with Phase(nc, "lora") as ph:
        w = ph.sb("w", [P, KT, 32])
        gw = ph.sb("gw", [16, 2, T])
        gr = ph.sb("gr", [16, 2, N])
        az = ph.sb("az", [P, N])
        mz = ph.sb("mz", [P, N])
        g_ps = ph.banks("g", 2)
        z_ps = ph.banks("z", 4)
        w_in, gr_done, gr_stored, z_done, abs_done, m_done, l_done, out_done, a = ph.sems(
            "w_in", "gr_done", "gr_stored", "z_done", "abs_done", "min_done", "log_done", "out_done", "a")
        block = ph.block()
        pairs = [(h, dr) for h in range(GLA_H) for dr in range(2)]
        gb = VEC["gk_b"][0]

        @block.sync
        def _(sp):
            sp.dma_start(w[:], d["w_gr"].rearrange("(k p) m -> p k m", p=P)).then_inc(w_in, 16)
            sp.dma_start(gw[:], d["gk_w"].rearrange("d r m -> r d m")).then_inc(w_in, 16)

        @block.tensor
        def _(pe):
            pe.wait_ge(w_in, 32)
            for dr in range(2):
                if dr:
                    pe.wait_ge(gr_stored, 1)
                for j, (src, n) in enumerate(((K.h, T), (K.hc, TC))):
                    for k in range(KT):
                        last = nc.tensor.matmul(g_ps[0:16, j * T:j * T + n], w[:, k, 16 * dr:16 * dr + 16], src[:, k, :],
                                                start=k == 0, stop=k == KT - 1)
                last.then_inc(gr_done, 1)
            pe.wait_ge(gr_stored, 2)
            for i, (h, dr) in enumerate(pairs):
                b = 2 * (i % 2) * T
                if i >= 2:
                    pe.wait_ge(m_done, i - 1)
                nc.tensor.matmul(z_ps[:, b:b + T], gw[:, dr, h * P:(h + 1) * P], gr[:, dr, 0:T], start=True, stop=True)
                nc.tensor.matmul(z_ps[:, b + T:b + N], gw[:, dr, h * P:(h + 1) * P], gr[:, dr, T:N], start=True,
                                 stop=True).then_inc(z_done, 1)

        @block.scalar
        def _(act):
            st = Steps(act, a)
            for i, (h, dr) in enumerate(pairs):
                b = 2 * (i % 2) * T
                act.wait_ge(z_done, i + 1)
                bias = K.vec[:, gb + dr * GLA_H + h:gb + dr * GLA_H + h + 1]
                if i:
                    act.wait_ge(out_done, i)
                nc.scalar.activation(az[:], z_ps[:, b:b + N], ACT.Abs, bias=bias).then_inc(abs_done, 1)
                act.wait_ge(abs_done, i + 1)
                st.then(nc.scalar.activation(az[:], az[:], ACT.Exp, scale=-1.0))
                nc.scalar.activation(az[:], az[:], ACT.Ln, bias=1.0).then_inc(l_done, 1)

        @block.vector
        def _(dve):
            for dr in range(2):
                dve.wait_ge(gr_done, dr + 1)
                nc.vector.tensor_copy(gr[:, dr, :], g_ps[0:16, 0:N]).then_inc(gr_stored, 1)
            for i, (h, dr) in enumerate(pairs):
                b = 2 * (i % 2) * T
                dve.wait_ge(abs_done, i + 1)
                bias = K.vec[:, gb + dr * GLA_H + h:gb + dr * GLA_H + h + 1]
                nc.vector.tensor_scalar(mz[:], z_ps[:, b:b + N], bias, 0.0, ALU.add, ALU.min).then_inc(m_done, 1)
                dve.wait_ge(m_done, i + 1)
                dve.wait_ge(l_done, i + 1)
                nc.vector.tensor_tensor(log_gates[:, h * 2 + dr, :], mz[:], az[:], ALU.subtract).then_inc(out_done, 1)


def merge_phase(nc, K, d, y_hg, y_gla, merged):
    with Phase(nc, "merge") as ph:
        ring = ph.sb("ring", [P, 4, KT * P])
        sg = ph.sb("sg", [P, 2, T])
        part = ph.sb("part", [P, T])
        ps = ph.banks("ps", 4)
        M = Modulation(nc, K, ph, d, 16, 32, 4, [(0, 16)])
        ready = ph.sems(*[f"w_ready{i}" for i in range(4)])
        done, sig, out, v = ph.sems("tile_done", "sig_done", "out_done", "v")
        block = ph.block()
        src = [K.h, y_hg, K.h, y_gla]

        @block.sync
        def _(sp):
            stream(sp, [ring[:, s, :] for s in range(4)], lambda t: d["w_merge"][t], 4 * KT, ready, done)

        @block.gpsimd
        def _(g):
            for n, (row, _) in enumerate(M.vecs):
                g.dma_start(M.rows[:, n, :], d["c_rows"][row].partition_broadcast(P)).then_inc(M.rows_in, 16)
            for s in range(4):
                g.dma_start(M.ring[:, s, :], d["w_mod"][16 + s]).then_inc(M.ready[s], 16)
            M.start_mul(g, nc.gpsimd)

            def turn(i, last):
                for s in range(4):
                    M.multiply(g, nc.gpsimd, i * 4 + s, s, i * 16)
                    if not last:
                        g.wait_ge(M.multiplied, i * 4 + (s + 1))
                        g.dma_start(M.ring[:, s, :], d["w_mod"][i * 4 + (s + 20)]).then_inc(M.ready[s], 16)

            with g.Fori(0, KT - 1) as i:
                turn(i, False)
            turn(KT - 1, True)
            st = M.finish(g, nc.gpsimd)
            g1 = VEC["norm_ffn_g"][0]
            st.then(nc.gpsimd.tensor_tensor(K.gs_ffn[:], K.mod[:, 32:40], K.vec[:, g1:g1 + KT], ALU.mult))
            st.then(nc.gpsimd.tensor_tensor(K.gs_ffn[:], K.gs_ffn[:], K.vec[:, g1:g1 + KT], ALU.add))

        @block.tensor
        def _(pe):
            with pe.Fori(0, KT) as i:
                for s in range(4):
                    pe.wait_ge(ready[s], i * 16 + 16)
                    if s in (0, 1):
                        pe.wait_ge(out, i * 2 + 1)
                    for k in range(KT):
                        last = nc.tensor.matmul(ps[:, s * T:(s + 1) * T], ring[:, s, k * P:(k + 1) * P], src[s][:, k, :],
                                                start=k == 0, stop=k == KT - 1)
                    last.then_inc(done, 1)

        @block.scalar
        def _(act):
            M.start_act(act)
            with act.Fori(0, KT) as i:
                for b in range(2):
                    act.wait_ge(done, i * 4 + 2 * b + 1)
                    act.wait_ge(out, i * 2 + 1)
                    nc.scalar.activation(sg[:, b, :], ps[:, 2 * b * T:(2 * b + 1) * T], ACT.Sigmoid).then_inc(sig, 1)
                    M.sum(act, i * 4 + 2 * b)
                    M.sum(act, i * 4 + 2 * b + 1)

        @block.vector
        def _(dve):
            dve.sem_inc(out, 1)
            with dve.Fori(0, KT) as i:
                m = merged[:, bass.ds(i, 1), :].squeeze(1)
                dve.wait_ge(sig, i * 2 + 1)
                dve.wait_ge(done, i * 4 + 2)
                nc.vector.tensor_tensor(part[:], sg[:, 0, :], ps[:, T:2 * T], ALU.mult).then_inc(out, 1)
                dve.wait_ge(sig, i * 2 + 2)
                dve.wait_ge(done, i * 4 + 4)
                nc.vector.tensor_tensor(sg[:, 1, :], sg[:, 1, :], ps[:, 3 * T:4 * T], ALU.mult).then_inc(v, 1)
                dve.wait_ge(v, i + 1)
                dve.wait_ge(out, i * 2 + 2)
                nc.vector.tensor_tensor(m, part[:], sg[:, 1, :], ALU.add).then_inc(out, 1)


def parts_product(nc, out, w, x, ks, start, stop, wait=None):
    for k in ks:
        if wait is not None:
            wait(k)
        for n, (a, b) in enumerate(((0, 0), (0, 1), (1, 0))):
            last = nc.tensor.matmul(out, w(a, k), x(b, k), start=start and k == ks[0] and n == 0,
                                    stop=stop and k == ks[-1] and n == 2)
    return last


def linear_phase(nc, K, name, w, src, tiles, finish, chunks=1, parts=None):
    with Phase(nc, name) as ph:
        B, R = 4, 4
        S = B * chunks
        turns = tiles // B
        raw = ph.sb("raw", [P, R, KT * P])
        wp = ph.sb("w_parts", [P, 2, 2, KT * P], F32R)
        ps = ph.banks("ps", B)
        bufs = ph.sb("buf", [P, B, T])
        if parts is None:
            parts = ph.sb("src_parts", [P, 2, KT, T], F32R)
        ready = ph.sems(*[f"w_ready{i}" for i in range(R)])
        w_hi, w_lo, used, src_hi, src_lo, mid, out, v = ph.sems(
            "w_hi", "w_lo", "chunk_used", "src_hi", "src_lo", "act_done", "out_done", "v")
        block = ph.block()
        act_step, dve_step, per = finish

        @block.sync
        def _(sp):
            stream(sp, [raw[:, s, :] for s in range(R)], w, tiles * chunks, ready, w_lo)

        @block.tensor
        def _(pe):
            pe.sem_inc(used, 2)

            def src_wait(k):
                pe.wait_ge(src_lo, k + 1)

            with pe.Fori(0, turns) as i:
                for s in range(S):
                    b, c = s // chunks, s % chunks
                    pe.wait_ge(w_lo, i * S + (s + 1))
                    if c == 0:
                        pe.wait_ge(out, i * B + (b + 1))
                    parts_product(nc, ps[:, b * T:(b + 1) * T], lambda a, k: wp[:, s % 2, a, k * P:(k + 1) * P],
                                  lambda a, k: parts[:, a, c * KT + k, :], range(KT), c == 0, c == chunks - 1,
                                  src_wait if src is not None and s == 0 else None).then_inc(used, 1)

        def turns_of(st, per, body):
            if turns > 1:
                st.loop(turns - 1, per, lambda i: body(i, False))
            body(turns - 1, True)

        @block.scalar
        def _(act):
            if src is not None:
                for k in range(KT):
                    nc.scalar.activation(parts[:, 0, k, :], src[:, k, :], ACT.Copy).then_inc(src_hi, 1)
            if dve_step is None:
                act.sem_inc(out, B)

            def high(i, s):
                act.wait_ge(ready[s % R], i * (16 * S // R) + 16 * (s // R + 1))
                act.wait_ge(used, i * S + (s + 1))
                nc.scalar.activation(wp[:, s % 2, 0, :], raw[:, s % R, :], ACT.Copy).then_inc(w_hi, 1)

            def turn(i, last):
                for s in range(S):
                    if not (last and s == S - 1):
                        high(i, s + 1)
                    if act_step is not None and s % chunks == chunks - 1:
                        b = s // chunks
                        act.wait_ge(used, i * S + (s + 3))
                        act.wait_ge(out, i * B + (b + 1))
                        act_step(i * B + b, ps[:, b * T:(b + 1) * T], bufs[:, b, :]).then_inc(mid if dve_step else out, 1)

            high(0, 0)
            turns_of(Steps(act, v), 0, turn)

        @block.vector
        def _(dve):
            if dve_step is not None:
                dve.sem_inc(out, B)
            st = Steps(dve, v)
            if src is not None:
                for k in range(KT):
                    dve.wait_ge(src_hi, k + 1)
                    nc.vector.tensor_tensor(parts[:, 1, k, :], src[:, k, :], parts[:, 0, k, :].bitcast(F32), ALU.subtract).then_inc(src_lo, 1)

            def low(i, s):
                dve.wait_ge(w_hi, i * S + (s + 1))
                nc.vector.tensor_tensor(wp[:, s % 2, 1, :], raw[:, s % R, :], wp[:, s % 2, 0, :].bitcast(F32), ALU.subtract).then_inc(w_lo, 1)

            def turn(i, last):
                for s in range(S):
                    if not (last and s == S - 1):
                        low(i, s + 1)
                    if dve_step is not None and s % chunks == chunks - 1:
                        b = s // chunks
                        if act_step is not None:
                            dve.wait_ge(mid, i * B + (b + 1))
                        else:
                            dve.wait_ge(used, i * S + (s + 3))
                        dve_step(st, i * B + b, ps[:, b * T:(b + 1) * T], bufs[:, b, :]).then_inc(out, 1)

            low(0, 0)
            turns_of(st, per * B, turn)
            if dve_step is not None:
                dve.wait_ge(out, tiles + B)


def peer_route(nc, K, d, sel):
    NK = TOPK
    with Phase(nc, "route") as ph:
        R = 4
        ring = ph.sb("ring", [P, R, KT * P])
        keys = ph.sb("keys", [P, 2, NKEY])
        q_sb = ph.sb("q", [P, 2, T])
        rest = ph.sb("rest", [P, TT, 2 * P])
        val = ph.sb("val", [P, 2, TT, NK])
        idx = ph.sb("idx", [P, 2, TT, NK], U32)
        idxf = ph.sb("idxf", [P, 2, TT, NK])
        cand = ph.sb("cand", [P, TT, NK, NK])
        top = ph.sb("top", [P, TT, NK])
        topi = ph.sb("topi", [P, TT, NK], U32)
        rc_u = ph.sb("rc_u", [P, 2, TT, NK], U32)
        rc = ph.sb("rc", [P, 2, TT, NK])
        pick = ph.sb("pick", [P, TT, NK, NK])
        iota16 = ph.sb("iota16", [P, NK])
        expd = ph.sb("expd", [P, TT, NK])
        total = ph.sb("total", [P, 2, TT])
        q_ps = ph.banks("q_ps", 2)
        s_ps = ph.banks("s_ps", 2)
        ready = ph.sems(*[f"w_ready{i}" for i in range(R)])
        keys_in, proj_done, q_stored, s_done, s_read, cst, logit_done, exp_done, v, passed = ph.sems(
            "keys_in", "proj_done", "q_stored", "scores_done", "scores_read", "consts", "logit_done", "exp_done", "v", "passed")
        block = ph.block()
        tiles = 2 * PEER_H

        @block.sync
        def _(sp):
            sp.dma_start(keys[:], d["peer_keys"]).then_inc(keys_in, 16)
            stream(sp, [ring[:, s, :] for s in range(R)], lambda t: d["peer_wq"][t], tiles, ready, proj_done)

        @block.gpsimd
        def _(g):
            nc.gpsimd.iota(iota16[:], [[1, NK]], base=0, channel_multiplier=0,
                           allow_small_or_imprecise_dtypes=True).then_inc(cst, 1)

        @block.tensor
        def _(pe):
            pe.wait_ge(keys_in, 16)
            pe.sem_inc(s_done, 1)

            def project(i, s):
                pe.wait_ge(ready[s], i * 16 + 16)
                pe.wait_ge(q_stored, i * R + s + 1)
                for k in range(KT):
                    last = nc.tensor.matmul(q_ps[:, (s % 2) * T:(s % 2) * T + T], ring[:, s, k * P:(k + 1) * P], K.h[:, k, :],
                                            start=k == 0, stop=k == KT - 1)
                last.then_inc(proj_done, 1)

            def scores(i, s):
                pe.wait_ge(q_stored, i * R + s + 3)
                pe.wait_ge(s_read, i * R + s + 1)
                for t in range(TT):
                    last = nc.tensor.matmul(s_ps[:, (s % 2) * T + t * P:(s % 2) * T + (t + 1) * P],
                                            q_sb[:, s % 2, t * P:(t + 1) * P], keys[:, s % 2, :], start=True, stop=True)
                last.then_inc(s_done, 1)

            with pe.Fori(0, tiles // R) as i:
                project(i, 0)
                for s in range(1, R):
                    project(i, s)
                    scores(i, s - 1)
                scores(i, R - 1)

        @block.scalar
        def _(act):
            act.sem_inc(q_stored, 2)
            with act.Fori(0, tiles // R) as i:
                for s in range(R):
                    act.wait_ge(proj_done, i * R + s + 1)
                    act.wait_ge(s_done, i * R + (s + 1))
                    nc.scalar.activation(q_sb[:, s % 2, :], q_ps[:, (s % 2) * T:(s % 2) * T + T], ACT.Copy).then_inc(q_stored, 1)
                    if s % 2 and s > 1:
                        act.wait_ge(logit_done, i * 2 + 1)
                        nc.scalar.activation(expd[:], expd[:], ACT.Exp).then_inc(exp_done, 1)
                act.wait_ge(logit_done, i * 2 + 2)
                nc.scalar.activation(expd[:], expd[:], ACT.Exp).then_inc(exp_done, 1)

        @block.vector
        def _(dve):
            V = nc.vector
            dve.sem_inc(s_read, 2)
            dve.wait_ge(cst, 1)
            st = Steps(dve, v)

            def top16(src, values, indices, n):
                for t in range(TT):
                    st.do(V.max(values[:, t, 0:8], src(t)))
                st.sync(passed)
                for t in range(TT):
                    st.do(V.max_index(indices[:, t, 0:8], values[:, t, 0:8], src(t)))
                    st.do(V.match_replace(rest[:, t, 0:n], values[:, t, 0:8], src(t), -3.0e38))
                st.sync(passed)
                for t in range(TT):
                    st.do(V.max(values[:, t, 8:16], rest[:, t, 0:n]))
                st.sync(passed)
                for t in range(TT):
                    st.do(V.max_index(indices[:, t, 8:16], values[:, t, 8:16], rest[:, t, 0:n]))
                st.sync()

            def head(i, par):
                for s in range(2):
                    dve.wait_ge(s_done, i * R + (par * 2 + s + 2))
                    dve.sem_inc(passed, 1)
                    top16(lambda t: s_ps[:, s * T + t * P:s * T + (t + 1) * P], val[:, s], idx[:, s], P)
                    V.tensor_copy(idxf[:, s], idx[:, s]).then_inc(s_read, 1)
                st.then(V.tensor_tensor(cand[:], val[:, 0].unsqueeze(3).to_broadcast([P, TT, NK, NK]),
                                        val[:, 1].unsqueeze(2).to_broadcast([P, TT, NK, NK]), ALU.add))
                dve.sem_inc(passed, 1)
                top16(lambda t: cand[:, t].rearrange("p a b -> p (a b)"), top, topi, NK * NK)
                V.tensor_tensor(expd[:], top[:], top[:, :, 0:1].to_broadcast([P, TT, NK]), ALU.subtract).then_inc(logit_done, 1)
                st.do(V.tensor_scalar(rc_u[:, 0], topi[:], 4, None, ALU.logical_shift_right))
                st.then(V.tensor_scalar(rc_u[:, 1], topi[:], 15, None, ALU.bitwise_and))
                st.then(V.tensor_copy(rc[:], rc_u[:]))
                cols = slice(None)
                for s in range(2):
                    st.then(V.tensor_tensor(pick[:], rc[:, s].unsqueeze(3).to_broadcast([P, TT, NK, NK]),
                                            iota16[:].unsqueeze(1).unsqueeze(1).to_broadcast([P, TT, NK, NK]), ALU.is_equal))
                    st.then(V.tensor_tensor(pick[:], pick[:], idxf[:, s].unsqueeze(2).to_broadcast([P, TT, NK, NK]), ALU.mult))
                    st.then(V.tensor_reduce(sel[:, s, :, bass.ds(i * (2 * NK) + par * NK, NK)], pick[:], AXX, ALU.add))
                dve.wait_ge(exp_done, i * 2 + par + 1)
                st.then(V.tensor_reduce(total[:, 0, :], expd[:], AXX, ALU.add))
                st.then(V.reciprocal(total[:, 1, :], total[:, 0, :]))
                st.then(V.tensor_tensor(sel[:, 2, :, bass.ds(i * (2 * NK) + par * NK, NK)], expd[:],
                                        total[:, 1, :].unsqueeze(2).to_broadcast([P, TT, NK]), ALU.mult))

            per = 2 * (3 * 5 * TT + 1 + 3 + 6 + 3)

            def pair(i):
                head(i, 0)
                head(i, 1)
            st.loop(PEER_H // 2, per, pair)

def peer_gates(nc, K, d, sel, gates):
    G = 8
    GP = 4
    with Phase(nc, "gates") as ph:
        selt = ph.sb("selt", [P, 3, T])
        iota = ph.sb("iota", [P, NKEY])
        rows = ph.sb("rows", [P, 2, G, NKEY])
        cols = ph.sb("cols", [P, 2, G, NKEY])
        slab = ph.sb("slab", [P, 2, NKEY, P])
        t_ps = ph.banks("t_ps", 3)
        g_ps = ph.banks("g_ps", 4)
        cst, tr_done, tr_stored, rows_dist, rows_near, rows_done, cols_done, g_done, g_stored, passed = ph.sems(
            "consts", "trans_done", "trans_stored", "rows_dist", "rows_by_pool", "rows_by_dve", "cols_done", "g_done", "g_stored",
            "passed")
        slab_out = ph.sems("slab_out0", "slab_out1")
        block = ph.block()
        groups = P // G

        @block.gpsimd
        def _(g):
            nc.gpsimd.iota(iota[:], [[1, NKEY]], base=0, channel_multiplier=0,
                           allow_small_or_imprecise_dtypes=True).then_inc(cst, 1)
            g.wait_ge(cst, 1)
            g.wait_ge(tr_stored, 3)
            with g.Fori(0, T // (2 * G)) as i:
                for b in range(2):
                    g.wait_ge(g_done, i * 2 + b + 1)
                    nc.gpsimd.tensor_tensor(rows[:, b, 0:GP], iota[:].unsqueeze(1).to_broadcast([P, GP, NKEY]),
                                            selt[:, 0, bass.ds(i * (2 * G) + b * G, GP)].unsqueeze(2).to_broadcast([P, GP, NKEY]),
                                            ALU.subtract).then_inc(rows_dist, 1)
                    g.wait_ge(rows_dist, i * 2 + b + 1)
                    g.sem_inc(passed, 1)
                    nc.gpsimd.tensor_scalar(rows[:, b, 0:GP], rows[:, b, 0:GP], 0.0, None, ALU.is_equal).then_inc(rows_near, 1)

        @block.vector
        def _(dve):
            for w in range(3):
                dve.wait_ge(tr_done, w + 1)
                nc.vector.tensor_copy(selt[:, w, :], t_ps[:, w * T:(w + 1) * T]).then_inc(tr_stored, 1)
            dve.wait_ge(cst, 1)
            dve.wait_ge(tr_stored, 3)

            with dve.Fori(0, T // (2 * G)) as i:
                for b in range(2):
                    dve.wait_ge(g_done, i * 2 + b + 1)
                    at = bass.ds(i * (2 * G) + (b * G + GP), G - GP)
                    nc.vector.tensor_tensor(rows[:, b, GP:], iota[:].unsqueeze(1).to_broadcast([P, G - GP, NKEY]),
                                            selt[:, 0, at].unsqueeze(2).to_broadcast([P, G - GP, NKEY]), ALU.is_equal).then_inc(rows_done, 1)
                    for t in range(G):
                        one = bass.ds(i * (2 * G) + (b * G + t), 1)
                        last = nc.vector.tensor_scalar(cols[:, b, t, :], iota[:], selt[:, 1, one], selt[:, 2, one],
                                                       ALU.is_equal, ALU.mult)
                    last.then_inc(cols_done, 1)

        @block.tensor
        def _(pe):
            for w in range(3):
                for t in range(TT):
                    last = nc.tensor.transpose(t_ps[:, w * T + t * P:w * T + (t + 1) * P], sel[:, w, t, :], K.ident[:])
                last.then_inc(tr_done, 1)
            pe.sem_inc(g_done, 2)
            with pe.Fori(0, T // (2 * G)) as i:
                for b in range(2):
                    pe.wait_ge(rows_near, i * 2 + b + 1)
                    pe.wait_ge(rows_done, i * 2 + b + 1)
                    pe.wait_ge(cols_done, i * 2 + b + 1)
                    pe.wait_ge(g_stored, i * 2 + b + 1)
                    for t in range(G):
                        last = nc.tensor.matmul(g_ps[:, b * 1024 + t * P:b * 1024 + (t + 1) * P], rows[:, b, t, :], cols[:, b, t, :],
                                                start=True, stop=True)
                    last.then_inc(g_done, 1)

        @block.scalar
        def _(act):
            act.sem_inc(g_stored, 2)

            def group(i, n, par, b):
                act.wait_ge(g_done, i + 3)
                nc.scalar.activation(slab[:, par, :, bass.ds(n * G, G)].rearrange("p i t -> p t i"),
                                     g_ps[:, b * 1024:b * 1024 + G * P].rearrange("p (t i) -> p t i", t=G),
                                     ACT.Copy).then_inc(g_stored, 1)

            for tt in range(TT):
                par = tt % 2
                if tt >= 2:
                    act.wait_ge(slab_out[par], 16)
                with act.Fori(0, groups // 2) as i:
                    for b in range(2):
                        group(i * 2 + (tt * groups + b), i * 2 + b, par, b)
                act.wait_ge(g_stored, (tt + 1) * groups + 2)
                act.dma_start(gates[tt], slab[:, par].rearrange("p i t -> p (i t)")).then_inc(slab_out[par], 16)
            for s in slab_out:
                act.wait_ge(s, 32)


def peer_experts(nc, K, d, gates):
    J = 4
    with Phase(nc, "experts") as ph:
        R = 4
        hp = ph.sb("h_parts", [P, 2, KT, T], F32R)
        u_raw = ph.sb("u_raw", [P, R, KT * P])
        v_raw = ph.sb("v_raw", [P, R, D])
        slab = ph.sb("slab", [P, R, TT, P])
        up = ph.sb("u_parts", [P, 2, 2, KT * P], F32R)
        vp = ph.sb("v_parts", [P, J, 2, D], F32R)
        act_sb = ph.sb("gelu", [P, 2, T])
        wact = ph.sb("wact", [P, 2, T])
        wp = ph.sb("wact_parts", [P, J, 2, T], F32R)
        acc = K.h
        MG = 4 * 24 // (NKEY // J)
        M = Modulation(nc, K, ph, d, 48, 4 * 24, MG, [(2, 48)])
        a_ps = ph.banks("a_ps", 4)
        o_ps = ph.banks("o_ps", 4)
        u_in = ph.sems(*[f"u_in{i}" for i in range(R)])
        g_in = ph.sems(*[f"g_in{i}" for i in range(R)])
        v_in = ph.sems(*[f"v_in{i}" for i in range(R)])
        (h_hi, h_lo, u_hi, u_lo, v_hi, v_lo, a_done, gelu_done, w_done, w_hi, w_lo, o_done, acc_done, v) = ph.sems(
            "h_hi", "h_lo", "u_hi", "u_lo", "v_hi", "v_lo", "a_done", "gelu_done", "weighted_done", "w_hi", "w_lo",
            "o_done", "acc_done", "v")
        block = ph.block()
        groups = NKEY // J
        g_h = gates.rearrange("b p (i t) -> i p b t", t=P)

        @block.sync
        def _(sp):
            for s in range(R):
                sp.dma_start(u_raw[:, s, :], d["peer_u"][s]).then_inc(u_in[s], 16)
                sp.dma_start(slab[:, s], g_h[s]).then_inc(g_in[s], 16)
            with sp.Fori(0, groups - 1) as i:
                for s in range(R):
                    sp.wait_ge(u_lo, i * R + (s + 1))
                    sp.dma_start(u_raw[:, s, :], d["peer_u"][i * R + (s + R)]).then_inc(u_in[s], 16)
                    sp.wait_ge(w_done, i * R + (s + 3))
                    sp.dma_start(slab[:, s], g_h[i * R + (s + R)]).then_inc(g_in[s], 16)

        @block.gpsimd
        def _(g):
            for s in range(R):
                g.dma_start(v_raw[:, s, :], d["peer_v"][s]).then_inc(v_in[s], 16)
            g.dma_start(M.rows[:, 0, :], d["c_rows"][2].partition_broadcast(P)).then_inc(M.rows_in, 16)
            for s in range(MG):
                g.dma_start(M.ring[:, s, :], d["w_mod"][48 + s]).then_inc(M.ready[s], 16)
            M.start_mul(g, nc.gpsimd)

            def modulation(i, last):
                for s in range(MG):
                    M.multiply(g, nc.gpsimd, i * MG + s, s, i * 16)
                    if not last:
                        g.wait_ge(M.multiplied, i * MG + (s + 1))
                        g.dma_start(M.ring[:, s, :], d["w_mod"][i * MG + (s + 48 + MG)]).then_inc(M.ready[s], 16)

            with g.Fori(0, groups - 1) as i:
                for s in range(R):
                    g.wait_ge(v_lo, i * R + (s + 1))
                    g.dma_start(v_raw[:, s, :], d["peer_v"][i * R + (s + R)]).then_inc(v_in[s], 16)
                modulation(i, False)
            modulation(groups - 1, True)
            M.finish(g, nc.gpsimd)

        @block.tensor
        def _(pe):
            pe.sem_inc(a_done, 2)
            pe.sem_inc(o_done, 1)

            def h_wait(k):
                pe.wait_ge(h_lo, k + 1)

            def values(i, k, js):
                b = k % 4
                for j in js:
                    if k == 0:
                        pe.wait_ge(v_lo, i * J + (j + 1))
                        pe.wait_ge(w_lo, i * J + (j + 3))
                    last = parts_product(nc, o_ps[:, b * T:(b + 1) * T], lambda a, _: vp[:, j, a, k * P:(k + 1) * P],
                                         lambda a, _: wp[:, j, a, :], (0,), j == 0, j == J - 1)
                return last

            with pe.Fori(0, groups) as i:
                for j in range(J):
                    pe.wait_ge(u_lo, i * J + (j + 1))
                    pe.wait_ge(gelu_done, i * J + (j + 1))
                    parts_product(nc, a_ps[:, j * T:(j + 1) * T], lambda a, k: up[:, j % 2, a, k * P:(k + 1) * P],
                                  lambda a, k: hp[:, a, k, :], range(KT), True, True, h_wait if j == 0 else None).then_inc(a_done, 1)
                pe.wait_ge(acc_done, i * KT + 2)
                for k in (0, 1):
                    values(i, k, range(J - 1))
                for k in (0, 1):
                    values(i, k, (J - 1,)).then_inc(o_done, 1)
                for k in range(2, KT):
                    pe.wait_ge(acc_done, i * KT + (k + 1))
                    values(i, k, range(J)).then_inc(o_done, 1)

        def groups_of(st, per, body):
            st.loop(groups - 1, per, lambda i: body(i, False))
            body(groups - 1, True)

        @block.scalar
        def _(act):
            A = nc.scalar.activation
            act.sem_inc(gelu_done, 4)
            act.sem_inc(w_hi, 2)

            def u_high(i, j):
                act.wait_ge(u_in[j % R], i * 16 + 16 * (j // R + 1))
                act.wait_ge(a_done, i * J + (j + 1))
                A(up[:, j % 2, 0, :], u_raw[:, j % R, :], ACT.Copy).then_inc(u_hi, 1)

            def group(i, last):
                for j in range(J):
                    if not (last and j == J - 1):
                        u_high(i, j + 1)
                    act.wait_ge(v_in[j], i * 16 + 16)
                    act.wait_ge(o_done, i * KT + 1)
                    A(vp[:, j, 0, :], v_raw[:, j, :], ACT.Copy).then_inc(v_hi, 1)
                    act.wait_ge(a_done, i * J + (j + 3))
                    act.wait_ge(w_done, i * J + (j + 1))
                    A(act_sb[:, j % 2, :], a_ps[:, j * T:(j + 1) * T], ACT.Gelu).then_inc(gelu_done, 1)
                    act.wait_ge(w_done, i * J + (j + 3))
                    A(wp[:, j, 0, :], wact[:, j % 2, :], ACT.Copy).then_inc(w_hi, 1)
                for s in range(MG):
                    M.sum(act, i * MG + s)

            M.start_act(act)
            for k in range(KT):
                A(hp[:, 0, k, :], K.h[:, k, :], ACT.Copy).then_inc(h_hi, 1)
            u_high(0, 0)
            groups_of(Steps(act, v), 0, group)

        @block.vector
        def _(dve):
            V = nc.vector
            st = Steps(dve, v)
            dve.sem_inc(acc_done, 4)
            dve.sem_inc(w_done, 2)
            dve.sem_inc(w_lo, 2)
            for k in range(KT):
                dve.wait_ge(h_hi, k + 1)
                V.tensor_tensor(hp[:, 1, k, :], K.h[:, k, :], hp[:, 0, k, :].bitcast(F32), ALU.subtract).then_inc(h_lo, 1)
            dve.wait_ge(h_lo, KT)

            def u_low(i, j):
                dve.wait_ge(u_hi, i * J + (j + 1))
                V.tensor_tensor(up[:, j % 2, 1, :], u_raw[:, j % R, :], up[:, j % 2, 0, :].bitcast(F32), ALU.subtract).then_inc(u_lo, 1)

            def group(i, last):
                for j in range(J):
                    if not (last and j == J - 1):
                        u_low(i, j + 1)
                    dve.wait_ge(v_hi, i * J + (j + 1))
                    V.tensor_tensor(vp[:, j, 1, :], v_raw[:, j, :], vp[:, j, 0, :].bitcast(F32), ALU.subtract).then_inc(v_lo, 1)
                    dve.wait_ge(gelu_done, i * J + (j + 5))
                    dve.wait_ge(g_in[j], i * 16 + 16)
                    dve.wait_ge(w_hi, i * J + (j + 1))
                    dve.wait_ge(w_lo, i * J + (j + 1))
                    V.tensor_tensor(wact[:, j % 2, :], act_sb[:, j % 2, :], slab[:, j].rearrange("p b t -> p (b t)"),
                                    ALU.mult).then_inc(w_done, 1)
                    dve.wait_ge(w_hi, i * J + (j + 3))
                    dve.wait_ge(w_done, i * J + (j + 3))
                    V.tensor_tensor(wp[:, j, 1, :], wact[:, j % 2, :], wp[:, j, 0, :].bitcast(F32), ALU.subtract).then_inc(w_lo, 1)
                for k in range(KT):
                    dve.wait_ge(o_done, i * KT + (k + 2))
                    dve.wait_ge(acc_done, i * KT + 4)
                    V.tensor_tensor(acc[:, k, :], acc[:, k, :], o_ps[:, (k % 4) * T:(k % 4 + 1) * T], ALU.add).then_inc(acc_done, 1)

            st.then(V.memset(acc[:], 0.0))
            u_low(0, 0)
            groups_of(st, 0, group)
            dve.wait_ge(acc_done, groups * KT + 4)
            for k in range(KT):
                st.do(V.scalar_tensor_tensor(out=K.x[:, k, :], in0=acc[:, k, :], scalar=K.mod[:, 40 + k:41 + k],
                                             in1=K.x[:, k, :], op0=ALU.mult, op1=ALU.add))
            dve.wait_ge(M.v, 1)
            for s in range(4):
                st.do(V.tensor_scalar(K.ops[:, s, :], K.mod[:, 48 + 24 * s + 8:48 + 24 * s + 24], 1.0, None, ALU.add))
            st.sync()


def peer(nc, K, d):
    gates = nc.dram_tensor("peer_gates", (TT, P, NKEY * P), F32, kind="Internal").ap()
    with nc.sbuf_tensor("sel", [P, 3, TT, P], F32) as sel:
        peer_route(nc, K, d, sel)
        peer_gates(nc, K, d, sel, gates)
    peer_experts(nc, K, d, gates)


def lay_out_peer(w):
    u = w["peer_u"][0].reshape(NKEY, NKEY, KT, P)
    return {
        "peer_keys": np.ascontiguousarray(np.stack([w["peer_k1"][0].T, w["peer_k2"][0].T], 1)),
        "peer_wq": _tiles(w["peer_wq"][0]),
        "peer_u": np.ascontiguousarray(u.transpose(1, 3, 2, 0)).reshape(NKEY, P, D),
        "peer_v": np.ascontiguousarray(w["peer_v"][0].reshape(NKEY, NKEY, D).transpose(1, 0, 2)),
    }


def modulate(nc, K, s):
    at = 48 + 24 * s
    with Phase(nc, f"modulate{s}") as ph:
        a, v = ph.sems("a", "v")
        block = ph.block()

        @block.scalar
        def _(act):
            for k in range(0, KT, 2):
                nc.scalar.activation(K.h[:, k, :], K.x[:, k, :], ACT.Identity, scale=K.ops[:, s, k:k + 1],
                                     bias=K.mod[:, at + k:at + k + 1]).then_inc(a, 1)
            act.wait_ge(a, KT // 2)

        @block.vector
        def _(dve):
            for k in range(1, KT, 2):
                nc.vector.tensor_scalar(K.h[:, k, :], K.x[:, k, :], K.ops[:, s, k:k + 1], K.mod[:, at + k:at + k + 1],
                                        ALU.mult, ALU.add).then_inc(v, 1)
            dve.wait_ge(v, KT // 2)


def residual_alpha(nc, K, s, bias=None):
    def act_step(i, bank, buf):
        xk = K.x[:, bass.ds(i, 1), :].squeeze(1)
        if bias is None:
            return nc.scalar.activation(buf, xk, ACT.Copy, scale=ALPHA)
        return nc.scalar.activation(buf, xk, ACT.Identity, scale=ALPHA, bias=bias[:, bass.ds(i, 1)])

    def dve_step(st, i, bank, buf):
        xk = K.x[:, bass.ds(i, 1), :].squeeze(1)
        return nc.vector.scalar_tensor_tensor(out=xk, in0=bank, scalar=K.ops[:, s, bass.ds(i + 8, 1)], in1=buf,
                                              op0=ALU.mult, op1=ALU.add)
    return act_step, dve_step, 0


def mlp(nc, K, d, l):
    s = 2 * l + 1
    b1 = VEC["mlp_b1"][0] + 32 * l
    b2 = VEC["mlp_b2"][0] + 8 * l
    HT = FF // P // 2
    modulate(nc, K, s)
    with ExitStack() as c:
        hp = c.enter_context(nc.sbuf_tensor(f"h_parts{l}", [P, 2, KT, T], F32R))
        hidden = c.enter_context(nc.sbuf_tensor(f"hidden{l}", [P, 2, HT, T], F32R))
        gb2 = c.enter_context(nc.sbuf_tensor(f"gb2_{l}", [P, KT], F32))

        def square(st, i, bank, buf):
            hi, lo = [hidden[:, a, bass.ds(i, 1), :].squeeze(1) for a in range(2)]
            st.then(nc.vector.tensor_tensor(buf, buf, buf, ALU.mult))
            st.then(nc.vector.tensor_copy(hi, buf))
            return nc.vector.tensor_tensor(lo, buf, hi.bitcast(F32), ALU.subtract)

        gated_bias(nc, K, f"gb{l}", gb2, s, b2)
        for half in range(2):
            def relu(i, bank, buf):
                return nc.scalar.activation(buf, bank, ACT.Relu, bias=K.vec[:, bass.ds(i + (b1 + half * HT), 1)])

            linear_phase(nc, K, f"mlp1_{l}{half}", lambda n: d[f"mlp_w1_{l}"][n + half * HT], None if half else K.h, HT,
                         (relu, square, 2), parts=hp)
            linear_phase(nc, K, f"mlp2_{l}{half}", lambda n: d[f"mlp_w2_{l}"][half, n], None, KT,
                         residual(K, K.ops[:, s, 8:16]) if half else residual_alpha(nc, K, s, gb2), chunks=2, parts=hidden)
    g, b = VEC["ln_ffn_g"][0] + 8 * l, VEC["ln_ffn_b"][0] + 8 * l
    norm_phase(nc, K, f"ln_ffn{l}", [(K.x, K.x, T, K.vec[:, g:g + KT], K.vec[:, b:b + KT])], center=True)


def gated_bias(nc, K, name, out, s, b):
    with Phase(nc, name) as ph:
        v = ph.sems("v")
        block = ph.block()

        @block.vector
        def _(dve):
            nc.vector.tensor_tensor(out[:], K.ops[:, s, 8:16], K.vec[:, b:b + KT], ALU.mult).then_inc(v, 1)
            dve.wait_ge(v, 1)


TWO_PI = 2 * math.pi
C1 = 6.28125
C2 = float(np.float32(round((TWO_PI - C1) * 2 ** 22) / 2 ** 22))
C3 = float(np.float32(TWO_PI - C1 - C2))
PI_IN = 3.1415925


def reduce_angle(V, st, ang, n):
    st.then(V.tensor_scalar(n, ang, 1.0 / TWO_PI, ROUNDMAGIC, ALU.mult, ALU.add))
    st.then(V.tensor_scalar(n, n, ROUNDMAGIC, None, ALU.subtract))
    for c in (C1, C2, C3):
        st.then(V.scalar_tensor_tensor(out=ang, in0=n, scalar=-c, in1=ang, op0=ALU.mult, op1=ALU.add))


def quarter_turn(V, st, out, ang, n):
    st.then(V.tensor_scalar(out, ang, math.pi / 2, None, ALU.add))
    st.then(V.tensor_scalar(n, out, math.pi, None, ALU.is_gt))
    st.then(V.scalar_tensor_tensor(out=out, in0=n, scalar=-TWO_PI, in1=out, op0=ALU.mult, op1=ALU.add))
    st.then(V.tensor_scalar(out, out, PI_IN, -PI_IN, ALU.min, ALU.max))


QN = 192 ** -0.5


def mla(nc, K, d):
    modulate(nc, K, 0)
    with ExitStack() as c:
        cq = c.enter_context(nc.sbuf_tensor("cq", [P, 2, T], F32))
        ckv = c.enter_context(nc.sbuf_tensor("ckv", [P, T], F32))
        kpe = c.enter_context(nc.sbuf_tensor("kpe", [P, T], F32))
        csq = c.enter_context(nc.sbuf_tensor("csq", [P, T], F32))
        mla_in(nc, K, d, cq, ckv, kpe, csq)
        mla_heads(nc, K, d, cq, ckv, kpe, csq)
    linear_phase(nc, K, "mla_out", lambda n: d["mla_wo"][n], K.h, KT, residual_alpha(nc, K, 0))
    g, b = VEC["ln_mix_g"][0], VEC["ln_mix_b"][0]
    norm_phase(nc, K, "ln_mix0", [(K.x, K.x, T, K.vec[:, g:g + KT], K.vec[:, b:b + KT])], center=True)


def mla_in(nc, K, d, cq, ckv, kpe, csq):
    with Phase(nc, "mla_in") as ph:
        ring = ph.sb("ring", [P, 5, KT * P])
        pos = ph.sb("pos", [P, T], I32)
        ang = ph.sb("ang", [P, T])
        ang2 = ph.sb("ang2", [P, T])
        n = ph.sb("n", [P, T])
        zsq = ph.sb("zsq", [P, 3, T])
        rstd = ph.sb("rstd", [P, 2, T])
        z = ph.banks("z", 5)
        sums = ph.banks("sums", 2)
        w_in = ph.sems(*[f"w_in{i}" for i in range(5)])
        pos_in, z_done, v, ang_done, trig_done, sq_done, sum_done, rstd_done, a = ph.sems(
            "pos_in", "z_done", "v", "angle_done", "trig_done", "sq_done", "sum_done", "rstd_done", "a")
        block = ph.block()
        fq, sg = VEC["inv_freq"][0], VEC["rope_sign"][0]
        qn, kvn = VEC["q_norm"][0], VEC["kv_norm"][0]

        @block.sync
        def _(sp):
            sp.dma_start(pos[:], d["positions"].partition_broadcast(P)).then_inc(pos_in, 16)
            for t in range(5):
                sp.dma_start(ring[:, t, :], d["mla_win"][t]).then_inc(w_in[t], 16)

        @block.tensor
        def _(pe):
            for t in range(5):
                pe.wait_ge(w_in[t], 16)
                for k in range(KT):
                    last = nc.tensor.matmul(z[:, t * T:(t + 1) * T], ring[:, t, k * P:(k + 1) * P], K.h[:, k, :],
                                            start=k == 0, stop=k == KT - 1)
                last.then_inc(z_done, 1)
            pe.wait_ge(sq_done, 3)
            nc.tensor.matmul(sums[:, 0:T], K.ones[:], zsq[:, 0, :], start=True, stop=False)
            nc.tensor.matmul(sums[:, 0:T], K.ones[:], zsq[:, 1, :], start=False, stop=True)
            nc.tensor.matmul(sums[:, T:2 * T], K.ones[:], zsq[:, 2, :], start=True, stop=True).then_inc(sum_done, 1)

        @block.scalar
        def _(act):
            st = Steps(act, a)
            act.wait_ge(ang_done, 2)
            nc.scalar.activation(ang[:], ang[:], ACT.Sin).then_inc(trig_done, 1)
            nc.scalar.activation(ang2[:], ang2[:], ACT.Sin).then_inc(trig_done, 1)
            for t in range(3):
                act.wait_ge(z_done, t + 1)
                nc.scalar.activation(zsq[:, t, :], z[:, t * T:(t + 1) * T], ACT.Square).then_inc(sq_done, 1)
            act.wait_ge(sum_done, 1)
            st.do(nc.scalar.activation(rstd[:, 0, :], sums[:, 0:T], ACT.Ln, scale=1.0 / 256, bias=EPS))
            st.then(nc.scalar.activation(rstd[:, 1, :], sums[:, T:2 * T], ACT.Ln, scale=1.0 / 128, bias=EPS))
            nc.scalar.activation(rstd[:], rstd[:], ACT.Exp, scale=-0.5).then_inc(rstd_done, 1)

        @block.vector
        def _(dve):
            V = nc.vector
            st = Steps(dve, v)
            dve.wait_ge(pos_in, 16)
            st.then(V.tensor_copy(ang[:], pos[:]))
            st.then(V.tensor_scalar(ang[:], ang[:], K.vec[:, fq:fq + 1], None, ALU.mult))
            reduce_angle(V, st, ang[:], n[:])
            quarter_turn(V, st, ang2[:], ang[:], n[:])
            V.tensor_scalar(ang[:], ang[:], PI_IN, -PI_IN, ALU.min, ALU.max).then_inc(ang_done, 2)
            dve.wait_ge(trig_done, 2)
            st.then(V.tensor_scalar(ang[:], ang[:], K.vec[:, sg:sg + 1], None, ALU.mult))
            st.do(V.tensor_copy(csq[0:64, :], ang2[0:64, :]))
            st.do(V.tensor_copy(csq[64:128, :], ang[64:128, :]))
            dve.wait_ge(z_done, 5)
            st.do(V.tensor_tensor(n[:], ang2[:], z[:, 3 * T:4 * T], ALU.mult))
            st.then(V.tensor_tensor(kpe[:], ang[:], z[:, 4 * T:5 * T], ALU.mult))
            st.do(V.tensor_tensor(kpe[:], kpe[:], n[:], ALU.add))
            dve.wait_ge(rstd_done, 1)
            for t in range(3):
                out = cq[:, t, :] if t < 2 else ckv[:]
                g = K.vec[:, qn + t:qn + t + 1] if t < 2 else K.vec[:, kvn:kvn + 1]
                st.do(V.scalar_tensor_tensor(out=out, in0=z[:, t * T:(t + 1) * T], scalar=g, in1=rstd[:, t // 2, :],
                                             op0=ALU.mult, op1=ALU.mult))
            st.sync()


def mla_heads(nc, K, d, cq, ckv, kpe, csq):
    W = 2 * 256 + 128 + 128
    with Phase(nc, "mla") as ph:
        wts = ph.sb("wts", [P, 2, W])
        qn = ph.sb("qn", [P, 2, T])
        qp = ph.sb("qp", [P, 2, T])
        kn = ph.sb("kn", [P, 2, T])
        vt = ph.sb("vt", [P, 2, TT, P])
        big = ph.sb("mask", [P, TT * P])
        prob = ph.sb("prob", [P, 2, T])
        probt = ph.sb("probt", [P, 2, T])
        stat = ph.sb("stat", [P, 2, 3])
        sm = ph.sb("rowsum", [P, 2, 1])
        pr = ph.banks("proj", 4)
        sc = ph.banks("score", 2)
        tr = ph.banks("trans")
        op = ph.banks("out")
        w_ready = ph.sems("w_ready0", "w_ready1")
        (p_done, q_stored, qp_stored, s_done, masked, max_done, exp_done, prob_done, t_done, t_stored, o_done, o_stored,
         cst, v) = ph.sems("proj_done", "q_stored", "qpe_stored", "score_done", "masked", "max_done", "exp_done", "prob_done",
                           "trans_done", "trans_stored", "out_done", "out_stored", "consts", "v")
        block = ph.block()
        H = 8

        @block.gpsimd
        def _(g):
            nc.gpsimd.memset(big[:], 0.0).then_inc(cst, 1)
            g.wait_ge(cst, 1)
            nc.gpsimd.affine_select(out=big[:], in_=big[:], compare_op=ALU.is_ge, fill=-1.0e30, base=(TT - 1) * P,
                                    pattern=[[-1, TT * P]], channel_multiplier=1).then_inc(cst, 1)

        @block.sync
        def _(sp):
            for b in range(2):
                sp.dma_start(wts[:, b, :], d["mla_wh"][b]).then_inc(w_ready[b], 16)
            with sp.Fori(0, H // 2 - 1) as i:
                for b in range(2):
                    sp.wait_ge(p_done, i * 4 + 2 * b + 2)
                    sp.dma_start(wts[:, b, :], d["mla_wh"][i * 2 + (b + 2)]).then_inc(w_ready[b], 16)

        @block.tensor
        def _(pe):
            def project(i, b):
                pe.wait_ge(w_ready[b], i * 16 + 16)
                if b:
                    pe.wait_ge(q_stored, i * 6 + 3)
                    pe.wait_ge(qp_stored, i * 2 + 1)
                else:
                    pe.wait_ge(q_stored, i * 6)
                    pe.wait_ge(qp_stored, i * 2)
                for o, c in ((0, 0), (1, P)):
                    for k in range(2):
                        nc.tensor.matmul(pr[:, o * T:(o + 1) * T], wts[:, b, k * 256 + c:k * 256 + c + P], cq[:, k, :],
                                         start=k == 0, stop=k == 1)
                nc.tensor.matmul(pr[:, 2 * T:3 * T], wts[:, b, 512:640], ckv[:], start=True, stop=True).then_inc(p_done, 1)
                for t in range(TT):
                    last = nc.tensor.matmul(pr[:, 3 * T + t * P:3 * T + (t + 1) * P], ckv[:, t * P:(t + 1) * P], wts[:, b, 640:768],
                                            start=True, stop=True)
                last.then_inc(p_done, 1)

            def scores(i, b, qt):
                n = i * 8 + (b * 4 + qt)
                if qt == 0:
                    pe.wait_ge(q_stored, i * 6 + 3 * b + 3)
                    pe.wait_ge(qp_stored, i * 2 + b + 1)
                pe.wait_ge(masked, n + 1)
                o = (qt % 2) * T
                w = (qt + 1) * P
                nc.tensor.matmul(sc[:, o:o + w], qn[:, b, qt * P:w], kn[:, b, 0:w], start=True, stop=False)
                nc.tensor.matmul(sc[:, o:o + w], qp[:, b, qt * P:w], kpe[:, 0:w], start=False, stop=True).then_inc(s_done, 1)

            def weigh(i, b, qt):
                n = i * 8 + (b * 4 + qt)
                pe.wait_ge(prob_done, n + 1)
                pe.wait_ge(t_stored, n + 1)
                for k in range(qt + 1):
                    last = nc.tensor.transpose(tr[:, k * P:(k + 1) * P], prob[:, qt % 2, k * P:(k + 1) * P], K.ident[:])
                last.then_inc(t_done, 1)

            def output(i, b, qt):
                n = i * 8 + (b * 4 + qt)
                pe.wait_ge(t_stored, n + 2)
                if qt == 0:
                    pe.wait_ge(o_stored, i * 2 + b + 1)
                for k in range(qt + 1):
                    last = nc.tensor.matmul(op[:, qt * P:(qt + 1) * P], vt[:, b, k, :], probt[:, qt % 2, k * P:(k + 1) * P],
                                            start=k == 0, stop=k == qt)
                last.then_inc(o_done, 1)

            pe.sem_inc(t_done, 2)
            pe.sem_inc(o_done, 1)
            project(0, 0)
            scores(0, 0, 0)

            def head(i, b, nxt):
                scores(i, b, 1)
                weigh(i, b, 0)
                if nxt:
                    project(*nxt)
                output(i, b, 0)
                scores(i, b, 2)
                weigh(i, b, 1)
                output(i, b, 1)
                scores(i, b, 3)
                weigh(i, b, 2)
                output(i, b, 2)
                if nxt:
                    scores(*nxt, 0)
                weigh(i, b, 3)
                output(i, b, 3)

            with pe.Fori(0, H // 2 - 1) as i:
                head(i, 0, (i, 1))
                head(i, 1, (i + 1, 0))
            head(H // 2 - 1, 0, (H // 2 - 1, 1))
            head(H // 2 - 1, 1, None)

        @block.scalar
        def _(act):
            def store(i, b):
                act.wait_ge(p_done, i * 4 + 2 * b + 1)
                nc.scalar.activation(qn[:, b, :], pr[:, 0:T], ACT.Copy).then_inc(q_stored, 1)
                nc.scalar.activation(kn[:, b, :], pr[:, 2 * T:3 * T], ACT.Copy).then_inc(q_stored, 1)
                act.wait_ge(p_done, i * 4 + 2 * b + 2)
                nc.scalar.activation(vt[:, b], pr[:, 3 * T:4 * T].rearrange("p (t v) -> p t v", t=TT), ACT.Copy).then_inc(q_stored, 1)

            def exp(i, b, qt):
                n = i * 8 + (b * 4 + qt)
                w = (qt + 1) * P
                act.wait_ge(max_done, n + 1)
                nc.scalar.activation(prob[:, qt % 2, 0:w], prob[:, qt % 2, 0:w], ACT.Exp, scale=QN,
                                     bias=stat[:, qt % 2, 1:2], accum_out=sm[:, qt % 2, :]).then_inc(exp_done, 1)

            def store_t(i, b, qt):
                n = i * 8 + (b * 4 + qt)
                w = (qt + 1) * P
                act.wait_ge(t_done, n + 3)
                if qt >= 2:
                    act.wait_ge(o_done, n)
                else:
                    act.wait_ge(o_done, i * 8 + b * 4 + 1)
                nc.scalar.activation(probt[:, qt % 2, 0:w], tr[:, 0:w], ACT.Copy).then_inc(t_stored, 1)

            def head(i, b, nxt):
                exp(i, b, 1)
                store_t(i, b, 0)
                if nxt:
                    store(*nxt)
                exp(i, b, 2)
                store_t(i, b, 1)
                exp(i, b, 3)
                store_t(i, b, 2)
                if nxt:
                    exp(*nxt, 0)
                store_t(i, b, 3)
                act.wait_ge(o_done, i * 8 + b * 4 + 5)
                nc.scalar.activation(K.h[:, bass.ds(i * 2 + b, 1), :].squeeze(1), op[:, 0:T], ACT.Copy).then_inc(o_stored, 1)

            act.sem_inc(t_stored, 1)
            act.sem_inc(o_stored, 1)
            store(0, 0)
            exp(0, 0, 0)
            with act.Fori(0, H // 2 - 1) as i:
                head(i, 0, (i, 1))
                head(i, 1, (i + 1, 0))
            head(H // 2 - 1, 0, (H // 2 - 1, 1))
            head(H // 2 - 1, 1, None)
            act.wait_ge(o_stored, H + 1)

        @block.vector
        def _(dve):
            V = nc.vector
            st = Steps(dve, v)
            dve.wait_ge(cst, 2)
            dve.sem_inc(masked, 2)

            def store(i, b):
                dve.wait_ge(p_done, i * 4 + 2 * b + 1)
                V.tensor_tensor(qp[:, b, :], csq[:], pr[:, T:2 * T], ALU.mult).then_inc(qp_stored, 1)

            def logits(i, b, qt):
                n = i * 8 + (b * 4 + qt)
                w = (qt + 1) * P
                dve.wait_ge(s_done, n + 1)
                dve.wait_ge(t_done, n + 1)
                V.tensor_tensor(prob[:, qt % 2, 0:w], big[:, (TT - 1 - qt) * P:TT * P], sc[:, (qt % 2) * T:(qt % 2) * T + w],
                                ALU.add).then_inc(masked, 1)
                dve.wait_ge(masked, n + 3)
                st.then(V.reduce_max(stat[:, qt % 2, 0:1], prob[:, qt % 2, 0:w], AXX))
                V.tensor_scalar(stat[:, qt % 2, 1:2], stat[:, qt % 2, 0:1], -QN, None, ALU.mult).then_inc(max_done, 1)

            def normalize(i, b, qt):
                n = i * 8 + (b * 4 + qt)
                w = (qt + 1) * P
                dve.wait_ge(exp_done, n + 1)
                st.then(V.reciprocal(stat[:, qt % 2, 2:3], sm[:, qt % 2, :]))
                V.tensor_scalar(prob[:, qt % 2, 0:w], prob[:, qt % 2, 0:w], stat[:, qt % 2, 2:3], None, ALU.mult).then_inc(prob_done, 1)

            def head(i, b, nxt):
                logits(i, b, 1)
                normalize(i, b, 0)
                if nxt:
                    store(*nxt)
                normalize(i, b, 1)
                logits(i, b, 2)
                normalize(i, b, 2)
                logits(i, b, 3)
                if nxt:
                    logits(*nxt, 0)
                normalize(i, b, 3)

            store(0, 0)
            logits(0, 0, 0)
            n0 = st.n
            with dve.Fori(0, H // 2 - 1) as i:
                st.turn = i * 16
                head(i, 0, (i, 1))
                head(i, 1, (i + 1, 0))
            assert st.n - n0 == 16, st.n - n0
            st.n, st.turn = n0 + 16 * (H // 2 - 1), 0
            head(H // 2 - 1, 0, (H // 2 - 1, 1))
            head(H // 2 - 1, 1, None)


def lay_out_mla(w):
    wi = w["mla_w_in_2"][0]
    x1, x2 = wi[:, 384:416], wi[:, 416:448]
    wi = np.concatenate([wi[:, 0:384], x1, x2, x1, x2, x2, x1, x2, x1], 1)
    qb = w["mla_w_qb_2"][0].reshape(256, 8, 192)
    qb = np.concatenate([qb, qb[:, :, 160:192], qb[:, :, 128:160]], 2)
    kvb = w["mla_w_kvb_2"][0].reshape(128, 8, 256)
    wh = np.concatenate([qb[0:128].transpose(1, 0, 2), qb[128:256].transpose(1, 0, 2), kvb.transpose(1, 0, 2)], 2)
    return {"mla_win": _tiles(wi), "mla_wh": np.ascontiguousarray(wh), "mla_wo": _tiles(w["mla_w_o_2"][0]),
            "positions": np.asarray(w["positions_2"]).reshape(T)}


def lay_out_rest(w):
    a = {}
    for l in range(2):
        a[f"mlp_w1_{l}"] = _tiles(w["mlp_w1_2"][l])
        w2 = _tiles(w["mlp_w2_2"][l]).reshape(KT, P, 4, D)
        a[f"mlp_w2_{l}"] = np.ascontiguousarray(w2.transpose(2, 0, 1, 3)).reshape(2, 2, KT, P, D).transpose(0, 2, 1, 3, 4).reshape(2, 2 * KT, P, D)
    return a


LB, LA = 32, 16
NST = 32


def ssm(nc, K, d):
    modulate(nc, K, 2)
    with ExitStack() as c:
        def keep(name, shape):
            return c.enter_context(nc.sbuf_tensor(name, shape, F32))

        u = keep("ssm_u", [P, KT, T])
        g = keep("ssm_g", [P, KT, T])

        def store(st, i, bank, buf):
            return nc.vector.tensor_copy(u[:, bass.ds(i, 1), :].squeeze(1), bank)

        linear_phase(nc, K, "ssm_in", lambda n: d["ssm_win"][n], K.h, KT, (None, store, 0))
        with ExitStack() as c2:
            S = Consts()
            S.mag = c2.enter_context(nc.sbuf_tensor("s_mag", [P, NST], F32))
            S.cb = c2.enter_context(nc.sbuf_tensor("s_cb", [P, 2, NST, LB], F32))
            S.ca = c2.enter_context(nc.sbuf_tensor("s_ca", [P, 2, NST, LA], F32))
            S.bd = c2.enter_context(nc.sbuf_tensor("s_bd", [P, 2, NST, 32], F32))
            S.cd = c2.enter_context(nc.sbuf_tensor("s_cd", [P, 2, NST, 32], F32))
            ssm_tables(nc, K, d, S)
            ssm_scan(nc, K, d, S, u, g)
        bg = VEC["b_glu"][0]

        def gate(i, bank, buf):
            return nc.scalar.activation(buf, bank, ACT.Sigmoid, bias=K.vec[:, bass.ds(i + bg, 1)])

        def times(st, i, bank, buf):
            return nc.vector.tensor_tensor(u[:, bass.ds(i, 1), :].squeeze(1), buf, g[:, bass.ds(i, 1), :].squeeze(1), ALU.mult)

        linear_phase(nc, K, "glu", lambda n: d["ssm_wglu"][n], g, KT, (gate, times, 0))
        linear_phase(nc, K, "ssm_out", lambda n: d["ssm_wout"][n], u, KT, residual_alpha(nc, K, 2))
    gg, bb = VEC["ln_mix_g"][0] + 8, VEC["ln_mix_b"][0] + 8
    norm_phase(nc, K, "ln_mix1", [(K.x, K.x, T, K.vec[:, gg:gg + KT], K.vec[:, bb:bb + KT])], center=True)


def ssm_tables(nc, K, d, S):
    with Phase(nc, "tables") as ph:
        prm = ph.sb("prm", [P, 3, NST])
        bc = ph.sb("bc", [P, 4, NST, 16])
        w = ph.sb("w", [P, 14, NST])
        bb = ph.sb("bb", [P, 2, NST, 16])
        t1 = ph.sb("t1", [P, NST, 16])
        steps = ph.sb("steps", [P, LB])
        ang = ph.sb("ang", [P, NST, LB])
        ang2 = ph.sb("ang2", [P, NST, LB])
        n = ph.sb("n", [P, NST, LB])
        prm_in, cst, dt_done, mag_in, mag_done, ang_done, trig_done, v = ph.sems(
            "prm_in", "consts", "dt_done", "mag_arg", "mag_done", "angle_done", "trig_done", "v")
        block = ph.block()

        @block.sync
        def _(sp):
            sp.dma_start(prm[:], d["ssm_prm"]).then_inc(prm_in, 16)
            sp.dma_start(bc[:], d["ssm_bc"]).then_inc(prm_in, 16)

        @block.gpsimd
        def _(g):
            nc.gpsimd.iota(steps[:], [[1, LB]], base=0, channel_multiplier=0,
                           allow_small_or_imprecise_dtypes=True).then_inc(cst, 1)

        @block.scalar
        def _(act):
            act.wait_ge(prm_in, 32)
            nc.scalar.activation(w[:, 0, :], prm[:, 2, :], ACT.Exp).then_inc(dt_done, 1)
            act.wait_ge(mag_in, 1)
            nc.scalar.activation(S.mag[:], w[:, 1, :], ACT.Exp).then_inc(mag_done, 1)
            act.wait_ge(ang_done, 1)
            nc.scalar.activation(w[:, 4:6, :], w[:, 4:6, :], ACT.Sin).then_inc(trig_done, 1)
            for m, (t, l) in enumerate(((S.cb, LB), (S.ca, LA))):
                act.wait_ge(ang_done, m + 2)
                nc.scalar.activation(t[:, 1], ang[:, :, 0:l], ACT.Sin)
                nc.scalar.activation(t[:, 0], ang2[:, :, 0:l], ACT.Sin).then_inc(trig_done, 1)

        @block.vector
        def _(dve):
            V = nc.vector
            st = Steps(dve, v)
            lr, li = prm[:, 0, :], prm[:, 1, :]
            dt, m, th, th32, sn, cs, are, aim, den, rden, cre, cim, ta, tb = [w[:, k, :] for k in
                                                                            (0, 1, 2, 3, 4, 5, 6, 7, 8, 9, 10, 11, 12, 13)]
            dve.wait_ge(dt_done, 1)
            V.tensor_tensor(m, lr, dt, ALU.mult).then_inc(mag_in, 1)
            st.then(V.tensor_tensor(th, li, dt, ALU.mult))
            reduce_angle(V, st, th, ta)
            st.then(V.tensor_scalar(th, th, PI_IN, -PI_IN, ALU.min, ALU.max))
            st.then(V.tensor_scalar(th32, th, float(LB), None, ALU.mult))
            reduce_angle(V, st, th32, ta)
            quarter_turn(V, st, cs, th, ta)
            V.tensor_copy(sn, th).then_inc(ang_done, 1)
            dve.wait_ge(trig_done, 1)
            dve.wait_ge(mag_done, 1)
            st.then(V.tensor_tensor(are, S.mag[:], cs, ALU.mult))
            st.then(V.tensor_tensor(aim, S.mag[:], sn, ALU.mult))
            st.then(V.tensor_scalar(are, are, -1.0, None, ALU.add))
            st.do(V.tensor_tensor(ta, lr, lr, ALU.mult))
            st.then(V.tensor_tensor(tb, li, li, ALU.mult))
            st.then(V.tensor_tensor(den, ta, tb, ALU.add))
            st.then(V.reciprocal(rden, den))
            for out, x, y, op in ((cre, (are, lr), (aim, li), ALU.add), (cim, (aim, lr), (are, li), ALU.subtract)):
                st.do(V.tensor_tensor(ta, *x, ALU.mult))
                st.then(V.tensor_tensor(tb, *y, ALU.mult))
                st.then(V.tensor_tensor(out, ta, tb, op))
                st.then(V.tensor_tensor(out, out, rden, ALU.mult))

            def wide(x):
                return x.unsqueeze(2).to_broadcast([P, NST, 16])
            br, bi = bc[:, 0], bc[:, 1]
            for k, (x, y, op) in enumerate((((br, cre), (bi, cim), ALU.subtract), ((bi, cre), (br, cim), ALU.add))):
                st.do(V.tensor_tensor(bb[:, k], x[0], wide(x[1]), ALU.mult))
                st.then(V.tensor_tensor(t1[:], y[0], wide(y[1]), ALU.mult))
                st.then(V.tensor_tensor(bb[:, k], bb[:, k], t1[:], op))
            st.do(V.memset(S.bd[:], 0.0))
            st.then(V.memset(S.cd[:], 0.0))
            for k in range(2):
                for hf in range(2):
                    r, c = slice(64 * hf, 64 * hf + 64), slice(16 * hf, 16 * hf + 16)
                    st.do(V.tensor_copy(S.bd[r, k, :, c], bb[r, k]))
                    st.do(V.tensor_scalar(S.cd[r, k, :, c], bc[r, 2 + k], (1.0, -1.0)[k], None, ALU.mult))
            dve.wait_ge(cst, 1)
            for m_, (x, l) in enumerate(((th, LB), (th32, LA))):
                if m_:
                    dve.wait_ge(trig_done, 2)
                st.then(V.tensor_tensor(ang[:, :, 0:l], x.unsqueeze(2).to_broadcast([P, NST, l]),
                                        steps[:, 0:l].unsqueeze(1).to_broadcast([P, NST, l]), ALU.mult))
                reduce_angle(V, st, ang[:, :, 0:l], n[:, :, 0:l])
                quarter_turn(V, st, ang2[:, :, 0:l], ang[:, :, 0:l], n[:, :, 0:l])
                V.tensor_scalar(ang[:, :, 0:l], ang[:, :, 0:l], PI_IN, -PI_IN, ALU.min, ALU.max).then_inc(ang_done, 1)
            st.sync()


def ssm_scan(nc, K, d, S, u, g):
    with Phase(nc, "scan") as ph:
        bst = ph.sb("bst", [P, 2, P])
        bt = ph.sb("bt", [P, 2, P])
        ust = ph.sb("ust", [P, T])
        ct = ph.sb("ct", [P, 2, 4, 32])
        rot = ph.sb("rot", [P, 2, 2, T])
        tmp = ph.sb("tmp", [P, 2, T])
        bu = ph.sb("bu", [P, 2, T])
        wv = ph.sb("wv", [P, 2, T])
        m = ph.sb("m", [P, 4, T])
        xs = ph.sb("xs", [P, 2, 2, T])
        yb = ph.sb("yb", [P, T])
        b_ps = ph.banks("b_ps")
        bu_ps = ph.banks("bu_ps", 4)
        y_ps = ph.banks("y_ps", 2)
        staged, bt_done, bt_stored, bu_done, bu_read, rot_done, rot_used, x_done, y_done, yb_done, g_done, v, gp = ph.sems(
            "staged", "bt_done", "bt_stored", "bu_done", "bu_read", "rot_done", "rot_used", "x_done", "y_done", "yb_done", "g_done", "v", "g")
        block = ph.block()
        dcol = VEC["ssm_d"][0]

        @block.gpsimd
        def _(eng):
            st = Steps(eng, gp)
            G = nc.gpsimd

            def turn(i):
                for t in range(4):
                    b = t % 2
                    eng.wait_ge(rot_used, i * 4 + (t + 1))
                    ca = [S.ca[:, k, bass.ds(i * 4 + t, 1), :].squeeze(1).unsqueeze(2).to_broadcast([P, LA, LB]) for k in range(2)]
                    cb = [S.cb[:, k, bass.ds(i * 4 + t, 1), :].squeeze(1).unsqueeze(1).to_broadcast([P, LA, LB]) for k in range(2)]
                    r = [rot[:, b, k, :].rearrange("p (a b) -> p a b", b=LB) for k in range(2)]
                    q = [tmp[:, k, :].rearrange("p (a b) -> p a b", b=LB) for k in range(2)]
                    st.do(G.tensor_tensor(r[0], ca[0], cb[0], ALU.mult))
                    st.do(G.tensor_tensor(q[0], ca[1], cb[1], ALU.mult))
                    st.do(G.tensor_tensor(r[1], ca[1], cb[0], ALU.mult))
                    st.do(G.tensor_tensor(q[1], ca[0], cb[1], ALU.mult))
                    st.sync()
                    G.tensor_tensor(r[0], r[0], q[0], ALU.subtract).then_inc(rot_done, 1)
                    G.tensor_tensor(r[1], r[1], q[1], ALU.add).then_inc(rot_done, 1)
                    eng.wait_ge(rot_done, i * 8 + (2 * t + 2))
            st.loop(KT, 16, turn)

        @block.tensor
        def _(pe):
            pe.sem_inc(y_done, 1)
            with pe.Fori(0, KT) as i:
                pe.wait_ge(staged, i * 2 + 1)
                for k in range(2):
                    last = nc.tensor.transpose(b_ps[:, k * P:(k + 1) * P], bst[:, k, :], K.ident[:])
                last.then_inc(bt_done, 1)
                pe.wait_ge(bt_stored, i + 2)

                def inputs(t):
                    pe.wait_ge(bu_read, i * 4 + (t + 1))
                    r = slice(32 * t, 32 * t + 32)
                    for k in range(2):
                        o = (2 * (t % 2) + k) * T
                        last = nc.tensor.matmul(bu_ps[:, o:o + T], bt[r, k, :], ust[r, :], start=True, stop=True)
                    last.then_inc(bu_done, 1)

                def outputs(t):
                    pe.wait_ge(x_done, i * 8 + (2 * t + 2))
                    for k in range(2):
                        last = nc.tensor.matmul(y_ps[32 * t:32 * t + 32, 0:T], ct[:, k, t, :], xs[:, t % 2, k, :], start=k == 0, stop=k == 1)
                    last.then_inc(y_done, 1)

                inputs(0)
                inputs(1)
                pe.wait_ge(yb_done, i + 1)
                for t in range(4):
                    outputs(t)
                    if t < 2:
                        inputs(t + 2)

        @block.scalar
        def _(act):
            act.sem_inc(bt_stored, 1)
            act.sem_inc(g_done, 1)
            with act.Fori(0, KT) as i:
                act.wait_ge(bt_done, i + 1)
                act.wait_ge(yb_done, i + 1)
                nc.scalar.activation(ust[:], u[:, bass.ds(i, 1), :].squeeze(1), ACT.Copy)
                nc.scalar.activation(bt[:], b_ps[:, 0:2 * P].rearrange("p (k s) -> p k s", k=2), ACT.Copy).then_inc(bt_stored, 1)
                act.wait_ge(yb_done, i + 2)
                nc.scalar.activation(g[:, bass.ds(i, 1), :].squeeze(1), yb[:], ACT.Gelu_apprx_tanh).then_inc(g_done, 1)
            act.wait_ge(g_done, KT + 1)

        @block.vector
        def _(dve):
            V = nc.vector
            st = Steps(dve, v)
            dve.sem_inc(rot_used, 2)
            dve.sem_inc(yb_done, 1)
            dve.sem_inc(bu_read, 2)

            def turn(i):
                dve.wait_ge(bt_stored, i + 1)
                V.tensor_copy(bst[:].rearrange("p k (t c) -> p k t c", c=32), S.bd[:, :, bass.ds(i * 4, 4), :]).then_inc(staged, 1)
                dve.wait_ge(y_done, i * 4 + 1)
                V.tensor_copy(ct[:], S.cd[:, :, bass.ds(i * 4, 4), :]).then_inc(staged, 1)
                for t in range(4):
                    b = t % 2
                    dve.wait_ge(bu_done, i * 4 + (t + 1))
                    dve.wait_ge(rot_done, i * 8 + (2 * t + 2))
                    co, si = rot[:, b, 0, :], rot[:, b, 1, :]
                    br = bu_ps[:, 2 * b * T:(2 * b + 1) * T]
                    bi = bu_ps[:, (2 * b + 1) * T:(2 * b + 2) * T]
                    st.do(V.tensor_tensor(m[:, 0, :], co, br, ALU.mult))
                    st.do(V.tensor_tensor(m[:, 1, :], si, bi, ALU.mult))
                    st.do(V.tensor_tensor(m[:, 2, :], co, bi, ALU.mult))
                    V.tensor_tensor(m[:, 3, :], si, br, ALU.mult).then_inc(bu_read, 1)
                    st.sync()
                    dve.wait_ge(bu_read, i * 4 + (t + 3))
                    st.do(V.tensor_tensor(bu[:, 0, :], m[:, 0, :], m[:, 1, :], ALU.add))
                    st.then(V.tensor_tensor(bu[:, 1, :], m[:, 2, :], m[:, 3, :], ALU.subtract))
                    mg = S.mag[:, bass.ds(i * 4 + t, 1)].to_broadcast([P, T])
                    for k in range(2):
                        st.do(V.tensor_tensor_scan(wv[:, k, :], mg, bu[:, k, :], 0.0, ALU.mult, ALU.add))
                    st.sync()
                    dve.wait_ge(y_done, i * 4 + (t if t >= 2 else 1))
                    st.do(V.tensor_tensor(m[:, 0, :], co, wv[:, 0, :], ALU.mult))
                    st.do(V.tensor_tensor(m[:, 1, :], si, wv[:, 1, :], ALU.mult))
                    st.do(V.tensor_tensor(m[:, 2, :], co, wv[:, 1, :], ALU.mult))
                    V.tensor_tensor(m[:, 3, :], si, wv[:, 0, :], ALU.mult).then_inc(rot_used, 1)
                    st.sync()
                    dve.wait_ge(rot_used, i * 4 + (t + 3))
                    V.tensor_tensor(xs[:, b, 0, :], m[:, 0, :], m[:, 1, :], ALU.subtract).then_inc(x_done, 1)
                    V.tensor_tensor(xs[:, b, 1, :], m[:, 2, :], m[:, 3, :], ALU.add).then_inc(x_done, 1)
                    dve.wait_ge(x_done, i * 8 + (2 * t + 2))
                dve.wait_ge(y_done, i * 4 + 5)
                dve.wait_ge(g_done, i + 1)
                V.scalar_tensor_tensor(out=yb[:], in0=ust[:], scalar=K.vec[:, bass.ds(i + dcol, 1)],
                                       in1=y_ps[:, 0:T], op0=ALU.mult, op1=ALU.add).then_inc(yb_done, 1)
            st.loop(KT, 40, turn)


def lay_out_ssm(w):
    def states(v):
        v = np.asarray(v)
        return np.moveaxis(v.reshape((NST, P) + v.shape[2:]), 0, 1)
    ldt = np.broadcast_to(w["ssm_log_dt_2"][0][:, None], (64, 64))
    prm = np.stack([states(w["ssm_a_re_2"][0]), states(w["ssm_a_im_2"][0]), states(ldt)], 1)
    bc = np.stack([states(w["ssm_b_re_2"][0]), states(w["ssm_b_im_2"][0]),
                   states(w["ssm_c_re_2"][0].transpose(0, 2, 1)), states(w["ssm_c_im_2"][0].transpose(0, 2, 1))], 1)
    return {"ssm_prm": np.ascontiguousarray(prm), "ssm_bc": np.ascontiguousarray(bc), "ssm_win": _tiles(w["ssm_w_in_2"][0]),
            "ssm_wglu": _tiles(w["ssm_w_glu_2"][0]), "ssm_wout": _tiles(w["ssm_w_out_2"][0])}


class Consts:
    pass


def residual(K, gate):
    def step(st, i, bank, buf):
        xk = K.x[:, bass.ds(i, 1), :].squeeze(1)
        return K.nc.vector.scalar_tensor_tensor(out=xk, in0=bank, scalar=gate[:, bass.ds(i, 1)],
                                                    in1=xk, op0=ALU.mult, op1=ALU.add)
    return None, step, 0


def build(nc, d, out, upto=99):
    SPENT.clear()
    ctx = ExitStack()
    with ctx:
        K = Consts()
        K.nc = nc

        K.x = ctx.enter_context(nc.sbuf_tensor("x", [P, KT, T], F32))
        K.h = ctx.enter_context(nc.sbuf_tensor("h", [P, KT, T], F32))
        K.vec = ctx.enter_context(nc.sbuf_tensor("vec", [P, NVEC], F32))
        K.mod = ctx.enter_context(nc.sbuf_tensor("modv", [P, MOD_TILES + 16], F32))
        K.ops = ctx.enter_context(nc.sbuf_tensor("ops", [P, 4, 16], F32))
        K.gs_mix = ctx.enter_context(nc.sbuf_tensor("gs_mix", [P, KT], F32))
        K.gs_ctx = ctx.enter_context(nc.sbuf_tensor("gs_ctx", [P, KT], F32))
        K.gs_ffn = ctx.enter_context(nc.sbuf_tensor("gs_ffn", [P, KT], F32))
        K.ones = ctx.enter_context(nc.sbuf_tensor("ones", [P, P], F32))
        K.ident = ctx.enter_context(nc.sbuf_tensor("ident", [P, P], F32))
        K.lb = ctx.enter_context(nc.sbuf_tensor("lb", [P, 16], F32))
        K.oml = ctx.enter_context(nc.sbuf_tensor("oml", [P, 16], F32))

        with ExitStack() as mix:
            K.hc = mix.enter_context(nc.sbuf_tensor("hc", [P, KT, TC], F32))
            K.segf = mix.enter_context(nc.sbuf_tensor("segf", [P, T + TC], F32))
            K.segb = mix.enter_context(nc.sbuf_tensor("segb", [P, T + TC], F32))
            K.tri = mix.enter_context(nc.sbuf_tensor("tri", [CH, 2, CH], F32))
            K.triu = mix.enter_context(nc.sbuf_tensor("triu", [CH, 2, NCH, CH], U32))
            setup_and_modulation(nc, K, d)
            if upto >= 1:
                norm_phase(nc, K, "norm1", [(K.x, K.h, T, K.gs_mix, K.mod[:, 0:8]),
                                            (K.hc, K.hc, TC, K.gs_ctx, K.mod[:, MOD_TILES:MOD_TILES + 8])])
            y_hg = mix.enter_context(nc.sbuf_tensor("y_hg", [P, HG_H, T], F32))
            g0 = VEC["hgrn_norm_g"][0]
            if upto >= 2:
                heads_phase(nc, K, d, "hgrn", d["w_hg"], HG_H, 1, K.vec[:, g0:g0 + 1], y_hg, 1.0)
            y_gla = K.x
            if upto >= 3:
                with nc.sbuf_tensor("log_gates", [P, 2 * GLA_H, T + TC], F32) as lg:
                    lora_gates(nc, K, d, lg)
                    g1 = VEC["gla_norm_g"][0]
                    if upto >= 4:
                        heads_phase(nc, K, d, "gla", d["w_gla"], GLA_H, GLA_VT, K.vec[:, g1:g1 + 2], y_gla, 1.0 / 16.0, lg)
            if upto >= 5:
                with nc.sbuf_tensor("merged", [P, KT, T], F32) as merged:
                    merge_phase(nc, K, d, y_hg, y_gla, merged)
                    load_x(nc, K, d)
                    linear_phase(nc, K, "wo", lambda n: d["w_out"][n], merged, KT, residual(K, K.mod[:, 16:24]))
            dump = {1: K.h, 2: y_hg, 3: lg if upto == 3 else None, 4: y_gla}.get(upto, K.x)
            if 0 <= upto < 6:
                store_out(nc, dump, out)
                return
        if upto < 0:
            load_x(nc, K, d)
            [lambda: mla(nc, K, d), lambda: mlp(nc, K, d, 0), lambda: ssm(nc, K, d), lambda: mlp(nc, K, d, 1)][-upto - 7]()
        if upto >= 6:
            recycle(nc)
            norm_phase(nc, K, "norm2", [(K.x, K.h, T, K.gs_ffn, K.mod[:, 24:32])])
            peer(nc, K, d)
            f = VEC["final_g"][0]
            norm_phase(nc, K, "normf", [(K.x, K.x, T, K.vec[:, f:f + KT], None)])
        if upto >= 7:
            recycle(nc)
            mla(nc, K, d)
        if upto >= 8:
            mlp(nc, K, d, 0)
        if upto >= 9:
            recycle(nc)
            ssm(nc, K, d)
        if upto >= 10:
            mlp(nc, K, d, 1)
        store_out(nc, K.x, out)


def load_x(nc, K, d):
    with Phase(nc, "load_x") as ph:
        loaded = ph.sems("loaded")
        block = ph.block()

        @block.sync
        def _(sp):
            sp.dma_start(K.x[:], d["xT"].rearrange("(k p) t -> p k t", p=P)).then_inc(loaded, 16)
            sp.wait_ge(loaded, 16)


def store_out(nc, x, out):
    with Phase(nc, "out") as ph:
        stored = ph.sems("stored")
        block = ph.block()

        @block.sync
        def _(sp):
            sp.dma_start(out.rearrange("(k p) t -> p k t", p=P), x[:, 0:KT, 0:T]).then_inc(stored, 16)
            sp.wait_ge(stored, 16)


def _tiles(w):
    k, m = w.shape
    return np.ascontiguousarray(w.reshape(k // P, P, m // P, P).transpose(2, 1, 0, 3).reshape(m // P, P, k))


def _cols(v):
    return np.asarray(v).reshape(-1, P).T


def lay_out(inp):
    w = {k: np.asarray(v) for k, v in inp.items()}
    a = {}
    a["xT"] = np.ascontiguousarray(w["x"][0].T)
    a["ctxT"] = np.ascontiguousarray(w["ctx"][0].T)
    inv = (np.float32(10000.0) ** (-np.arange(0, 64, 2, dtype=np.float32) / np.float32(64))).astype(np.float32)
    order = {
        "mod_b": np.concatenate([_cols(w["ada_b"][0]), _cols(w["mod_mix_b_2"][0]), _cols(w["mod_ffn_b_2"][0]),
                                 _cols(w["mod_mix_b_2"][1]), _cols(w["mod_ffn_b_2"][1])], 1),
        "norm_mix_g": _cols(w["norm_mix_g"][0]), "lb_logits": _cols(w["hgrn_lb_logits"].reshape(-1)),
        "hgrn_norm_g": _cols(w["hgrn_norm_g"][0]), "gk_b": _cols(w["gla_gk_b"][0].reshape(-1)),
        "gla_norm_g": _cols(w["gla_norm_g"][0]), "norm_ffn_g": _cols(w["norm_ffn_g"][0]), "final_g": _cols(w["final_g"]),
        "q_norm": _cols(w["mla_q_norm_2"][0]), "kv_norm": _cols(w["mla_kv_norm_2"][0]), "ssm_d": _cols(w["ssm_d_2"][0]),
        "b_glu": _cols(w["ssm_b_glu_2"][0]), "mlp_b1": _cols(w["mlp_b1_2"].reshape(-1)), "mlp_b2": _cols(w["mlp_b2_2"].reshape(-1)),
        "ln_mix_g": _cols(w["ln_mix_g_2"].reshape(-1)), "ln_mix_b": _cols(w["ln_mix_b_2"].reshape(-1)),
        "ln_ffn_g": _cols(w["ln_ffn_g_2"].reshape(-1)), "ln_ffn_b": _cols(w["ln_ffn_b_2"].reshape(-1)),
        "inv_freq": np.tile(inv, 4).reshape(P, 1),
        "rope_sign": np.where(np.arange(P) % 64 < 32, -1.0, 1.0).astype(np.float32).reshape(P, 1),
    }
    a["vec"] = np.ascontiguousarray(np.concatenate([order[n] for n, _ in VEC_SIZES], 1))
    a["w_mod"] = np.concatenate([m.T for m in (w["ada_w"][0], w["mod_mix_w_2"][0], w["mod_ffn_w_2"][0],
                                               w["mod_mix_w_2"][1], w["mod_ffn_w_2"][1])]).reshape(MOD_TILES, P, D)
    a["c_rows"] = np.stack([w["c"][0], w["c_ctx"], w["c_2"][0]])
    wi = w["w_in"][0]
    at = np.cumsum([0, 1024, 1024, 1024, 1024, 1024, 512, 512, 1024, 1024, 16, 16, 1024, 1024])
    hq, ff, fb, hi, hg, gq, gk, gv, gg, _, _, mh, mg = [wi[:, at[i]:at[i + 1]] for i in range(13)]
    t = {n: _tiles(x) for n, x in dict(hq=hq, ff=ff, fb=fb, hi=hi, hg=hg, gq=gq, gk=gk, gv=gv, gg=gg, mh=mh, mg=mg).items()}
    a["w_hg"] = np.stack([t["ff"], t["fb"], t["hi"], t["hq"], t["hg"]], 1).reshape(-1, P, D)
    a["w_gla"] = np.stack([t["gk"], t["gv"][0::2], t["gv"][1::2], t["gq"], t["gg"][0::2], t["gg"][1::2]], 1).reshape(-1, P, D)
    a["w_gr"] = np.ascontiguousarray(wi[:, at[9]:at[11]])
    a["gk_w"] = w["gla_gk_w"][0]
    a["w_merge"] = np.stack([t["mh"], _tiles(w["w_branch_hgrn"][0]), t["mg"], _tiles(w["w_branch_gla"][0])], 1).reshape(-1, P, D)
    a["w_out"] = _tiles(w["w_out"][0])
    a.update(lay_out_peer(w))
    a.update(lay_out_mla(w))
    a.update(lay_out_rest(w))
    a.update(lay_out_ssm(w))
    return a


def kernel(**inputs):
    import concourse.bacc as _bacc
    from concourse.bass_utils import run_bass_kernel_spmd as _run

    nc = _bacc.Bacc("TRN2", target_bir_lowering=False, num_devices=1)
    arrays = lay_out(inputs)
    d = {n: nc.dram_tensor(f"in_{n}", a.shape, mybir.dt.from_np(a.dtype), kind="ExternalInput").ap() for n, a in arrays.items()}
    out = nc.dram_tensor("out_0", (D, T), F32, kind="ExternalOutput").ap()
    build(nc, d, out)
    r = _run(nc, [{f"in_{n}": a for n, a in arrays.items()}], core_ids=[0])
    return np.ascontiguousarray(r.results[0]["out_0"].T)[None]
```

```python
import concourse.bass as bass
from concourse import mybir
from contextlib import ExitStack
import math
import numpy as np

F32 = mybir.dt.float32
U32 = mybir.dt.uint32
I32 = mybir.dt.int32
F32R = mybir.dt.float32r
ALU = mybir.AluOpType
ACT = mybir.ActivationFunctionType
AXX = mybir.AxisListType.X

P = 128
T = 512
TC = 256
D = 1024
KT = D // P
CH = 64
NCH = T // CH
EPS = 1e-6
LN_EPS = 1e-5
ALPHA = 4 ** 0.25
HG_H, GLA_H = 8, 4
GLA_VT = 2
PEER_H, NKEY, TOPK = 8, 128, 16
TT = T // P
FF = 4096
ROUNDMAGIC = 12582912.0

VEC_SIZES = [
    ("mod_b", 144), ("norm_mix_g", 8), ("lb_logits", 32),
    ("hgrn_norm_g", 1), ("gk_b", 8), ("gla_norm_g", 2), ("norm_ffn_g", 8), ("final_g", 8),
    ("q_norm", 2), ("kv_norm", 1), ("ssm_d", 8), ("b_glu", 8), ("mlp_b1", 64), ("mlp_b2", 16),
    ("ln_mix_g", 16), ("ln_mix_b", 16), ("ln_ffn_g", 16), ("ln_ffn_b", 16), ("inv_freq", 1), ("rope_sign", 1),
]
VEC = {}
_at = 0
for _n, _k in VEC_SIZES:
    VEC[_n] = (_at, _k)
    _at += _k
NVEC = _at
MOD_TILES = 48 + 4 * 24


class Steps:

    def __init__(self, eng, sem):
        self.eng, self.sem, self.n, self.turn = eng, sem, 0, 0

    def do(self, ins):
        self.n += 1
        ins.then_inc(self.sem, 1)

    def sync(self, passed=None):
        self.eng.wait_ge(self.sem, self.turn + self.n)
        if passed is not None:
            self.eng.sem_inc(passed, 1)

    def then(self, ins):
        self.do(ins)
        self.sync()

    def loop(self, n, per, body):
        at = self.n
        with self.eng.Fori(0, n) as i:
            self.turn = i * per if per else 0
            body(i)
        assert self.n - at == per, (self.sem, self.n - at)
        self.n, self.turn = at + per * n, 0


SPENT = []


def recycle(nc):
    nc.all_engine_barrier()
    nc.clear_and_free_semaphores(list(SPENT))
    nc.all_engine_barrier()
    SPENT.clear()


class Phase:

    def __init__(self, nc, name):
        self.nc, self.name, self.ctx = nc, name, ExitStack()

    def __enter__(self):
        self.ctx.__enter__()
        return self

    def __exit__(self, *a):
        return self.ctx.__exit__(*a)

    def sb(self, name, shape, dt=F32):
        return self.ctx.enter_context(self.nc.sbuf_tensor(f"{self.name}_{name}", shape, dt))

    def banks(self, name, n=1):
        return self.ctx.enter_context(self.nc.psum_tensor(f"{self.name}_{name}", [P, n * 512], F32))

    def sems(self, *names):
        out = [self.nc.alloc_semaphore(f"{self.name}_{n}") for n in names]
        SPENT.extend(out)
        return out if len(out) > 1 else out[0]

    def block(self):
        return self.ctx.enter_context(self.nc.Block())


def stream(sp, slots, tiles, n, ready, used):
    r = len(slots)
    for s in range(min(r, n)):
        sp.dma_start(slots[s], tiles(s)).then_inc(ready[s], 16)
    if n > r:
        assert n % r == 0
        with sp.Fori(0, n // r - 1) as i:
            for s in range(r):
                sp.wait_ge(used, i * r + (s + 1))
                sp.dma_start(slots[s], tiles(i * r + (r + s))).then_inc(ready[s], 16)


class Modulation:

    def __init__(self, nc, K, ph, d, first, tiles, R, vecs):
        self.nc, self.K, self.d, self.first, self.tiles, self.vecs = nc, K, d, first, tiles, vecs
        V = len(vecs)
        self.ring = ph.sb("mod_ring", [P, R, D])
        self.rows = ph.sb("c_rows", [P, V, D])
        self.prod = ph.sb("mod_prod", [P, V, D])
        self.ready = ph.sems(*[f"mod_in{i}" for i in range(R)])
        self.rows_in, self.sig, self.silu, self.multiplied, self.summed, self.v = ph.sems(
            "c_rows_in", "c_sigmoid", "c_silu", "mod_multiplied", "mod_summed", "mod_biased")

    def load(self, eng):
        for n, (row, _) in enumerate(self.vecs):
            eng.dma_start(self.rows[:, n, :], self.d["c_rows"][row].partition_broadcast(P)).then_inc(self.rows_in, 16)
        stream(eng, [self.ring[:, s, :] for s in range(self.ring.shape[1])], lambda t: self.d["w_mod"][t + self.first],
               self.tiles, self.ready, self.multiplied)

    def start_act(self, act):
        V = len(self.vecs)
        act.sem_inc(self.summed, V)
        act.wait_ge(self.rows_in, 16 * V)
        self.nc.scalar.activation(self.prod[:], self.rows[:], ACT.Sigmoid).then_inc(self.sig, 1)

    def start_mul(self, eng, V_):
        eng.wait_ge(self.sig, 1)
        V_.tensor_tensor(self.rows[:], self.rows[:], self.prod[:], ALU.mult).then_inc(self.silu, 1)
        eng.wait_ge(self.silu, 1)

    def multiply(self, eng, V_, n, slot, at):
        V = len(self.vecs)
        eng.wait_ge(self.ready[slot], at + 16)
        for u in range(V):
            eng.wait_ge(self.summed, n * V + (u + 1))
            ins = V_.tensor_tensor(self.prod[:, u, :], self.ring[:, slot, :], self.rows[:, u, :], ALU.mult)
            ins.then_inc(self.multiplied if u == V - 1 else self.silu, 1)

    def sum(self, act, n):
        for u, (_, at) in enumerate(self.vecs):
            V = len(self.vecs)
            act.wait_ge(*((self.multiplied, n + 1) if u == V - 1 else (self.silu, n + 2)))
            self.nc.scalar.activation(self.prod[:, u, :], self.prod[:, u, :], ACT.Copy,
                                      accum_out=self.K.mod[:, bass.ds(n + at, 1)]).then_inc(self.summed, 1)

    def finish(self, eng, V_):
        V, n = len(self.vecs), self.tiles
        st = Steps(eng, self.v)
        b = VEC["mod_b"][0] + self.first
        eng.wait_ge(self.summed, V * (n + 1))
        for _, at in self.vecs:
            m = self.K.mod[:, at:at + n]
            st.do(V_.tensor_tensor(m, m, self.K.vec[:, b:b + n], ALU.add))
        st.sync()
        return st


def setup_and_modulation(nc, K, d):
    with Phase(nc, "mod") as ph:
        small = ph.sb("small", [P, 5, 16])
        M = Modulation(nc, K, ph, d, 0, 16, 8, [(0, 0), (1, MOD_TILES)])
        (vec_in, x_in, v, lb_in, lb_exp, g_step) = ph.sems(
            "vec_in", "x_in", "v", "lb_max", "lb_exp", "g_step")
        block = ph.block()

        @block.sync
        def _(sp):
            M.load(sp)

        @block.scalar
        def _(act):
            act.dma_start(K.vec[:], d["vec"]).then_inc(vec_in, 16)
            act.dma_start(K.x[:], d["xT"].rearrange("(k p) t -> p k t", p=P)).then_inc(x_in, 16)
            act.dma_start(K.hc[:], d["ctxT"].rearrange("(k p) t -> p k t", p=P)).then_inc(x_in, 16)
            M.start_act(act)
            act.wait_ge(lb_in, 1)
            nc.scalar.activation(small[:, 1:3, :], small[:, 1:3, :], ACT.Exp).then_inc(lb_exp, 1)
            for n in range(16):
                M.sum(act, n)
            act.wait_ge(x_in, 32)

        @block.gpsimd
        def _(g):
            st = Steps(g, g_step)
            st.do(nc.gpsimd.memset(K.ones[:], 1.0))
            st.do(nc.gpsimd.memset(K.ident[:], 0.0))
            st.do(nc.gpsimd.memset(K.segf[:], 1.0))
            st.do(nc.gpsimd.memset(K.segb[:], 1.0))
            st.do(nc.gpsimd.memset(K.tri[:], 1.0))
            st.sync()
            st.do(nc.gpsimd.affine_select(out=K.ident[:], in_=K.ident[:], compare_op=ALU.not_equal, fill=1.0,
                                          base=0, pattern=[[-1, P]], channel_multiplier=1))
            st.do(nc.gpsimd.memset(K.segf[:, 0:T:CH], 0.0))
            st.do(nc.gpsimd.memset(K.segf[:, T:T + 1], 0.0))
            st.do(nc.gpsimd.memset(K.segb[:, CH - 1:T:CH], 0.0))
            st.do(nc.gpsimd.memset(K.segb[:, T + TC - 1:T + TC], 0.0))
            st.do(nc.gpsimd.affine_select(out=K.tri[:, 0, :], in_=K.tri[:, 0, :], compare_op=ALU.is_ge, fill=0.0,
                                          base=0, pattern=[[1, CH]], channel_multiplier=-1))
            st.do(nc.gpsimd.affine_select(out=K.tri[:, 1, :], in_=K.tri[:, 1, :], compare_op=ALU.is_ge, fill=0.0,
                                          base=0, pattern=[[-1, CH]], channel_multiplier=1))
            st.sync()
            for c in range(NCH):
                last = nc.gpsimd.tensor_copy(K.triu[:, :, c, :], K.tri[:])
            st.then(last)

        @block.vector
        def _(dve):
            st = Steps(dve, v)
            dve.wait_ge(vec_in, 16)
            a = VEC["lb_logits"][0]
            l0, l1 = K.vec[:, a:a + 16], K.vec[:, a + 16:a + 32]
            st.then(nc.vector.tensor_tensor(small[:, 0, :], l0, l1, ALU.max))
            st.do(nc.vector.tensor_tensor(small[:, 1, :], l0, small[:, 0, :], ALU.subtract))
            nc.vector.tensor_tensor(small[:, 2, :], l1, small[:, 0, :], ALU.subtract).then_inc(lb_in, 1)
            dve.wait_ge(lb_exp, 1)
            st.then(nc.vector.tensor_tensor(small[:, 3, :], small[:, 1, :], small[:, 2, :], ALU.add))
            st.then(nc.vector.reciprocal(small[:, 4, :], small[:, 3, :]))
            st.then(nc.vector.tensor_tensor(K.lb[:], small[:, 1, :], small[:, 4, :], ALU.mult))
            st.then(nc.vector.tensor_scalar(K.oml[:], K.lb[:], -1.0, 1.0, ALU.mult, ALU.add))

            M.start_mul(dve, nc.vector)
            for n in range(16):
                M.multiply(dve, nc.vector, n, n % 8, n // 8 * 16)
            st = M.finish(dve, nc.vector)
            g0 = VEC["norm_mix_g"][0]
            for dst, at in ((K.gs_mix, 8), (K.gs_ctx, MOD_TILES + 8)):
                st.then(nc.vector.tensor_scalar(dst[:], K.mod[:, at:at + 8], 1.0, None, ALU.add))
                st.then(nc.vector.tensor_tensor(dst[:], dst[:], K.vec[:, g0:g0 + KT], ALU.mult))


def norm_phase(nc, K, name, jobs, center=False):
    with Phase(nc, name) as ph:
        sq = ph.sb("sq", [P, 2, T])
        rstd = ph.sb("rstd", [P, T])
        tmp = ph.sb("tmp", [P, 2, T])
        sums = ph.banks("sums", 2)[:].rearrange("p (s t) -> p s t", s=2)
        sq_ready, sums_done, rstd_ready, v, a, cent, mean_done, scaled, applied = ph.sems(
            "sq_ready", "sums_done", "rstd_ready", "v", "a", "centered", "mean_done", "scaled", "applied")
        block = ph.block()
        J = len(jobs)

        @block.tensor
        def _(pe):
            for j, (src, dst, n, mul, add) in enumerate(jobs):
                if center:
                    for k in range(KT):
                        last = nc.tensor.matmul(sums[:, 1, 0:n], K.ones[:], src[:, k, 0:n], start=k == 0, stop=k == KT - 1)
                    last.then_inc(mean_done, 1)
                if j:
                    pe.wait_ge(rstd_ready, j)
                for k in range(KT):
                    pe.wait_ge(sq_ready, j * KT + k + 1)
                    nc.tensor.matmul(sums[:, 0, 0:n], K.ones[:], sq[:, k % 2, 0:n], start=k == 0,
                                     stop=k == KT - 1).then_inc(sums_done, 1)

        @block.scalar
        def _(act):
            st = Steps(act, a)
            for j, (src, dst, n, mul, add) in enumerate(jobs):
                for k in range(KT):
                    if j * KT + k >= 2:
                        act.wait_ge(sums_done, j * KT + k - 1)
                    if center:
                        act.wait_ge(cent, j * KT + k + 1)
                    nc.scalar.activation(sq[:, k % 2, 0:n], (dst if center else src)[:, k, 0:n],
                                         ACT.Square).then_inc(sq_ready, 1)
                act.wait_ge(sums_done, (j + 1) * KT)
                if j:
                    act.wait_ge(cent, 100 * j)
                st.then(nc.scalar.activation(rstd[:, 0:n], sums[:, 0, 0:n], ACT.Ln, scale=1.0 / D,
                                             bias=LN_EPS if center else EPS))
                nc.scalar.activation(rstd[:, 0:n], rstd[:, 0:n], ACT.Exp, scale=-0.5).then_inc(rstd_ready, 1)
                if add is not None and j == J - 1:
                    for k in range(KT):
                        act.wait_ge(scaled, k + 1)
                        nc.scalar.activation(dst[:, k, 0:n], tmp[:, k % 2, 0:n], ACT.Identity, scale=mul[:, k:k + 1],
                                             bias=add[:, k:k + 1]).then_inc(applied, 1)
                    act.wait_ge(applied, KT)

        @block.vector
        def _(dve):
            st = Steps(dve, v)
            for j, (src, dst, n, mul, add) in enumerate(jobs):
                if center:
                    dve.wait_ge(mean_done, 1)
                    for k in range(KT):
                        nc.vector.scalar_tensor_tensor(out=dst[:, k, 0:n], in0=sums[:, 1, 0:n], scalar=-1.0 / D,
                                                       in1=src[:, k, 0:n], op0=ALU.mult, op1=ALU.add).then_inc(cent, 1)
                base = dst if center else src
                dve.wait_ge(rstd_ready, j + 1)
                for k in range(KT):
                    if add is None:
                        st.do(nc.vector.scalar_tensor_tensor(out=dst[:, k, 0:n], in0=base[:, k, 0:n], scalar=mul[:, k:k + 1],
                                                             in1=rstd[:, 0:n], op0=ALU.mult, op1=ALU.mult))
                    elif j < J - 1:
                        st.then(nc.vector.scalar_tensor_tensor(out=tmp[:, k % 2, 0:n], in0=base[:, k, 0:n], scalar=mul[:, k:k + 1],
                                                               in1=rstd[:, 0:n], op0=ALU.mult, op1=ALU.mult))
                        st.do(nc.vector.tensor_scalar(dst[:, k, 0:n], tmp[:, k % 2, 0:n], add[:, k:k + 1], None, ALU.add))
                    else:
                        if k >= 2:
                            dve.wait_ge(applied, k - 1)
                        nc.vector.tensor_tensor(tmp[:, k % 2, 0:n], base[:, k, 0:n], rstd[:, 0:n], ALU.mult).then_inc(scaled, 1)
                st.sync()
                if j < J - 1:
                    dve.sem_inc(cent, 100)


def heads_phase(nc, K, d, name, w_dram, heads, vt, gate_norm, y, scan_scale, log_gates=None):
    hg = log_gates is None
    NT = 5 if hg else 6
    with_ctx = 3
    QI = 3
    VI = 2 if hg else 1
    GI = 4
    START, AFTER_KEYS, AFTER_STATES = ((0,), ((1,), (3,)), ((2,), (4,))) if hg else ((0,), ((1, 2), (4,)), ((3,), (5,)))
    N = T + TC
    with Phase(nc, name) as ph:
        R = 5 if hg else 3
        if hg:
            ring4 = K.x[:].rearrange("p (r a) t -> p r (a t)", r=R - 1)
            ring = [ring4[:, s, :] for s in range(R - 1)] + [ph.sb("slot", [P, KT * P])[:]]
            hp = ph.sb("h_parts", [P, 2, KT, T], F32R)
            wp = ph.sb("w_parts", [P, 2, 2, KT * P], F32R)
        else:
            ring_sb = ph.sb("ring", [P, R, KT * P])
            ring = [ring_sb[:, s, :] for s in range(R)]
        proj_sb = ph.sb("proj", [P, 2, with_ctx * N + (NT - with_ctx) * T])
        sgate = ph.sb("sgate", [P, 2, vt, T])
        if hg:
            forget = ph.sb("forget", [P, 2, N])
            key2 = ph.sb("key2", [P, 2, N])
        cum = ph.sb("cum", [P, N])
        dif = ph.sb("dif", [P, T])
        dif2 = ph.sb("dif2", [P, N])
        e_q = ph.sb("e_q", [P, T])
        e_k = ph.sb("e_k", [P, T])
        e_kd = ph.sb("e_kd", [P, N])
        q_dec = ph.sb("q_dec", [P, 2, T])
        e_last = ph.sb("e_last", [P, 2, NCH])
        vtok = ph.sb("vtok", [CH, NCH, vt, P])
        vtok_c = ph.sb("vtok_c", [P, 2, vt, P])
        ktok = ph.sb("ktok", [CH, NCH, P])
        ktok_c = ph.sb("ktok_c", [P, 2, P])
        score = ph.sb("score", [CH, 2, T])
        state = ph.sb("state", [P, 2, NCH, vt, P])
        osq = ph.sb("osq", [P, T])
        rstd = dif if hg else ph.sb("rstd", [P, T])
        pg = ph.banks("proj_ps", 3)
        ptr = ph.banks("trans_ps", 2)
        psc = ph.banks("score_ps")
        pkv = ph.banks("kv_ps", 2)
        kv = pkv[:].rearrange("p (n v) -> p n v", n=NCH)
        o_ps = [psc, ptr[:, 0:T]]
        ready = ph.sems(*[f"w_ready{i}" for i in range(R)])
        (proj_done, proj_stored, sig_done, f_done, ln_done, dif_done, exp_done, prep_done, vtr_done,
         vtok_done, b_done, ktok_done, mask_done, kv_done, state_done, o_done, osq_done, sum_done,
         rstd_done, y_done, v, a, passed) = ph.sems(
            "proj_done", "proj_stored", "sig_done", "forget_done", "log_done", "dif_done", "exp_done",
            "prep_done", "vtrans_done", "vtok_done", "scores_done", "ktok_done", "mask_done", "kv_done",
            "state_done", "o_done", "osq_done", "sum_done", "rstd_done", "y_done", "v", "a", "passed")
        h_hi, h_lo, w_hi, w_lo, key_done = ph.sems("h_hi", "h_lo", "w_hi", "w_lo", "key_done")
        block = ph.block()

        def proj(par, j):
            at = j * N if j < with_ctx else with_ctx * N + (j - with_ctx) * T
            return proj_sb[:, par, at:at + (N if j < with_ctx else T)]

        def pgl(t):
            return pg[:, (t % 2) * T:(t % 2) * T + T]

        def pgc(t):
            return pg[:, 2 * T:2 * T + TC]

        @block.sync
        def _(sp):
            stream(sp, ring, lambda t: w_dram[t], heads * NT, ready, proj_done)

        @block.gpsimd
        def _(g):
            if hg:
                with g.Fori(0, heads // 2) as i:
                    for t in range(2 * NT):
                        g.wait_ge(w_hi, i * (2 * NT) + (t + 1))
                        nc.gpsimd.tensor_tensor(wp[:, t % 2, 1, :], ring[t % R], wp[:, t % 2, 0, :].bitcast(F32),
                                                ALU.subtract).then_inc(w_lo, 1)

        @block.tensor
        def _(pe):
            def project(h, par, j):
                t = par * NT + j
                s = t % R
                pe.wait_ge(ready[s], h // 2 * (16 * (2 * NT // R)) + 16 * (t // R + 1) if isinstance(h, int)
                           else (h - par) * (8 * (2 * NT // R)) + 16 * (t // R + 1))
                pe.wait_ge(proj_stored, h * NT + (j + 1))
                if hg:
                    pe.wait_ge(w_lo, h * NT + (j + 1))
                    wait = (lambda k: pe.wait_ge(h_lo, k + 1)) if isinstance(h, int) and h == 0 and j == 0 else None
                    last = parts_product(nc, pgl(t), lambda a, k: wp[:, t % 2, a, k * P:(k + 1) * P], lambda a, k: hp[:, a, k, :],
                                         range(KT), True, True, wait)
                else:
                    for k in range(KT):
                        last = nc.tensor.matmul(pgl(t), ring[s][:, k * P:(k + 1) * P], K.h[:, k, :], start=k == 0, stop=k == KT - 1)
                if j < with_ctx:
                    pe.wait_ge(proj_stored, h * NT + (j + 2))
                    for k in range(KT):
                        last = nc.tensor.matmul(pgc(t), ring[s][:, k * P:(k + 1) * P], K.hc[:, k, :], start=k == 0, stop=k == KT - 1)
                last.then_inc(proj_done, 1)

            def transposes(src, out, ctx_out):
                for n in range(NCH):
                    nc.tensor.transpose(out[0:CH, n * P:(n + 1) * P], src[:, n * CH:(n + 1) * CH], K.ident[:])
                for n in range(2):
                    last = nc.tensor.transpose(ctx_out[:, n * P:(n + 1) * P], src[:, T + n * P:T + (n + 1) * P], K.ident[:])
                return last

            def attend(h, par, nxt):
                def between(*js):
                    if nxt is not None:
                        for j in js:
                            project(nxt[0], nxt[1], j)

                between(*START)
                for u in range(vt):
                    pe.wait_ge(proj_stored, h * NT + NT + 2)
                    pe.wait_ge(y_done, h * vt + 1)
                    if u:
                        pe.wait_ge(vtok_done, h * vt + u)
                    pe.sem_inc(passed, 1)
                    transposes(proj(par, VI + u), ptr, pkv).then_inc(vtr_done, 1)
                for dr in range(2):
                    pe.wait_ge(vtok_done, h * vt + vt)
                    pe.wait_ge(prep_done, h * 2 + dr + 1)
                    if dr:
                        pe.wait_ge(ktok_done, h * 2 + 1)
                        pe.wait_ge(mask_done, h * 2 + 1)
                        pe.wait_ge(state_done, h * (2 * vt) + vt)
                    for n in range(NCH):
                        c = slice(n * CH, (n + 1) * CH)
                        nc.tensor.matmul(psc[0:CH, c], e_k[:, c], e_q[:, c], start=True, stop=True)
                    transposes(e_kd, ptr, pkv).then_inc(b_done, 1)
                    between(*AFTER_KEYS[dr])
                    pe.wait_ge(ktok_done, h * 2 + dr + 1)
                    for u in range(vt):
                        if u:
                            pe.wait_ge(state_done, h * (2 * vt) + dr * vt + u)
                        for n in range(NCH):
                            if n != (NCH - 1 if dr == 0 else 0):
                                nc.tensor.matmul(kv[:, n, :], ktok[:, n, :], vtok[:, n, u, :], start=True, stop=True)
                        s0 = NCH - 1 if dr == 0 else 0
                        for n in range(2):
                            last = nc.tensor.matmul(kv[:, s0, :], ktok_c[:, n, :], vtok_c[:, n, u, :], start=n == 0, stop=n == 1)
                        last.then_inc(kv_done, 1)
                    between(*AFTER_STATES[dr])
                pe.wait_ge(mask_done, h * 2 + 2)
                pe.wait_ge(state_done, h * (2 * vt) + 2 * vt)
                for u in range(vt):
                    for n in range(NCH):
                        c = slice(n * CH, (n + 1) * CH)
                        for dr in range(2):
                            nc.tensor.matmul(o_ps[u][:, c], vtok[:, n, u, :], score[:, dr, c], start=dr == 0, stop=False)
                            last = nc.tensor.matmul(o_ps[u][:, c], state[:, dr, n, u, :], q_dec[:, dr, c], start=False, stop=dr == 1)
                    last.then_inc(o_done, 1)
                for u in range(vt):
                    pe.wait_ge(osq_done, h * vt + u + 1)
                    last = nc.tensor.matmul(ptr[:, T:2 * T], K.ones[:], osq[:], start=u == 0, stop=u == vt - 1)
                    last.then_inc(sum_done, 1)

            for j in range(NT):
                project(0, 0, j)
            with pe.Fori(0, heads // 2 - 1) as i:
                attend(i * 2, 0, (i * 2 + 1, 1))
                attend(i * 2 + 1, 1, (i * 2 + 2, 0))
            attend(heads - 2, 0, (heads - 1, 1))
            attend(heads - 1, 1, None)

        @block.scalar
        def _(act):
            st = Steps(act, a)

            def store(h, par, j):
                t = par * NT + j
                act.wait_ge(proj_done, h * NT + j + 1)
                scale = P ** -0.5 if j == QI else 1.0
                if j < with_ctx:
                    nc.scalar.activation(proj(par, j)[:, T:N], pgc(t), ACT.Copy)
                nc.scalar.activation(proj(par, j)[:, 0:T], pgl(t), ACT.Copy, scale=scale).then_inc(proj_stored, 1)
                if hg and not (isinstance(h, int) and h == heads - 1 and j + 2 >= NT):
                    high(h, par, j + 2)

            def high(h, par, j):
                t = par * NT + j
                act.wait_ge(ready[t % R], (h - par) * (8 * 2 * NT // R) + 16 * (t // R + 1))
                nc.scalar.activation(wp[:, t % 2, 0, :], ring[t % R], ACT.Copy).then_inc(w_hi, 1)

            def exps(h, dr):
                act.wait_ge(dif_done, h * 6 + dr * 3 + 1)
                if dr:
                    act.wait_ge(b_done, h * 2 + 1)
                nc.scalar.activation(e_q[:], dif[:], ACT.Exp, scale=scan_scale)
                nc.scalar.activation(e_k[:], dif[:], ACT.Exp, scale=-scan_scale)
                nc.scalar.activation(q_dec[:, dr, :], cum[:, 0:T], ACT.Exp, scale=scan_scale)
                last = (slice(CH - 1, T, CH), slice(0, T, CH))[dr]
                nc.scalar.activation(e_last[:, dr, :], cum[:, last], ACT.Exp, scale=scan_scale)
                act.wait_ge(dif_done, h * 6 + dr * 3 + 3)
                nc.scalar.activation(e_kd[:], dif2[:], ACT.Exp, scale=scan_scale).then_inc(exp_done, 1)

            def attend(h, par, nxt):
                def between(*js):
                    if nxt is not None:
                        for j in js:
                            store(nxt[0], nxt[1], j)

                act.wait_ge(proj_stored, h * NT + NT + 2)
                for u in range(vt):
                    nc.scalar.activation(sgate[:, par, u, :], proj(par, GI + u), ACT.Sigmoid).then_inc(sig_done, 1)
                if hg:
                    for dr in range(2):
                        nc.scalar.activation(forget[:, dr, :], proj(par, dr), ACT.Sigmoid).then_inc(sig_done, 1)
                    for dr in range(2):
                        act.wait_ge(key_done, h * 2 + dr + 1)
                        nc.scalar.activation(forget[:, dr, :], forget[:, dr, :], ACT.Ln).then_inc(ln_done, 1)
                exps(h, 0)
                between(*START)
                for u in range(vt):
                    act.wait_ge(vtr_done, h * vt + u + 1)
                    nc.scalar.activation(vtok_c[:, :, u, :], pkv[:, 0:2 * P].rearrange("p (n v) -> p n v", n=2), ACT.Copy)
                    nc.scalar.activation(vtok[:, :, u, :], ptr[0:CH, :].rearrange("p (n v) -> p n v", n=NCH), ACT.Copy).then_inc(vtok_done, 1)
                for dr in range(2):
                    act.wait_ge(b_done, h * 2 + dr + 1)
                    nc.scalar.activation(ktok_c[:], pkv[:, 0:2 * P].rearrange("p (n v) -> p n v", n=2), ACT.Copy)
                    nc.scalar.activation(ktok[:], ptr[0:CH, :].rearrange("p (n v) -> p n v", n=NCH), ACT.Copy).then_inc(ktok_done, 1)
                    if dr == 0:
                        exps(h, 1)
                    between(*AFTER_KEYS[dr])
                    between(*AFTER_STATES[dr])
                for u in range(vt):
                    act.wait_ge(o_done, h * vt + u + 1)
                    if u:
                        act.wait_ge(sum_done, h * vt + u)
                    nc.scalar.activation(osq[:], o_ps[u][:, 0:T], ACT.Square).then_inc(osq_done, 1)
                act.wait_ge(sum_done, h * vt + vt)
                st.then(nc.scalar.activation(rstd[:], ptr[:, T:2 * T], ACT.Ln, scale=1.0 / (P * vt), bias=EPS))
                nc.scalar.activation(rstd[:], rstd[:], ACT.Exp, scale=-0.5).then_inc(rstd_done, 1)

            if hg:
                for k in range(KT):
                    nc.scalar.activation(hp[:, 0, k, :], K.h[:, k, :], ACT.Copy).then_inc(h_hi, 1)
                high(0, 0, 0)
                high(0, 0, 1)
            act.sem_inc(proj_stored, 2)
            for j in range(NT):
                store(0, 0, j)
            n0 = st.n
            with act.Fori(0, heads // 2 - 1) as i:
                st.turn = i * 2
                attend(i * 2, 0, (i * 2 + 1, 1))
                attend(i * 2 + 1, 1, (i * 2 + 2, 0))
            st.n, st.turn = n0 + 2 * (heads // 2 - 1), 0
            attend(heads - 2, 0, (heads - 1, 1))
            attend(heads - 1, 1, None)

        @block.vector
        def _(dve):
            st = Steps(dve, v)

            def differences(h, par, dr):
                seg = (K.segf, K.segb)[dr]
                lg = forget[:, dr, :] if hg else log_gates[:, bass.ds(h * 2 + dr, 1), :].squeeze(1)
                if hg:
                    dve.wait_ge(ln_done, h * 2 + dr + 1)
                if dr:
                    dve.wait_ge(exp_done, h * 2 + 1)
                if dr == 0:
                    st.then(nc.vector.tensor_tensor_scan(cum[:], seg[:], lg, 0.0, ALU.mult, ALU.add))
                else:
                    st.then(nc.vector.tensor_tensor_scan(cum[:, ::-1], seg[:, ::-1], lg[:, ::-1], 0.0, ALU.mult, ALU.add))
                ref = (CH // 2, CH // 2 - 1)[dr]
                end = (CH - 1, 0)[dr]
                cend = (N - 1, T)[dr]
                c3 = cum[:, 0:T].rearrange("p (n c) -> p n c", c=CH)
                nc.vector.tensor_tensor(dif[:].rearrange("p (n c) -> p n c", c=CH), c3,
                                        c3[:, :, ref:ref + 1].to_broadcast([P, NCH, CH]), ALU.subtract).then_inc(dif_done, 1)
                nc.vector.tensor_tensor(dif2[:, 0:T].rearrange("p (n c) -> p n c", c=CH),
                                        c3[:, :, end:end + 1].to_broadcast([P, NCH, CH]), c3, ALU.subtract).then_inc(dif_done, 1)
                nc.vector.tensor_scalar(dif2[:, T:N], cum[:, T:N], -1.0, cum[:, cend:cend + 1], ALU.mult, ALU.add).then_inc(dif_done, 1)

            def products(h, par, dr):
                dve.wait_ge(exp_done, h * 2 + dr + 1)
                key = key2[:, dr, :] if hg else proj(par, 0)
                q = proj(par, QI)
                nc.vector.tensor_tensor(e_q[:], e_q[:], q, ALU.mult)
                nc.vector.tensor_tensor(e_k[:], e_k[:], key[:, 0:T], ALU.mult)
                nc.vector.tensor_tensor(q_dec[:, dr, :], q_dec[:, dr, :], q, ALU.mult)
                nc.vector.tensor_tensor(e_kd[:], e_kd[:], key, ALU.mult).then_inc(prep_done, 1)

            def mask(h, dr):
                dve.wait_ge(b_done, h * 2 + dr + 1)
                dve.sem_inc(passed, 1)
                nc.vector.copy_predicated(score[:, dr, :], K.triu[:, dr, :, :].rearrange("p n c -> p (n c)"), psc[0:CH, :]).then_inc(mask_done, 1)

            def states(h, dr):
                order = list(range(NCH)) if dr == 0 else list(range(NCH))[::-1]
                for u in range(vt):
                    dve.wait_ge(kv_done, h * (2 * vt) + dr * vt + u + 1)
                    st.then(nc.vector.tensor_copy(state[:, dr, order[0], u, :], kv[:, order[-1], :]))
                    for a_, b_ in zip(order[:-1], order[1:]):
                        ins = nc.vector.scalar_tensor_tensor(
                            out=state[:, dr, b_, u, :], in0=state[:, dr, a_, u, :], scalar=e_last[:, dr, a_:a_ + 1],
                            in1=kv[:, a_, :], op0=ALU.mult, op1=ALU.add)
                        if b_ == order[-1]:
                            ins.then_inc(state_done, 1)
                        else:
                            st.then(ins)

            def attend(h, par):
                ns = vt + (2 if hg else 0)
                dve.wait_ge(proj_stored, h * NT + NT + 2)
                dve.wait_ge(sig_done, h * ns + vt)
                st.do(nc.vector.tensor_tensor(sgate[:, par], sgate[:, par], proj_sb[:, par, with_ctx * N + (GI - with_ctx) * T:with_ctx * N + (GI - with_ctx + vt) * T].rearrange("p (u t) -> p u t", u=vt), ALU.mult))
                if hg:
                    for dr in range(2):
                        dve.wait_ge(sig_done, h * ns + vt + dr + 1)
                        col = bass.ds(h + dr * HG_H, 1)
                        nc.vector.tensor_scalar(forget[:, dr, :], forget[:, dr, :], K.oml[:, col], K.lb[:, col],
                                                ALU.mult, ALU.add).then_inc(f_done, 1)
                        dve.wait_ge(f_done, h * 2 + dr + 1)
                        nc.vector.tensor_scalar(key2[:, dr, :], forget[:, dr, :], -1.0, 1.0, ALU.mult, ALU.add).then_inc(key_done, 1)
                differences(h, par, 0)
                products(h, par, 0)
                differences(h, par, 1)
                mask(h, 0)
                products(h, par, 1)
                states(h, 0)
                mask(h, 1)
                states(h, 1)
                dve.wait_ge(rstd_done, h + 1)
                for u in range(vt):
                    yo = y[:, bass.ds(h * vt + u, 1), :].squeeze(1)
                    st.then(nc.vector.scalar_tensor_tensor(out=osq[:] if u == 0 else dif[:], in0=o_ps[u][:, 0:T], scalar=gate_norm[:, u:u + 1],
                                                           in1=rstd[:], op0=ALU.mult, op1=ALU.mult))
                    nc.vector.tensor_tensor(yo, osq[:] if u == 0 else dif[:], sgate[:, par, u, :], ALU.mult).then_inc(y_done, 1)

            dve.sem_inc(y_done, 1)
            if hg:
                for k in range(KT):
                    dve.wait_ge(h_hi, k + 1)
                    nc.vector.tensor_tensor(hp[:, 1, k, :], K.h[:, k, :], hp[:, 0, k, :].bitcast(F32), ALU.subtract).then_inc(h_lo, 1)
            st.then(nc.vector.memset(score[:], 0.0))
            per = 1 + 2 + 2 * vt * (NCH - 1) + vt
            n0 = st.n
            with dve.Fori(0, heads // 2 - 1) as i:
                st.turn = i * (2 * per)
                attend(i * 2, 0)
                attend(i * 2 + 1, 1)
            assert st.n - n0 == 2 * per, (st.n - n0, per)
            st.n, st.turn = n0 + 2 * per * (heads // 2 - 1), 0
            attend(heads - 2, 0)
            attend(heads - 1, 1)


def lora_gates(nc, K, d, log_gates):
    N = T + TC
    with Phase(nc, "lora") as ph:
        w = ph.sb("w", [P, KT, 32])
        gw = ph.sb("gw", [16, 2, T])
        gr = ph.sb("gr", [16, 2, N])
        az = ph.sb("az", [P, N])
        mz = ph.sb("mz", [P, N])
        g_ps = ph.banks("g", 2)
        z_ps = ph.banks("z", 4)
        w_in, gr_done, gr_stored, z_done, abs_done, m_done, l_done, out_done, a = ph.sems(
            "w_in", "gr_done", "gr_stored", "z_done", "abs_done", "min_done", "log_done", "out_done", "a")
        block = ph.block()
        pairs = [(h, dr) for h in range(GLA_H) for dr in range(2)]
        gb = VEC["gk_b"][0]

        @block.sync
        def _(sp):
            sp.dma_start(w[:], d["w_gr"].rearrange("(k p) m -> p k m", p=P)).then_inc(w_in, 16)
            sp.dma_start(gw[:], d["gk_w"].rearrange("d r m -> r d m")).then_inc(w_in, 16)

        @block.tensor
        def _(pe):
            pe.wait_ge(w_in, 32)
            for dr in range(2):
                if dr:
                    pe.wait_ge(gr_stored, 1)
                for j, (src, n) in enumerate(((K.h, T), (K.hc, TC))):
                    for k in range(KT):
                        last = nc.tensor.matmul(g_ps[0:16, j * T:j * T + n], w[:, k, 16 * dr:16 * dr + 16], src[:, k, :],
                                                start=k == 0, stop=k == KT - 1)
                last.then_inc(gr_done, 1)
            pe.wait_ge(gr_stored, 2)
            for i, (h, dr) in enumerate(pairs):
                b = 2 * (i % 2) * T
                if i >= 2:
                    pe.wait_ge(m_done, i - 1)
                nc.tensor.matmul(z_ps[:, b:b + T], gw[:, dr, h * P:(h + 1) * P], gr[:, dr, 0:T], start=True, stop=True)
                nc.tensor.matmul(z_ps[:, b + T:b + N], gw[:, dr, h * P:(h + 1) * P], gr[:, dr, T:N], start=True,
                                 stop=True).then_inc(z_done, 1)

        @block.scalar
        def _(act):
            st = Steps(act, a)
            for i, (h, dr) in enumerate(pairs):
                b = 2 * (i % 2) * T
                act.wait_ge(z_done, i + 1)
                bias = K.vec[:, gb + dr * GLA_H + h:gb + dr * GLA_H + h + 1]
                if i:
                    act.wait_ge(out_done, i)
                nc.scalar.activation(az[:], z_ps[:, b:b + N], ACT.Abs, bias=bias).then_inc(abs_done, 1)
                act.wait_ge(abs_done, i + 1)
                st.then(nc.scalar.activation(az[:], az[:], ACT.Exp, scale=-1.0))
                nc.scalar.activation(az[:], az[:], ACT.Ln, bias=1.0).then_inc(l_done, 1)

        @block.vector
        def _(dve):
            for dr in range(2):
                dve.wait_ge(gr_done, dr + 1)
                nc.vector.tensor_copy(gr[:, dr, :], g_ps[0:16, 0:N]).then_inc(gr_stored, 1)
            for i, (h, dr) in enumerate(pairs):
                b = 2 * (i % 2) * T
                dve.wait_ge(abs_done, i + 1)
                bias = K.vec[:, gb + dr * GLA_H + h:gb + dr * GLA_H + h + 1]
                nc.vector.tensor_scalar(mz[:], z_ps[:, b:b + N], bias, 0.0, ALU.add, ALU.min).then_inc(m_done, 1)
                dve.wait_ge(m_done, i + 1)
                dve.wait_ge(l_done, i + 1)
                nc.vector.tensor_tensor(log_gates[:, h * 2 + dr, :], mz[:], az[:], ALU.subtract).then_inc(out_done, 1)


def merge_phase(nc, K, d, name, half, y, hp, yp, merged):
    with Phase(nc, name) as ph:
        R = 4
        raw = ph.sb("raw", [P, R, KT * P])
        wp = ph.sb("w_parts", [P, 2, 2, KT * P], F32R)
        sg = ph.sb("sg", [P, 2, T])
        ps = ph.banks("ps", 4)
        first = 16 + 16 * half
        M = Modulation(nc, K, ph, d, first, 16, 4, [(0, first)])
        ready = ph.sems(*[f"w_ready{i}" for i in range(R)])
        x_in = ph.sems("x_in")
        s_hi, s_lo, w_hi, w_lo, used, sig, out, v = ph.sems(
            "src_hi", "src_lo", "w_hi", "w_lo", "chunk_used", "sig_done", "out_done", "v")
        block = ph.block()
        sources = ([] if half else [(K.h, hp)]) + [(y, yp)]
        turns = 2 * KT // R

        @block.sync
        def _(sp):
            stream(sp, [raw[:, s, :] for s in range(R)], lambda t: d["w_merge"][half, t], 2 * KT, ready, w_lo)
            if half:
                sp.wait_ge(s_lo, KT)
                sp.dma_start(K.x[:], d["xT"].rearrange("(k p) t -> p k t", p=P)).then_inc(x_in, 16)
                K.slots.load_first(sp, lambda n: d["w_out"][n])
                sp.wait_ge(x_in, 16)

        @block.gpsimd
        def _(g):
            g.dma_start(M.rows[:, 0, :], d["c_rows"][0].partition_broadcast(P)).then_inc(M.rows_in, 16)
            for s in range(4):
                g.dma_start(M.ring[:, s, :], d["w_mod"][first + s]).then_inc(M.ready[s], 16)
            M.start_mul(g, nc.gpsimd)

            def turn(i, last):
                for s in range(4):
                    M.multiply(g, nc.gpsimd, i * 4 + s, s, i * 16)
                    if not last:
                        g.wait_ge(M.multiplied, i * 4 + (s + 1))
                        g.dma_start(M.ring[:, s, :], d["w_mod"][i * 4 + (s + first + 4)]).then_inc(M.ready[s], 16)

            with g.Fori(0, turns - 1) as i:
                turn(i, False)
            turn(turns - 1, True)
            st = M.finish(g, nc.gpsimd)
            if half:
                g1 = VEC["norm_ffn_g"][0]
                st.then(nc.gpsimd.tensor_tensor(K.gs_ffn[:], K.mod[:, 32:40], K.vec[:, g1:g1 + KT], ALU.mult))
                st.then(nc.gpsimd.tensor_tensor(K.gs_ffn[:], K.gs_ffn[:], K.vec[:, g1:g1 + KT], ALU.add))

        @block.tensor
        def _(pe):
            pe.sem_inc(used, 2)

            with pe.Fori(0, turns) as i:
                for s in range(R):
                    pe.wait_ge(w_lo, i * R + (s + 1))
                    pe.wait_ge(out, i * 2 + (s // 2 + 1))
                    at = 0 if half or s == 0 else KT
                    wait = (lambda k: pe.wait_ge(s_lo, at + k + 1)) if s == 1 or not half and s == 0 else None
                    src = yp if s % 2 else hp
                    parts_product(nc, ps[:, s * T:(s + 1) * T], lambda a, k: wp[:, s % 2, a, k * P:(k + 1) * P],
                                  lambda a, k: src[:, a, k, :], range(KT), True, True, wait).then_inc(used, 1)

        @block.scalar
        def _(act):
            def high(i, s):
                act.wait_ge(ready[s % R], i * 16 + 16 * (s // R + 1))
                act.wait_ge(used, i * R + (s + 1))
                nc.scalar.activation(wp[:, s % 2, 0, :], raw[:, s % R, :], ACT.Copy).then_inc(w_hi, 1)

            def turn(i, last):
                for s in range(R):
                    if not (last and s == R - 1):
                        high(i, s + 1)
                    if s % 2 == 0:
                        act.wait_ge(used, i * R + (s + 3))
                        act.wait_ge(out, i * 2 + (s // 2 + 1))
                        nc.scalar.activation(sg[:, s // 2, :], ps[:, s * T:(s + 1) * T], ACT.Sigmoid).then_inc(sig, 1)
                    M.sum(act, i * 4 + s)

            n = 0
            for src, dst in sources:
                for k in range(KT):
                    nc.scalar.activation(dst[:, 0, k, :], src[:, k, :], ACT.Copy).then_inc(s_hi, 1)
                if n == 0:
                    high(0, 0)
                n += KT
            M.start_act(act)
            with act.Fori(0, turns - 1) as i:
                turn(i, False)
            turn(turns - 1, True)

        @block.vector
        def _(dve):
            def low(i, s):
                dve.wait_ge(w_hi, i * R + (s + 1))
                nc.vector.tensor_tensor(wp[:, s % 2, 1, :], raw[:, s % R, :], wp[:, s % 2, 0, :].bitcast(F32), ALU.subtract).then_inc(w_lo, 1)

            def turn(i, last):
                for s in range(R):
                    if not (last and s == R - 1):
                        low(i, s + 1)
                    if s % 2:
                        b = s // 2
                        mt = merged[:, bass.ds(i * 2 + b, 1), :].squeeze(1)
                        dve.wait_ge(sig, i * 2 + (b + 1))
                        dve.wait_ge(used, i * R + (s + 3))
                        if half == 0:
                            nc.vector.tensor_tensor(mt, sg[:, b, :], ps[:, s * T:(s + 1) * T], ALU.mult).then_inc(out, 1)
                        else:
                            nc.vector.tensor_tensor(sg[:, b, :], sg[:, b, :], ps[:, s * T:(s + 1) * T], ALU.mult).then_inc(v, 1)
                            dve.wait_ge(v, i * 2 + (b + 1))
                            nc.vector.tensor_tensor(mt, mt, sg[:, b, :], ALU.add).then_inc(out, 1)

            dve.sem_inc(out, 2)
            n = 0
            for src, dst in sources:
                for k in range(KT):
                    dve.wait_ge(s_hi, n + 1)
                    n += 1
                    nc.vector.tensor_tensor(dst[:, 1, k, :], src[:, k, :], dst[:, 0, k, :].bitcast(F32), ALU.subtract).then_inc(s_lo, 1)
                if n == KT:
                    low(0, 0)
            with dve.Fori(0, turns - 1) as i:
                turn(i, False)
            turn(turns - 1, True)
            dve.wait_ge(out, KT + 2)
    K.slots.ahead = bool(half)


def parts_product(nc, out, w, x, ks, start, stop, wait=None):
    for k in ks:
        if wait is not None:
            wait(k)
        for n, (a, b) in enumerate(((0, 0), (0, 1), (1, 0))):
            last = nc.tensor.matmul(out, w(a, k), x(b, k), start=start and k == ks[0] and n == 0,
                                    stop=stop and k == ks[-1] and n == 2)
    return last


class WeightSlots:
    R = 4

    def __init__(self, nc, stack, name):
        self.raw = stack.enter_context(nc.sbuf_tensor(name, [P, self.R, KT * P], F32))
        self.ready = [nc.alloc_semaphore(f"{name}_ready{i}") for i in range(self.R)]
        self.loaded = 0
        self.ahead = False

    def load_first(self, sp, w):
        for s in range(self.R):
            sp.dma_start(self.raw[:, s, :], w(s)).then_inc(self.ready[s], 16)


def load_ahead(nc, K, name, w):
    with Phase(nc, name) as ph:
        block = ph.block()

        @block.sync
        def _(sp):
            K.slots.load_first(sp, w)
    K.slots.ahead = True


def linear_phase(nc, K, name, w, src, tiles, finish, chunks=1, parts=None, then=None):
    with Phase(nc, name) as ph:
        B, R = 4, WeightSlots.R
        S = B * chunks
        turns = tiles // B
        raw, ready = K.slots.raw, K.slots.ready
        base = 16 * (K.slots.loaded // R)
        n = tiles * chunks
        ahead = K.slots.ahead
        wp = ph.sb("w_parts", [P, 2, 2, KT * P], F32R)
        ps = ph.banks("ps", B)
        bufs = ph.sb("buf", [P, B, T])
        if parts is None:
            parts = ph.sb("src_parts", [P, 2, KT, T], F32R)
        w_hi, w_lo, used, src_hi, src_lo, mid, out, v = ph.sems(
            "w_hi", "w_lo", "chunk_used", "src_hi", "src_lo", "act_done", "out_done", "v")
        block = ph.block()
        act_step, dve_step, per = finish

        @block.sync
        def _(sp):
            if not ahead:
                K.slots.load_first(sp, w)
            with sp.Fori(0, n // R - 1) as i:
                for s in range(R):
                    sp.wait_ge(w_lo, i * R + (s + 1))
                    sp.dma_start(raw[:, s, :], w(i * R + (s + R))).then_inc(ready[s], 16)
            if then is not None:
                sp.wait_ge(w_lo, n)
                K.slots.load_first(sp, then)

        @block.tensor
        def _(pe):
            pe.sem_inc(used, 2)

            def src_wait(k):
                pe.wait_ge(src_lo, k + 1)

            with pe.Fori(0, turns) as i:
                for s in range(S):
                    b, c = s // chunks, s % chunks
                    pe.wait_ge(w_lo, i * S + (s + 1))
                    if c == 0:
                        pe.wait_ge(out, i * B + (b + 1))
                    parts_product(nc, ps[:, b * T:(b + 1) * T], lambda a, k: wp[:, s % 2, a, k * P:(k + 1) * P],
                                  lambda a, k: parts[:, a, c * KT + k, :], range(KT), c == 0, c == chunks - 1,
                                  src_wait if src is not None and s == 0 else None).then_inc(used, 1)

        def turns_of(st, per, body):
            if turns > 1:
                st.loop(turns - 1, per, lambda i: body(i, False))
            body(turns - 1, True)

        @block.scalar
        def _(act):
            if dve_step is None:
                act.sem_inc(out, B)

            def high(i, s):
                act.wait_ge(ready[s % R], i * (16 * S // R) + (base + 16 * (s // R + 1)))
                act.wait_ge(used, i * S + (s + 1))
                nc.scalar.activation(wp[:, s % 2, 0, :], raw[:, s % R, :], ACT.Copy).then_inc(w_hi, 1)

            def turn(i, last):
                for s in range(S):
                    if not (last and s == S - 1):
                        high(i, s + 1)
                    if act_step is not None and s % chunks == chunks - 1:
                        b = s // chunks
                        act.wait_ge(used, i * S + (s + 3))
                        act.wait_ge(out, i * B + (b + 1))
                        act_step(i * B + b, ps[:, b * T:(b + 1) * T], bufs[:, b, :]).then_inc(mid if dve_step else out, 1)

            if ahead:
                high(0, 0)
            if src is not None:
                for k in range(KT):
                    nc.scalar.activation(parts[:, 0, k, :], src[:, k, :], ACT.Copy).then_inc(src_hi, 1)
            if not ahead:
                high(0, 0)
            turns_of(Steps(act, v), 0, turn)

        @block.vector
        def _(dve):
            if dve_step is not None:
                dve.sem_inc(out, B)
            st = Steps(dve, v)

            def low(i, s):
                dve.wait_ge(w_hi, i * S + (s + 1))
                nc.vector.tensor_tensor(wp[:, s % 2, 1, :], raw[:, s % R, :], wp[:, s % 2, 0, :].bitcast(F32), ALU.subtract).then_inc(w_lo, 1)

            def turn(i, last):
                for s in range(S):
                    if not (last and s == S - 1):
                        low(i, s + 1)
                    if dve_step is not None and s % chunks == chunks - 1:
                        b = s // chunks
                        if act_step is not None:
                            dve.wait_ge(mid, i * B + (b + 1))
                        else:
                            dve.wait_ge(used, i * S + (s + 3))
                        dve_step(st, i * B + b, ps[:, b * T:(b + 1) * T], bufs[:, b, :]).then_inc(out, 1)

            if ahead:
                low(0, 0)
            if src is not None:
                for k in range(KT):
                    dve.wait_ge(src_hi, k + 1)
                    nc.vector.tensor_tensor(parts[:, 1, k, :], src[:, k, :], parts[:, 0, k, :].bitcast(F32), ALU.subtract).then_inc(src_lo, 1)
            if not ahead:
                low(0, 0)
            turns_of(st, per * B, turn)
            if dve_step is not None:
                dve.wait_ge(out, tiles + B)
    K.slots.loaded += n
    K.slots.ahead = then is not None


def peer_route(nc, K, d, sel):
    NK = TOPK
    with Phase(nc, "route") as ph:
        R = 4
        ring = ph.sb("ring", [P, R, KT * P])
        keys = ph.sb("keys", [P, 2, NKEY])
        q_sb = ph.sb("q", [P, 2, T])
        rest = ph.sb("rest", [P, TT, 2 * P])
        val = ph.sb("val", [P, 2, TT, NK])
        idx = ph.sb("idx", [P, 2, TT, NK], U32)
        idxf = ph.sb("idxf", [P, 2, TT, NK])
        cand = ph.sb("cand", [P, TT, NK, NK])
        top = ph.sb("top", [P, TT, NK])
        topi = ph.sb("topi", [P, TT, NK], U32)
        rc_u = ph.sb("rc_u", [P, 2, TT, NK], U32)
        rc = ph.sb("rc", [P, 2, TT, NK])
        pick = ph.sb("pick", [P, TT, NK, NK])
        iota16 = ph.sb("iota16", [P, NK])
        expd = ph.sb("expd", [P, TT, NK])
        total = ph.sb("total", [P, 2, TT])
        q_ps = ph.banks("q_ps", 2)
        s_ps = ph.banks("s_ps", 2)
        ready = ph.sems(*[f"w_ready{i}" for i in range(R)])
        keys_in, proj_done, q_stored, s_done, s_read, cst, logit_done, exp_done, v, passed = ph.sems(
            "keys_in", "proj_done", "q_stored", "scores_done", "scores_read", "consts", "logit_done", "exp_done", "v", "passed")
        block = ph.block()
        tiles = 2 * PEER_H

        @block.sync
        def _(sp):
            sp.dma_start(keys[:], d["peer_keys"]).then_inc(keys_in, 16)
            stream(sp, [ring[:, s, :] for s in range(R)], lambda t: d["peer_wq"][t], tiles, ready, proj_done)

        @block.gpsimd
        def _(g):
            nc.gpsimd.iota(iota16[:], [[1, NK]], base=0, channel_multiplier=0,
                           allow_small_or_imprecise_dtypes=True).then_inc(cst, 1)

        @block.tensor
        def _(pe):
            pe.wait_ge(keys_in, 16)
            pe.sem_inc(s_done, 1)

            def project(i, s):
                pe.wait_ge(ready[s], i * 16 + 16)
                pe.wait_ge(q_stored, i * R + s + 1)
                for k in range(KT):
                    last = nc.tensor.matmul(q_ps[:, (s % 2) * T:(s % 2) * T + T], ring[:, s, k * P:(k + 1) * P], K.h[:, k, :],
                                            start=k == 0, stop=k == KT - 1)
                last.then_inc(proj_done, 1)

            def scores(i, s):
                pe.wait_ge(q_stored, i * R + s + 3)
                pe.wait_ge(s_read, i * R + s + 1)
                for t in range(TT):
                    last = nc.tensor.matmul(s_ps[:, (s % 2) * T + t * P:(s % 2) * T + (t + 1) * P],
                                            q_sb[:, s % 2, t * P:(t + 1) * P], keys[:, s % 2, :], start=True, stop=True)
                last.then_inc(s_done, 1)

            with pe.Fori(0, tiles // R) as i:
                project(i, 0)
                for s in range(1, R):
                    project(i, s)
                    scores(i, s - 1)
                scores(i, R - 1)

        @block.scalar
        def _(act):
            act.sem_inc(q_stored, 2)
            with act.Fori(0, tiles // R) as i:
                for s in range(R):
                    act.wait_ge(proj_done, i * R + s + 1)
                    act.wait_ge(s_done, i * R + (s + 1))
                    nc.scalar.activation(q_sb[:, s % 2, :], q_ps[:, (s % 2) * T:(s % 2) * T + T], ACT.Copy).then_inc(q_stored, 1)
                    if s % 2 and s > 1:
                        act.wait_ge(logit_done, i * 2 + 1)
                        nc.scalar.activation(expd[:], expd[:], ACT.Exp).then_inc(exp_done, 1)
                act.wait_ge(logit_done, i * 2 + 2)
                nc.scalar.activation(expd[:], expd[:], ACT.Exp).then_inc(exp_done, 1)

        @block.vector
        def _(dve):
            V = nc.vector
            dve.sem_inc(s_read, 2)
            dve.wait_ge(cst, 1)
            st = Steps(dve, v)

            def top16(src, values, indices, n):
                for t in range(TT):
                    st.do(V.max(values[:, t, 0:8], src(t)))
                st.sync(passed)
                for t in range(TT):
                    st.do(V.max_index(indices[:, t, 0:8], values[:, t, 0:8], src(t)))
                    st.do(V.match_replace(rest[:, t, 0:n], values[:, t, 0:8], src(t), -3.0e38))
                st.sync(passed)
                for t in range(TT):
                    st.do(V.max(values[:, t, 8:16], rest[:, t, 0:n]))
                st.sync(passed)
                for t in range(TT):
                    st.do(V.max_index(indices[:, t, 8:16], values[:, t, 8:16], rest[:, t, 0:n]))
                st.sync()

            def head(i, par):
                for s in range(2):
                    dve.wait_ge(s_done, i * R + (par * 2 + s + 2))
                    dve.sem_inc(passed, 1)
                    top16(lambda t: s_ps[:, s * T + t * P:s * T + (t + 1) * P], val[:, s], idx[:, s], P)
                    V.tensor_copy(idxf[:, s], idx[:, s]).then_inc(s_read, 1)
                st.then(V.tensor_tensor(cand[:], val[:, 0].unsqueeze(3).to_broadcast([P, TT, NK, NK]),
                                        val[:, 1].unsqueeze(2).to_broadcast([P, TT, NK, NK]), ALU.add))
                dve.sem_inc(passed, 1)
                top16(lambda t: cand[:, t].rearrange("p a b -> p (a b)"), top, topi, NK * NK)
                V.tensor_tensor(expd[:], top[:], top[:, :, 0:1].to_broadcast([P, TT, NK]), ALU.subtract).then_inc(logit_done, 1)
                st.do(V.tensor_scalar(rc_u[:, 0], topi[:], 4, None, ALU.logical_shift_right))
                st.then(V.tensor_scalar(rc_u[:, 1], topi[:], 15, None, ALU.bitwise_and))
                st.then(V.tensor_copy(rc[:], rc_u[:]))
                cols = slice(None)
                for s in range(2):
                    st.then(V.tensor_tensor(pick[:], rc[:, s].unsqueeze(3).to_broadcast([P, TT, NK, NK]),
                                            iota16[:].unsqueeze(1).unsqueeze(1).to_broadcast([P, TT, NK, NK]), ALU.is_equal))
                    st.then(V.tensor_tensor(pick[:], pick[:], idxf[:, s].unsqueeze(2).to_broadcast([P, TT, NK, NK]), ALU.mult))
                    st.then(V.tensor_reduce(sel[:, s, :, bass.ds(i * (2 * NK) + par * NK, NK)], pick[:], AXX, ALU.add))
                dve.wait_ge(exp_done, i * 2 + par + 1)
                st.then(V.tensor_reduce(total[:, 0, :], expd[:], AXX, ALU.add))
                st.then(V.reciprocal(total[:, 1, :], total[:, 0, :]))
                st.then(V.tensor_tensor(sel[:, 2, :, bass.ds(i * (2 * NK) + par * NK, NK)], expd[:],
                                        total[:, 1, :].unsqueeze(2).to_broadcast([P, TT, NK]), ALU.mult))

            per = 2 * (3 * 5 * TT + 1 + 3 + 6 + 3)

            def pair(i):
                head(i, 0)
                head(i, 1)
            st.loop(PEER_H // 2, per, pair)

def peer_gates(nc, K, d, sel, gates):
    G = 8
    GP = 4
    with Phase(nc, "gates") as ph:
        selt = ph.sb("selt", [P, 3, T])
        iota = ph.sb("iota", [P, NKEY])
        rows = ph.sb("rows", [P, 2, G, NKEY])
        cols = ph.sb("cols", [P, 2, G, NKEY])
        slab = ph.sb("slab", [P, 2, NKEY, P])
        t_ps = ph.banks("t_ps", 3)
        g_ps = ph.banks("g_ps", 4)
        cst, tr_done, tr_stored, rows_dist, rows_near, rows_done, cols_done, g_done, g_stored, passed = ph.sems(
            "consts", "trans_done", "trans_stored", "rows_dist", "rows_by_pool", "rows_by_dve", "cols_done", "g_done", "g_stored",
            "passed")
        slab_out = ph.sems("slab_out0", "slab_out1")
        block = ph.block()
        groups = P // G

        @block.gpsimd
        def _(g):
            nc.gpsimd.iota(iota[:], [[1, NKEY]], base=0, channel_multiplier=0,
                           allow_small_or_imprecise_dtypes=True).then_inc(cst, 1)
            g.wait_ge(cst, 1)
            g.wait_ge(tr_stored, 3)
            with g.Fori(0, T // (2 * G)) as i:
                for b in range(2):
                    g.wait_ge(g_done, i * 2 + b + 1)
                    nc.gpsimd.tensor_tensor(rows[:, b, 0:GP], iota[:].unsqueeze(1).to_broadcast([P, GP, NKEY]),
                                            selt[:, 0, bass.ds(i * (2 * G) + b * G, GP)].unsqueeze(2).to_broadcast([P, GP, NKEY]),
                                            ALU.subtract).then_inc(rows_dist, 1)
                    g.wait_ge(rows_dist, i * 2 + b + 1)
                    g.sem_inc(passed, 1)
                    nc.gpsimd.tensor_scalar(rows[:, b, 0:GP], rows[:, b, 0:GP], 0.0, None, ALU.is_equal).then_inc(rows_near, 1)

        @block.vector
        def _(dve):
            for w in range(3):
                dve.wait_ge(tr_done, w + 1)
                nc.vector.tensor_copy(selt[:, w, :], t_ps[:, w * T:(w + 1) * T]).then_inc(tr_stored, 1)
            dve.wait_ge(cst, 1)
            dve.wait_ge(tr_stored, 3)

            with dve.Fori(0, T // (2 * G)) as i:
                for b in range(2):
                    dve.wait_ge(g_done, i * 2 + b + 1)
                    at = bass.ds(i * (2 * G) + (b * G + GP), G - GP)
                    nc.vector.tensor_tensor(rows[:, b, GP:], iota[:].unsqueeze(1).to_broadcast([P, G - GP, NKEY]),
                                            selt[:, 0, at].unsqueeze(2).to_broadcast([P, G - GP, NKEY]), ALU.is_equal).then_inc(rows_done, 1)
                    for t in range(G):
                        one = bass.ds(i * (2 * G) + (b * G + t), 1)
                        last = nc.vector.tensor_scalar(cols[:, b, t, :], iota[:], selt[:, 1, one], selt[:, 2, one],
                                                       ALU.is_equal, ALU.mult)
                    last.then_inc(cols_done, 1)

        @block.tensor
        def _(pe):
            for w in range(3):
                for t in range(TT):
                    last = nc.tensor.transpose(t_ps[:, w * T + t * P:w * T + (t + 1) * P], sel[:, w, t, :], K.ident[:])
                last.then_inc(tr_done, 1)
            pe.sem_inc(g_done, 2)
            with pe.Fori(0, T // (2 * G)) as i:
                for b in range(2):
                    pe.wait_ge(rows_near, i * 2 + b + 1)
                    pe.wait_ge(rows_done, i * 2 + b + 1)
                    pe.wait_ge(cols_done, i * 2 + b + 1)
                    pe.wait_ge(g_stored, i * 2 + b + 1)
                    for t in range(G):
                        last = nc.tensor.matmul(g_ps[:, b * 1024 + t * P:b * 1024 + (t + 1) * P], rows[:, b, t, :], cols[:, b, t, :],
                                                start=True, stop=True)
                    last.then_inc(g_done, 1)

        @block.scalar
        def _(act):
            act.sem_inc(g_stored, 2)

            def group(i, n, par, b):
                act.wait_ge(g_done, i + 3)
                nc.scalar.activation(slab[:, par, :, bass.ds(n * G, G)].rearrange("p i t -> p t i"),
                                     g_ps[:, b * 1024:b * 1024 + G * P].rearrange("p (t i) -> p t i", t=G),
                                     ACT.Copy).then_inc(g_stored, 1)

            for tt in range(TT):
                par = tt % 2
                if tt >= 2:
                    act.wait_ge(slab_out[par], 16)
                with act.Fori(0, groups // 2) as i:
                    for b in range(2):
                        group(i * 2 + (tt * groups + b), i * 2 + b, par, b)
                act.wait_ge(g_stored, (tt + 1) * groups + 2)
                act.dma_start(gates[tt], slab[:, par].rearrange("p i t -> p (i t)")).then_inc(slab_out[par], 16)
            for s in slab_out:
                act.wait_ge(s, 32)


def peer_experts(nc, K, d, gates):
    J = 4
    with Phase(nc, "experts") as ph:
        R = 4
        hp = ph.sb("h_parts", [P, 2, KT, T], F32R)
        u_raw = ph.sb("u_raw", [P, R, KT * P])
        v_raw = ph.sb("v_raw", [P, R, D])
        slab = ph.sb("slab", [P, R, TT, P])
        up = ph.sb("u_parts", [P, 2, 2, KT * P], F32R)
        vp = ph.sb("v_parts", [P, J, 2, D], F32R)
        act_sb = ph.sb("gelu", [P, 2, T])
        wact = ph.sb("wact", [P, 2, T])
        wp = ph.sb("wact_parts", [P, J, 2, T], F32R)
        acc = K.h
        MG = 4 * 24 // (NKEY // J)
        M = Modulation(nc, K, ph, d, 48, 4 * 24, MG, [(2, 48)])
        a_ps = ph.banks("a_ps", 4)
        o_ps = ph.banks("o_ps", 4)
        u_in = ph.sems(*[f"u_in{i}" for i in range(R)])
        g_in = ph.sems(*[f"g_in{i}" for i in range(R)])
        v_in = ph.sems(*[f"v_in{i}" for i in range(R)])
        (h_hi, h_lo, u_hi, u_lo, v_hi, v_lo, a_done, gelu_done, w_done, w_hi, w_lo, o_done, acc_done, v) = ph.sems(
            "h_hi", "h_lo", "u_hi", "u_lo", "v_hi", "v_lo", "a_done", "gelu_done", "weighted_done", "w_hi", "w_lo",
            "o_done", "acc_done", "v")
        block = ph.block()
        groups = NKEY // J
        g_h = gates.rearrange("b p (i t) -> i p b t", t=P)

        @block.sync
        def _(sp):
            for s in range(R):
                sp.dma_start(u_raw[:, s, :], d["peer_u"][s]).then_inc(u_in[s], 16)
                sp.dma_start(slab[:, s], g_h[s]).then_inc(g_in[s], 16)
            with sp.Fori(0, groups - 1) as i:
                for s in range(R):
                    sp.wait_ge(u_lo, i * R + (s + 1))
                    sp.dma_start(u_raw[:, s, :], d["peer_u"][i * R + (s + R)]).then_inc(u_in[s], 16)
                    sp.wait_ge(w_done, i * R + (s + 3))
                    sp.dma_start(slab[:, s], g_h[i * R + (s + R)]).then_inc(g_in[s], 16)

        @block.gpsimd
        def _(g):
            g.dma_start(M.rows[:, 0, :], d["c_rows"][2].partition_broadcast(P)).then_inc(M.rows_in, 16)
            for s in range(R):
                g.dma_start(v_raw[:, s, :], d["peer_v"][s]).then_inc(v_in[s], 16)
            for s in range(MG):
                g.dma_start(M.ring[:, s, :], d["w_mod"][48 + s]).then_inc(M.ready[s], 16)
            M.start_mul(g, nc.gpsimd)

            def modulation(i, last):
                for s in range(MG):
                    M.multiply(g, nc.gpsimd, i * MG + s, s, i * 16)
                    if not last:
                        g.wait_ge(M.multiplied, i * MG + (s + 1))
                        g.dma_start(M.ring[:, s, :], d["w_mod"][i * MG + (s + 48 + MG)]).then_inc(M.ready[s], 16)

            with g.Fori(0, groups - 1) as i:
                for s in range(R):
                    g.wait_ge(v_lo, i * R + (s + 1))
                    g.dma_start(v_raw[:, s, :], d["peer_v"][i * R + (s + R)]).then_inc(v_in[s], 16)
                modulation(i, False)
            modulation(groups - 1, True)
            M.finish(g, nc.gpsimd)

        @block.tensor
        def _(pe):
            pe.sem_inc(a_done, 2)
            pe.sem_inc(o_done, 1)

            def h_wait(k):
                pe.wait_ge(h_lo, k + 1)

            def values(i, k, js):
                b = k % 4
                for j in js:
                    if k == 0:
                        pe.wait_ge(v_lo, i * J + (j + 1))
                        pe.wait_ge(w_lo, i * J + (j + 3))
                    last = parts_product(nc, o_ps[:, b * T:(b + 1) * T], lambda a, _: vp[:, j, a, k * P:(k + 1) * P],
                                         lambda a, _: wp[:, j, a, :], (0,), j == 0, j == J - 1)
                return last

            with pe.Fori(0, groups) as i:
                for j in range(J):
                    pe.wait_ge(u_lo, i * J + (j + 1))
                    pe.wait_ge(gelu_done, i * J + (j + 1))
                    parts_product(nc, a_ps[:, j * T:(j + 1) * T], lambda a, k: up[:, j % 2, a, k * P:(k + 1) * P],
                                  lambda a, k: hp[:, a, k, :], range(KT), True, True, h_wait if j == 0 else None).then_inc(a_done, 1)
                pe.wait_ge(acc_done, i * KT + 3)
                for k in range(3):
                    values(i, k, range(J - 1))
                for k in range(3):
                    values(i, k, (J - 1,)).then_inc(o_done, 1)
                for k in range(3, KT):
                    pe.wait_ge(acc_done, i * KT + (k + 1))
                    values(i, k, range(J)).then_inc(o_done, 1)

        def groups_of(st, per, body):
            st.loop(groups - 1, per, lambda i: body(i, False))
            body(groups - 1, True)

        @block.scalar
        def _(act):
            A = nc.scalar.activation
            act.sem_inc(gelu_done, 4)
            act.sem_inc(w_hi, 2)

            def u_high(i, j):
                act.wait_ge(u_in[j % R], i * 16 + 16 * (j // R + 1))
                act.wait_ge(a_done, i * J + (j + 1))
                A(up[:, j % 2, 0, :], u_raw[:, j % R, :], ACT.Copy).then_inc(u_hi, 1)

            def group(i, last):
                for j in range(J):
                    if not (last and j == J - 1):
                        u_high(i, j + 1)
                    act.wait_ge(v_in[j], i * 16 + 16)
                    act.wait_ge(o_done, i * KT + 1)
                    A(vp[:, j, 0, :], v_raw[:, j, :], ACT.Copy).then_inc(v_hi, 1)
                    act.wait_ge(a_done, i * J + (j + 3))
                    act.wait_ge(w_done, i * J + (j + 1))
                    A(act_sb[:, j % 2, :], a_ps[:, j * T:(j + 1) * T], ACT.Gelu).then_inc(gelu_done, 1)
                    act.wait_ge(w_done, i * J + (j + 3))
                    A(wp[:, j, 0, :], wact[:, j % 2, :], ACT.Copy).then_inc(w_hi, 1)
                for s in range(MG):
                    M.sum(act, i * MG + s)

            for k in range(KT):
                A(hp[:, 0, k, :], K.h[:, k, :], ACT.Copy).then_inc(h_hi, 1)
            u_high(0, 0)
            M.start_act(act)
            groups_of(Steps(act, v), 0, group)

        @block.vector
        def _(dve):
            V = nc.vector
            st = Steps(dve, v)
            dve.sem_inc(acc_done, 4)
            dve.sem_inc(w_done, 2)
            dve.sem_inc(w_lo, 2)
            for k in range(KT):
                dve.wait_ge(h_hi, k + 1)
                V.tensor_tensor(hp[:, 1, k, :], K.h[:, k, :], hp[:, 0, k, :].bitcast(F32), ALU.subtract).then_inc(h_lo, 1)
            dve.wait_ge(h_lo, KT)

            def u_low(i, j):
                dve.wait_ge(u_hi, i * J + (j + 1))
                V.tensor_tensor(up[:, j % 2, 1, :], u_raw[:, j % R, :], up[:, j % 2, 0, :].bitcast(F32), ALU.subtract).then_inc(u_lo, 1)

            def group(i, last):
                for j in range(J):
                    if not (last and j == J - 1):
                        u_low(i, j + 1)
                    dve.wait_ge(v_hi, i * J + (j + 1))
                    V.tensor_tensor(vp[:, j, 1, :], v_raw[:, j, :], vp[:, j, 0, :].bitcast(F32), ALU.subtract).then_inc(v_lo, 1)
                    dve.wait_ge(gelu_done, i * J + (j + 5))
                    dve.wait_ge(g_in[j], i * 16 + 16)
                    dve.wait_ge(w_hi, i * J + (j + 1))
                    dve.wait_ge(w_lo, i * J + (j + 1))
                    V.tensor_tensor(wact[:, j % 2, :], act_sb[:, j % 2, :], slab[:, j].rearrange("p b t -> p (b t)"),
                                    ALU.mult).then_inc(w_done, 1)
                    dve.wait_ge(w_hi, i * J + (j + 3))
                    dve.wait_ge(w_done, i * J + (j + 3))
                    V.tensor_tensor(wp[:, j, 1, :], wact[:, j % 2, :], wp[:, j, 0, :].bitcast(F32), ALU.subtract).then_inc(w_lo, 1)
                for k in range(KT):
                    dve.wait_ge(o_done, i * KT + (k + 2))
                    dve.wait_ge(acc_done, i * KT + 4)
                    V.tensor_tensor(acc[:, k, :], acc[:, k, :], o_ps[:, (k % 4) * T:(k % 4 + 1) * T], ALU.add).then_inc(acc_done, 1)

            st.then(V.memset(acc[:], 0.0))
            u_low(0, 0)
            groups_of(st, 0, group)
            dve.wait_ge(acc_done, groups * KT + 4)
            for k in range(KT):
                st.do(V.scalar_tensor_tensor(out=K.x[:, k, :], in0=acc[:, k, :], scalar=K.mod[:, 40 + k:41 + k],
                                             in1=K.x[:, k, :], op0=ALU.mult, op1=ALU.add))
            dve.wait_ge(M.v, 1)
            for s in range(4):
                st.do(V.tensor_scalar(K.ops[:, s, :], K.mod[:, 48 + 24 * s + 8:48 + 24 * s + 24], 1.0, None, ALU.add))
            st.sync()


def peer(nc, K, d):
    gates = nc.dram_tensor("peer_gates", (TT, P, NKEY * P), F32, kind="Internal").ap()
    with nc.sbuf_tensor("sel", [P, 3, TT, P], F32) as sel:
        peer_route(nc, K, d, sel)
        peer_gates(nc, K, d, sel, gates)
    peer_experts(nc, K, d, gates)


def lay_out_peer(w):
    u = w["peer_u"][0].reshape(NKEY, NKEY, KT, P)
    return {
        "peer_keys": np.ascontiguousarray(np.stack([w["peer_k1"][0].T, w["peer_k2"][0].T], 1)),
        "peer_wq": _tiles(w["peer_wq"][0]),
        "peer_u": np.ascontiguousarray(u.transpose(1, 3, 2, 0)).reshape(NKEY, P, D),
        "peer_v": np.ascontiguousarray(w["peer_v"][0].reshape(NKEY, NKEY, D).transpose(1, 0, 2)),
    }


def modulate(nc, K, s):
    at = 48 + 24 * s
    with Phase(nc, f"modulate{s}") as ph:
        a, v = ph.sems("a", "v")
        block = ph.block()

        @block.scalar
        def _(act):
            for k in range(0, KT, 2):
                nc.scalar.activation(K.h[:, k, :], K.x[:, k, :], ACT.Identity, scale=K.ops[:, s, k:k + 1],
                                     bias=K.mod[:, at + k:at + k + 1]).then_inc(a, 1)
            act.wait_ge(a, KT // 2)

        @block.vector
        def _(dve):
            for k in range(1, KT, 2):
                nc.vector.tensor_scalar(K.h[:, k, :], K.x[:, k, :], K.ops[:, s, k:k + 1], K.mod[:, at + k:at + k + 1],
                                        ALU.mult, ALU.add).then_inc(v, 1)
            dve.wait_ge(v, KT // 2)


def residual_alpha(nc, K, s, bias=None):
    def act_step(i, bank, buf):
        xk = K.x[:, bass.ds(i, 1), :].squeeze(1)
        if bias is None:
            return nc.scalar.activation(buf, xk, ACT.Copy, scale=ALPHA)
        return nc.scalar.activation(buf, xk, ACT.Identity, scale=ALPHA, bias=bias[:, bass.ds(i, 1)])

    def dve_step(st, i, bank, buf):
        xk = K.x[:, bass.ds(i, 1), :].squeeze(1)
        return nc.vector.scalar_tensor_tensor(out=xk, in0=bank, scalar=K.ops[:, s, bass.ds(i + 8, 1)], in1=buf,
                                              op0=ALU.mult, op1=ALU.add)
    return act_step, dve_step, 0


def mlp(nc, K, d, l, then):
    s = 2 * l + 1
    b1 = VEC["mlp_b1"][0] + 32 * l
    b2 = VEC["mlp_b2"][0] + 8 * l
    HT = FF // P // 2
    recycle(nc)
    modulate(nc, K, s)
    with ExitStack() as c:
        hp = c.enter_context(nc.sbuf_tensor(f"h_parts{l}", [P, 2, KT, T], F32R))
        hidden = c.enter_context(nc.sbuf_tensor(f"hidden{l}", [P, 2, HT, T], F32R))
        gb2 = c.enter_context(nc.sbuf_tensor(f"gb2_{l}", [P, KT], F32))

        def square(st, i, bank, buf):
            hi, lo = [hidden[:, a, bass.ds(i, 1), :].squeeze(1) for a in range(2)]
            st.then(nc.vector.tensor_tensor(buf, buf, buf, ALU.mult))
            st.then(nc.vector.tensor_copy(hi, buf))
            return nc.vector.tensor_tensor(lo, buf, hi.bitcast(F32), ALU.subtract)

        gated_bias(nc, K, f"gb{l}", gb2, s, b2)
        for half in range(2):
            def relu(i, bank, buf):
                return nc.scalar.activation(buf, bank, ACT.Relu, bias=K.vec[:, bass.ds(i + (b1 + half * HT), 1)])

            linear_phase(nc, K, f"mlp1_{l}{half}", lambda n: d[f"mlp_w1_{l}"][n + half * HT], None if half else K.h, HT,
                         (relu, square, 2), parts=hp, then=lambda n: d[f"mlp_w2_{l}"][half, n])
            linear_phase(nc, K, f"mlp2_{l}{half}", lambda n: d[f"mlp_w2_{l}"][half, n], None, KT,
                         residual(K, K.ops[:, s, 8:16]) if half else residual_alpha(nc, K, s, gb2), chunks=2, parts=hidden, then=then if half else lambda n: d[f"mlp_w1_{l}"][n + HT])
    g, b = VEC["ln_ffn_g"][0] + 8 * l, VEC["ln_ffn_b"][0] + 8 * l
    norm_phase(nc, K, f"ln_ffn{l}", [(K.x, K.x, T, K.vec[:, g:g + KT], K.vec[:, b:b + KT])], center=True)


def gated_bias(nc, K, name, out, s, b):
    with Phase(nc, name) as ph:
        v = ph.sems("v")
        block = ph.block()

        @block.vector
        def _(dve):
            nc.vector.tensor_tensor(out[:], K.ops[:, s, 8:16], K.vec[:, b:b + KT], ALU.mult).then_inc(v, 1)
            dve.wait_ge(v, 1)


TWO_PI = 2 * math.pi
C1 = 6.28125
C2 = float(np.float32(round((TWO_PI - C1) * 2 ** 22) / 2 ** 22))
C3 = float(np.float32(TWO_PI - C1 - C2))
PI_IN = 3.1415925


def reduce_angle(V, st, ang, n):
    st.then(V.tensor_scalar(n, ang, 1.0 / TWO_PI, ROUNDMAGIC, ALU.mult, ALU.add))
    st.then(V.tensor_scalar(n, n, ROUNDMAGIC, None, ALU.subtract))
    for c in (C1, C2, C3):
        st.then(V.scalar_tensor_tensor(out=ang, in0=n, scalar=-c, in1=ang, op0=ALU.mult, op1=ALU.add))


def quarter_turn(V, st, out, ang, n):
    st.then(V.tensor_scalar(out, ang, math.pi / 2, None, ALU.add))
    st.then(V.tensor_scalar(n, out, math.pi, None, ALU.is_gt))
    st.then(V.scalar_tensor_tensor(out=out, in0=n, scalar=-TWO_PI, in1=out, op0=ALU.mult, op1=ALU.add))
    st.then(V.tensor_scalar(out, out, PI_IN, -PI_IN, ALU.min, ALU.max))


QN = 192 ** -0.5


def mla(nc, K, d):
    load_ahead(nc, K, "mla_ahead", lambda n: d["mla_wo"][n])
    modulate(nc, K, 0)
    with ExitStack() as c:
        cq = c.enter_context(nc.sbuf_tensor("cq", [P, 2, T], F32))
        ckv = c.enter_context(nc.sbuf_tensor("ckv", [P, T], F32))
        kpe = c.enter_context(nc.sbuf_tensor("kpe", [P, T], F32))
        csq = c.enter_context(nc.sbuf_tensor("csq", [P, T], F32))
        mla_in(nc, K, d, cq, ckv, kpe, csq)
        mla_heads(nc, K, d, cq, ckv, kpe, csq)
    linear_phase(nc, K, "mla_out", lambda n: d["mla_wo"][n], K.h, KT, residual_alpha(nc, K, 0), then=lambda n: d["mlp_w1_0"][n])
    g, b = VEC["ln_mix_g"][0], VEC["ln_mix_b"][0]
    norm_phase(nc, K, "ln_mix0", [(K.x, K.x, T, K.vec[:, g:g + KT], K.vec[:, b:b + KT])], center=True)


def mla_in(nc, K, d, cq, ckv, kpe, csq):
    with Phase(nc, "mla_in") as ph:
        ring = ph.sb("ring", [P, 5, KT * P])
        pos = ph.sb("pos", [P, T], I32)
        ang = ph.sb("ang", [P, T])
        ang2 = ph.sb("ang2", [P, T])
        n = ph.sb("n", [P, T])
        zsq = ph.sb("zsq", [P, 3, T])
        rstd = ph.sb("rstd", [P, 2, T])
        z = ph.banks("z", 5)
        sums = ph.banks("sums", 2)
        w_in = ph.sems(*[f"w_in{i}" for i in range(5)])
        pos_in, z_done, v, ang_done, trig_done, sq_done, sum_done, rstd_done, a = ph.sems(
            "pos_in", "z_done", "v", "angle_done", "trig_done", "sq_done", "sum_done", "rstd_done", "a")
        block = ph.block()
        fq, sg = VEC["inv_freq"][0], VEC["rope_sign"][0]
        qn, kvn = VEC["q_norm"][0], VEC["kv_norm"][0]

        @block.sync
        def _(sp):
            sp.dma_start(pos[:], d["positions"].partition_broadcast(P)).then_inc(pos_in, 16)
            for t in range(5):
                sp.dma_start(ring[:, t, :], d["mla_win"][t]).then_inc(w_in[t], 16)

        @block.tensor
        def _(pe):
            for t in range(5):
                pe.wait_ge(w_in[t], 16)
                for k in range(KT):
                    last = nc.tensor.matmul(z[:, t * T:(t + 1) * T], ring[:, t, k * P:(k + 1) * P], K.h[:, k, :],
                                            start=k == 0, stop=k == KT - 1)
                last.then_inc(z_done, 1)
            pe.wait_ge(sq_done, 3)
            nc.tensor.matmul(sums[:, 0:T], K.ones[:], zsq[:, 0, :], start=True, stop=False)
            nc.tensor.matmul(sums[:, 0:T], K.ones[:], zsq[:, 1, :], start=False, stop=True)
            nc.tensor.matmul(sums[:, T:2 * T], K.ones[:], zsq[:, 2, :], start=True, stop=True).then_inc(sum_done, 1)

        @block.scalar
        def _(act):
            st = Steps(act, a)
            act.wait_ge(ang_done, 2)
            nc.scalar.activation(ang[:], ang[:], ACT.Sin).then_inc(trig_done, 1)
            nc.scalar.activation(ang2[:], ang2[:], ACT.Sin).then_inc(trig_done, 1)
            for t in range(3):
                act.wait_ge(z_done, t + 1)
                nc.scalar.activation(zsq[:, t, :], z[:, t * T:(t + 1) * T], ACT.Square).then_inc(sq_done, 1)
            act.wait_ge(sum_done, 1)
            st.do(nc.scalar.activation(rstd[:, 0, :], sums[:, 0:T], ACT.Ln, scale=1.0 / 256, bias=EPS))
            st.then(nc.scalar.activation(rstd[:, 1, :], sums[:, T:2 * T], ACT.Ln, scale=1.0 / 128, bias=EPS))
            nc.scalar.activation(rstd[:], rstd[:], ACT.Exp, scale=-0.5).then_inc(rstd_done, 1)

        @block.vector
        def _(dve):
            V = nc.vector
            st = Steps(dve, v)
            dve.wait_ge(pos_in, 16)
            st.then(V.tensor_copy(ang[:], pos[:]))
            st.then(V.tensor_scalar(ang[:], ang[:], K.vec[:, fq:fq + 1], None, ALU.mult))
            reduce_angle(V, st, ang[:], n[:])
            quarter_turn(V, st, ang2[:], ang[:], n[:])
            V.tensor_scalar(ang[:], ang[:], PI_IN, -PI_IN, ALU.min, ALU.max).then_inc(ang_done, 2)
            dve.wait_ge(trig_done, 2)
            st.then(V.tensor_scalar(ang[:], ang[:], K.vec[:, sg:sg + 1], None, ALU.mult))
            st.do(V.tensor_copy(csq[0:64, :], ang2[0:64, :]))
            st.do(V.tensor_copy(csq[64:128, :], ang[64:128, :]))
            dve.wait_ge(z_done, 5)
            st.do(V.tensor_tensor(n[:], ang2[:], z[:, 3 * T:4 * T], ALU.mult))
            st.then(V.tensor_tensor(kpe[:], ang[:], z[:, 4 * T:5 * T], ALU.mult))
            st.do(V.tensor_tensor(kpe[:], kpe[:], n[:], ALU.add))
            dve.wait_ge(rstd_done, 1)
            for t in range(3):
                out = cq[:, t, :] if t < 2 else ckv[:]
                g = K.vec[:, qn + t:qn + t + 1] if t < 2 else K.vec[:, kvn:kvn + 1]
                st.do(V.scalar_tensor_tensor(out=out, in0=z[:, t * T:(t + 1) * T], scalar=g, in1=rstd[:, t // 2, :],
                                             op0=ALU.mult, op1=ALU.mult))
            st.sync()


def mla_heads(nc, K, d, cq, ckv, kpe, csq):
    W = 2 * 256 + 128 + 128
    with Phase(nc, "mla") as ph:
        wts = ph.sb("wts", [P, 2, W])
        qn = ph.sb("qn", [P, 2, T])
        qp = ph.sb("qp", [P, 2, T])
        kn = ph.sb("kn", [P, 2, T])
        vt = ph.sb("vt", [P, 2, TT, P])
        big = ph.sb("mask", [P, TT * P])
        prob = ph.sb("prob", [P, 2, T])
        probt = ph.sb("probt", [P, 2, T])
        stat = ph.sb("stat", [P, 2, 3])
        sm = ph.sb("rowsum", [P, 2, 1])
        pr = ph.banks("proj", 4)
        sc = ph.banks("score", 2)
        tr = ph.banks("trans")
        op = ph.banks("out")
        w_ready = ph.sems("w_ready0", "w_ready1")
        (p_done, q_stored, qp_stored, s_done, masked, max_done, exp_done, prob_done, t_done, t_stored, o_done, o_stored,
         cst, v) = ph.sems("proj_done", "q_stored", "qpe_stored", "score_done", "masked", "max_done", "exp_done", "prob_done",
                           "trans_done", "trans_stored", "out_done", "out_stored", "consts", "v")
        block = ph.block()
        H = 8

        @block.gpsimd
        def _(g):
            nc.gpsimd.memset(big[:], 0.0).then_inc(cst, 1)
            g.wait_ge(cst, 1)
            nc.gpsimd.affine_select(out=big[:], in_=big[:], compare_op=ALU.is_ge, fill=-1.0e30, base=(TT - 1) * P,
                                    pattern=[[-1, TT * P]], channel_multiplier=1).then_inc(cst, 1)

        @block.sync
        def _(sp):
            for b in range(2):
                sp.dma_start(wts[:, b, :], d["mla_wh"][b]).then_inc(w_ready[b], 16)
            with sp.Fori(0, H // 2 - 1) as i:
                for b in range(2):
                    sp.wait_ge(p_done, i * 4 + 2 * b + 2)
                    sp.dma_start(wts[:, b, :], d["mla_wh"][i * 2 + (b + 2)]).then_inc(w_ready[b], 16)

        @block.tensor
        def _(pe):
            def project(i, b):
                pe.wait_ge(w_ready[b], i * 16 + 16)
                if b:
                    pe.wait_ge(q_stored, i * 6 + 3)
                    pe.wait_ge(qp_stored, i * 2 + 1)
                else:
                    pe.wait_ge(q_stored, i * 6)
                    pe.wait_ge(qp_stored, i * 2)
                for o, c in ((0, 0), (1, P)):
                    for k in range(2):
                        nc.tensor.matmul(pr[:, o * T:(o + 1) * T], wts[:, b, k * 256 + c:k * 256 + c + P], cq[:, k, :],
                                         start=k == 0, stop=k == 1)
                nc.tensor.matmul(pr[:, 2 * T:3 * T], wts[:, b, 512:640], ckv[:], start=True, stop=True).then_inc(p_done, 1)
                for t in range(TT):
                    last = nc.tensor.matmul(pr[:, 3 * T + t * P:3 * T + (t + 1) * P], ckv[:, t * P:(t + 1) * P], wts[:, b, 640:768],
                                            start=True, stop=True)
                last.then_inc(p_done, 1)

            def scores(i, b, qt):
                n = i * 8 + (b * 4 + qt)
                if qt == 0:
                    pe.wait_ge(q_stored, i * 6 + 3 * b + 3)
                    pe.wait_ge(qp_stored, i * 2 + b + 1)
                pe.wait_ge(masked, n + 1)
                o = (qt % 2) * T
                w = (qt + 1) * P
                nc.tensor.matmul(sc[:, o:o + w], qn[:, b, qt * P:w], kn[:, b, 0:w], start=True, stop=False)
                nc.tensor.matmul(sc[:, o:o + w], qp[:, b, qt * P:w], kpe[:, 0:w], start=False, stop=True).then_inc(s_done, 1)

            def weigh(i, b, qt):
                n = i * 8 + (b * 4 + qt)
                pe.wait_ge(prob_done, n + 1)
                pe.wait_ge(t_stored, n + 1)
                for k in range(qt + 1):
                    last = nc.tensor.transpose(tr[:, k * P:(k + 1) * P], prob[:, qt % 2, k * P:(k + 1) * P], K.ident[:])
                last.then_inc(t_done, 1)

            def output(i, b, qt):
                n = i * 8 + (b * 4 + qt)
                pe.wait_ge(t_stored, n + 2)
                if qt == 0:
                    pe.wait_ge(o_stored, i * 2 + b + 1)
                for k in range(qt + 1):
                    last = nc.tensor.matmul(op[:, qt * P:(qt + 1) * P], vt[:, b, k, :], probt[:, qt % 2, k * P:(k + 1) * P],
                                            start=k == 0, stop=k == qt)
                last.then_inc(o_done, 1)

            pe.sem_inc(t_done, 2)
            pe.sem_inc(o_done, 1)
            project(0, 0)
            scores(0, 0, 0)

            def head(i, b, nxt):
                scores(i, b, 1)
                weigh(i, b, 0)
                scores(i, b, 2)
                if nxt:
                    project(*nxt)
                output(i, b, 0)
                weigh(i, b, 1)
                scores(i, b, 3)
                output(i, b, 1)
                weigh(i, b, 2)
                if nxt:
                    scores(*nxt, 0)
                output(i, b, 2)
                weigh(i, b, 3)
                output(i, b, 3)

            with pe.Fori(0, H // 2 - 1) as i:
                head(i, 0, (i, 1))
                head(i, 1, (i + 1, 0))
            head(H // 2 - 1, 0, (H // 2 - 1, 1))
            head(H // 2 - 1, 1, None)

        @block.scalar
        def _(act):
            def store(i, b):
                act.wait_ge(p_done, i * 4 + 2 * b + 1)
                nc.scalar.activation(qn[:, b, :], pr[:, 0:T], ACT.Copy).then_inc(q_stored, 1)
                nc.scalar.activation(kn[:, b, :], pr[:, 2 * T:3 * T], ACT.Copy).then_inc(q_stored, 1)
                act.wait_ge(p_done, i * 4 + 2 * b + 2)
                nc.scalar.activation(vt[:, b], pr[:, 3 * T:4 * T].rearrange("p (t v) -> p t v", t=TT), ACT.Copy).then_inc(q_stored, 1)

            def exp(i, b, qt):
                n = i * 8 + (b * 4 + qt)
                w = (qt + 1) * P
                act.wait_ge(max_done, n + 1)
                nc.scalar.activation(prob[:, qt % 2, 0:w], prob[:, qt % 2, 0:w], ACT.Exp, scale=QN,
                                     bias=stat[:, qt % 2, 1:2], accum_out=sm[:, qt % 2, :]).then_inc(exp_done, 1)

            def store_t(i, b, qt):
                n = i * 8 + (b * 4 + qt)
                w = (qt + 1) * P
                act.wait_ge(t_done, n + 3)
                if qt >= 2:
                    act.wait_ge(o_done, n)
                else:
                    act.wait_ge(o_done, i * 8 + b * 4 + 1)
                nc.scalar.activation(probt[:, qt % 2, 0:w], tr[:, 0:w], ACT.Copy).then_inc(t_stored, 1)

            def head(i, b, nxt):
                exp(i, b, 1)
                store_t(i, b, 0)
                exp(i, b, 2)
                if nxt:
                    store(*nxt)
                store_t(i, b, 1)
                exp(i, b, 3)
                store_t(i, b, 2)
                if nxt:
                    exp(*nxt, 0)
                store_t(i, b, 3)
                act.wait_ge(o_done, i * 8 + b * 4 + 5)
                nc.scalar.activation(K.h[:, bass.ds(i * 2 + b, 1), :].squeeze(1), op[:, 0:T], ACT.Copy).then_inc(o_stored, 1)

            act.sem_inc(t_stored, 1)
            act.sem_inc(o_stored, 1)
            store(0, 0)
            exp(0, 0, 0)
            with act.Fori(0, H // 2 - 1) as i:
                head(i, 0, (i, 1))
                head(i, 1, (i + 1, 0))
            head(H // 2 - 1, 0, (H // 2 - 1, 1))
            head(H // 2 - 1, 1, None)
            act.wait_ge(o_stored, H + 1)

        @block.vector
        def _(dve):
            V = nc.vector
            st = Steps(dve, v)
            dve.wait_ge(cst, 2)
            dve.sem_inc(masked, 2)

            def store(i, b):
                dve.wait_ge(p_done, i * 4 + 2 * b + 1)
                V.tensor_tensor(qp[:, b, :], csq[:], pr[:, T:2 * T], ALU.mult).then_inc(qp_stored, 1)

            def logits(i, b, qt):
                n = i * 8 + (b * 4 + qt)
                w = (qt + 1) * P
                dve.wait_ge(s_done, n + 1)
                dve.wait_ge(t_done, n + 1)
                V.tensor_tensor(prob[:, qt % 2, 0:w], big[:, (TT - 1 - qt) * P:TT * P], sc[:, (qt % 2) * T:(qt % 2) * T + w],
                                ALU.add).then_inc(masked, 1)
                dve.wait_ge(masked, n + 3)
                st.then(V.reduce_max(stat[:, qt % 2, 0:1], prob[:, qt % 2, 0:w], AXX))
                V.tensor_scalar(stat[:, qt % 2, 1:2], stat[:, qt % 2, 0:1], -QN, None, ALU.mult).then_inc(max_done, 1)

            def normalize(i, b, qt):
                n = i * 8 + (b * 4 + qt)
                w = (qt + 1) * P
                dve.wait_ge(exp_done, n + 1)
                st.then(V.reciprocal(stat[:, qt % 2, 2:3], sm[:, qt % 2, :]))
                V.tensor_scalar(prob[:, qt % 2, 0:w], prob[:, qt % 2, 0:w], stat[:, qt % 2, 2:3], None, ALU.mult).then_inc(prob_done, 1)

            def head(i, b, nxt):
                logits(i, b, 1)
                normalize(i, b, 0)
                logits(i, b, 2)
                normalize(i, b, 1)
                if nxt:
                    store(*nxt)
                logits(i, b, 3)
                normalize(i, b, 2)
                if nxt:
                    logits(*nxt, 0)
                normalize(i, b, 3)

            store(0, 0)
            logits(0, 0, 0)
            n0 = st.n
            with dve.Fori(0, H // 2 - 1) as i:
                st.turn = i * 16
                head(i, 0, (i, 1))
                head(i, 1, (i + 1, 0))
            assert st.n - n0 == 16, st.n - n0
            st.n, st.turn = n0 + 16 * (H // 2 - 1), 0
            head(H // 2 - 1, 0, (H // 2 - 1, 1))
            head(H // 2 - 1, 1, None)


def lay_out_mla(w):
    wi = w["mla_w_in_2"][0]
    x1, x2 = wi[:, 384:416], wi[:, 416:448]
    wi = np.concatenate([wi[:, 0:384], x1, x2, x1, x2, x2, x1, x2, x1], 1)
    qb = w["mla_w_qb_2"][0].reshape(256, 8, 192)
    qb = np.concatenate([qb, qb[:, :, 160:192], qb[:, :, 128:160]], 2)
    kvb = w["mla_w_kvb_2"][0].reshape(128, 8, 256)
    wh = np.concatenate([qb[0:128].transpose(1, 0, 2), qb[128:256].transpose(1, 0, 2), kvb.transpose(1, 0, 2)], 2)
    return {"mla_win": _tiles(wi), "mla_wh": np.ascontiguousarray(wh), "mla_wo": _tiles(w["mla_w_o_2"][0]),
            "positions": np.asarray(w["positions_2"]).reshape(T)}


def lay_out_rest(w):
    a = {}
    for l in range(2):
        a[f"mlp_w1_{l}"] = _tiles(w["mlp_w1_2"][l])
        w2 = _tiles(w["mlp_w2_2"][l]).reshape(KT, P, 4, D)
        a[f"mlp_w2_{l}"] = np.ascontiguousarray(w2.transpose(2, 0, 1, 3)).reshape(2, 2, KT, P, D).transpose(0, 2, 1, 3, 4).reshape(2, 2 * KT, P, D)
    return a


LB, LA = 32, 16
NST = 32


def ssm(nc, K, d):
    modulate(nc, K, 2)
    with ExitStack() as c:
        def keep(name, shape):
            return c.enter_context(nc.sbuf_tensor(name, shape, F32))

        u = keep("ssm_u", [P, KT, T])
        g = keep("ssm_g", [P, KT, T])

        def store(st, i, bank, buf):
            return nc.vector.tensor_copy(u[:, bass.ds(i, 1), :].squeeze(1), bank)

        linear_phase(nc, K, "ssm_in", lambda n: d["ssm_win"][n], K.h, KT, (None, store, 0), then=lambda n: d["ssm_wglu"][n])
        with ExitStack() as c2:
            S = Consts()
            S.mag = c2.enter_context(nc.sbuf_tensor("s_mag", [P, NST], F32))
            S.cb = c2.enter_context(nc.sbuf_tensor("s_cb", [P, 2, NST, LB], F32))
            S.ca = c2.enter_context(nc.sbuf_tensor("s_ca", [P, 2, NST, LA], F32))
            S.bd = c2.enter_context(nc.sbuf_tensor("s_bd", [P, 2, NST, 32], F32))
            S.cd = c2.enter_context(nc.sbuf_tensor("s_cd", [P, 3, NST, 32], F32))
            ssm_tables(nc, K, d, S)
            ssm_scan(nc, K, d, S, u, g)
        bg = VEC["b_glu"][0]

        def gate(i, bank, buf):
            return nc.scalar.activation(buf, bank, ACT.Sigmoid, bias=K.vec[:, bass.ds(i + bg, 1)])

        def times(st, i, bank, buf):
            return nc.vector.tensor_tensor(u[:, bass.ds(i, 1), :].squeeze(1), buf, g[:, bass.ds(i, 1), :].squeeze(1), ALU.mult)

        linear_phase(nc, K, "glu", lambda n: d["ssm_wglu"][n], g, KT, (gate, times, 0), then=lambda n: d["ssm_wout"][n])
        linear_phase(nc, K, "ssm_out", lambda n: d["ssm_wout"][n], u, KT, residual_alpha(nc, K, 2), then=lambda n: d["mlp_w1_1"][n])
    gg, bb = VEC["ln_mix_g"][0] + 8, VEC["ln_mix_b"][0] + 8
    norm_phase(nc, K, "ln_mix1", [(K.x, K.x, T, K.vec[:, gg:gg + KT], K.vec[:, bb:bb + KT])], center=True)


def ssm_tables(nc, K, d, S):
    with Phase(nc, "tables") as ph:
        prm = ph.sb("prm", [P, 3, NST])
        bc = ph.sb("bc", [P, 4, NST, 16])
        w = ph.sb("w", [P, 14, NST])
        bb = ph.sb("bb", [P, 2, NST, 16])
        t1 = ph.sb("t1", [P, NST, 16])
        steps = ph.sb("steps", [P, LB])
        ang = ph.sb("ang", [P, NST, LB])
        ang2 = ph.sb("ang2", [P, NST, LB])
        n = ph.sb("n", [P, NST, LB])
        zeroed = ph.sems("zeroed")
        prm_in, cst, dt_done, mag_in, mag_done, ang_done, trig_done, v = ph.sems(
            "prm_in", "consts", "dt_done", "mag_arg", "mag_done", "angle_done", "trig_done", "v")
        block = ph.block()

        @block.sync
        def _(sp):
            sp.dma_start(prm[:], d["ssm_prm"]).then_inc(prm_in, 16)
            sp.dma_start(bc[:], d["ssm_bc"]).then_inc(prm_in, 16)

        @block.gpsimd
        def _(g):
            nc.gpsimd.memset(S.bd[:], 0.0).then_inc(zeroed, 1)
            nc.gpsimd.memset(S.cd[:], 0.0).then_inc(zeroed, 1)
            nc.gpsimd.iota(steps[:], [[1, LB]], base=0, channel_multiplier=0,
                           allow_small_or_imprecise_dtypes=True).then_inc(cst, 1)

        @block.scalar
        def _(act):
            act.wait_ge(prm_in, 32)
            nc.scalar.activation(w[:, 0, :], prm[:, 2, :], ACT.Exp).then_inc(dt_done, 1)
            act.wait_ge(mag_in, 1)
            nc.scalar.activation(S.mag[:], w[:, 1, :], ACT.Exp).then_inc(mag_done, 1)
            act.wait_ge(ang_done, 1)
            nc.scalar.activation(w[:, 4:6, :], w[:, 4:6, :], ACT.Sin).then_inc(trig_done, 1)
            for m, (t, l) in enumerate(((S.cb, LB), (S.ca, LA))):
                act.wait_ge(ang_done, m + 2)
                nc.scalar.activation(t[:, 1], ang[:, :, 0:l], ACT.Sin)
                nc.scalar.activation(t[:, 0], ang2[:, :, 0:l], ACT.Sin).then_inc(trig_done, 1)

        @block.vector
        def _(dve):
            V = nc.vector
            st = Steps(dve, v)
            lr, li = prm[:, 0, :], prm[:, 1, :]
            dt, m, th, th32, sn, cs, are, aim, den, rden, cre, cim, ta, tb = [w[:, k, :] for k in
                                                                            (0, 1, 2, 3, 4, 5, 6, 7, 8, 9, 10, 11, 12, 13)]
            dve.wait_ge(dt_done, 1)
            V.tensor_tensor(m, lr, dt, ALU.mult).then_inc(mag_in, 1)
            st.then(V.tensor_tensor(th, li, dt, ALU.mult))
            reduce_angle(V, st, th, ta)
            st.then(V.tensor_scalar(th, th, PI_IN, -PI_IN, ALU.min, ALU.max))
            st.then(V.tensor_scalar(th32, th, float(LB), None, ALU.mult))
            reduce_angle(V, st, th32, ta)
            quarter_turn(V, st, cs, th, ta)
            V.tensor_copy(sn, th).then_inc(ang_done, 1)
            dve.wait_ge(trig_done, 1)
            dve.wait_ge(mag_done, 1)
            st.then(V.tensor_tensor(are, S.mag[:], cs, ALU.mult))
            st.then(V.tensor_tensor(aim, S.mag[:], sn, ALU.mult))
            st.then(V.tensor_scalar(are, are, -1.0, None, ALU.add))
            st.do(V.tensor_tensor(ta, lr, lr, ALU.mult))
            st.then(V.tensor_tensor(tb, li, li, ALU.mult))
            st.then(V.tensor_tensor(den, ta, tb, ALU.add))
            st.then(V.reciprocal(rden, den))
            for out, x, y, op in ((cre, (are, lr), (aim, li), ALU.add), (cim, (aim, lr), (are, li), ALU.subtract)):
                st.do(V.tensor_tensor(ta, *x, ALU.mult))
                st.then(V.tensor_tensor(tb, *y, ALU.mult))
                st.then(V.tensor_tensor(out, ta, tb, op))
                st.then(V.tensor_tensor(out, out, rden, ALU.mult))

            def wide(x):
                return x.unsqueeze(2).to_broadcast([P, NST, 16])
            br, bi = bc[:, 0], bc[:, 1]
            for k, (x, y, op) in enumerate((((br, cre), (bi, cim), ALU.subtract), ((bi, cre), (br, cim), ALU.add))):
                st.do(V.tensor_tensor(bb[:, k], x[0], wide(x[1]), ALU.mult))
                st.then(V.tensor_tensor(t1[:], y[0], wide(y[1]), ALU.mult))
                st.then(V.tensor_tensor(bb[:, k], bb[:, k], t1[:], op))
            dve.wait_ge(zeroed, 2)
            for k in range(2):
                for hf in range(2):
                    r, c = slice(64 * hf, 64 * hf + 64), slice(16 * hf, 16 * hf + 16)
                    st.do(V.tensor_copy(S.bd[r, k, :, c], bb[r, k]))
                    st.do(V.tensor_scalar(S.cd[r, k, :, c], bc[r, 2 + k], (1.0, -1.0)[k], None, ALU.mult))
                    if k == 0:
                        st.do(V.tensor_scalar(S.cd[r, 2, :, c], bc[r, 2], -1.0, None, ALU.mult))
            dve.wait_ge(cst, 1)
            for m_, (x, l) in enumerate(((th, LB), (th32, LA))):
                if m_:
                    dve.wait_ge(trig_done, 2)
                st.then(V.tensor_tensor(ang[:, :, 0:l], x.unsqueeze(2).to_broadcast([P, NST, l]),
                                        steps[:, 0:l].unsqueeze(1).to_broadcast([P, NST, l]), ALU.mult))
                reduce_angle(V, st, ang[:, :, 0:l], n[:, :, 0:l])
                quarter_turn(V, st, ang2[:, :, 0:l], ang[:, :, 0:l], n[:, :, 0:l])
                V.tensor_scalar(ang[:, :, 0:l], ang[:, :, 0:l], PI_IN, -PI_IN, ALU.min, ALU.max).then_inc(ang_done, 1)
            st.sync()


def ssm_scan(nc, K, d, S, u, g):
    with Phase(nc, "scan") as ph:
        bst = ph.sb("bst", [P, 2, P])
        bt = ph.sb("bt", [P, 2, 2, P])
        ust = ph.sb("ust", [P, 2, T])
        ct = ph.sb("ct", [P, 2, 3, 4, 32])
        rot = ph.sb("rot", [P, 4, 2, T])
        tmp = ph.sb("tmp", [P, 2, T])
        m = ph.sb("m", [P, 2, 2, T])
        bu = ph.sb("bu", [P, 2, T])
        wv = ph.sb("wv", [P, 2, T])
        pq = ph.sb("pq", [P, 2, 2, 2, T])
        yb = ph.sb("yb", [P, T])
        b_ps = ph.banks("b_ps")
        bu_ps = ph.banks("bu_ps", 4)
        y_ps = ph.banks("y_ps", 2)
        (b_staged, c_staged, bt_done, bt_stored, bu_done, bu_read, rot_done, rotated, y_done, yb_done, g_done, v, gp) = ph.sems(
            "b_staged", "c_staged", "bt_done", "bt_stored", "bu_done", "bu_read", "rot_done", "rotated_back", "y_done",
            "yb_done", "gelu_done", "v", "g")
        block = ph.block()
        dcol = VEC["ssm_d"][0]

        def turns(eng, st, per, body):
            n0 = st.n
            with eng.Fori(0, KT // 2 - 1) as i:
                st.turn = i * (2 * per) if per else 0
                body(i * 2, 0, False)
                body(i * 2 + 1, 1, False)
            assert st.n - n0 == 2 * per, (st.n - n0, per)
            st.n, st.turn = n0 + 2 * per * (KT // 2 - 1), 0
            body(KT - 2, 0, False)
            body(KT - 1, 1, True)

        @block.gpsimd
        def _(eng):
            st = Steps(eng, gp)
            G = nc.gpsimd

            def turn(i):
                for t in range(4):
                    b = t
                    eng.wait_ge(rotated, i * 4 + (t + 1))
                    ca = [S.ca[:, k, bass.ds(i * 4 + t, 1), :].squeeze(1).unsqueeze(2).to_broadcast([P, LA, LB]) for k in range(2)]
                    cb = [S.cb[:, k, bass.ds(i * 4 + t, 1), :].squeeze(1).unsqueeze(1).to_broadcast([P, LA, LB]) for k in range(2)]
                    r = [rot[:, b, k, :].rearrange("p (a b) -> p a b", b=LB) for k in range(2)]
                    q = [tmp[:, k, :].rearrange("p (a b) -> p a b", b=LB) for k in range(2)]
                    st.do(G.tensor_tensor(r[0], ca[0], cb[0], ALU.mult))
                    st.do(G.tensor_tensor(q[0], ca[1], cb[1], ALU.mult))
                    st.do(G.tensor_tensor(r[1], ca[1], cb[0], ALU.mult))
                    st.do(G.tensor_tensor(q[1], ca[0], cb[1], ALU.mult))
                    st.sync()
                    G.tensor_tensor(r[0], r[0], q[0], ALU.subtract).then_inc(rot_done, 1)
                    G.tensor_tensor(r[1], r[1], q[1], ALU.add).then_inc(rot_done, 1)
                    eng.wait_ge(rot_done, i * 8 + (2 * t + 2))
            st.loop(KT, 16, turn)

        @block.tensor
        def _(pe):
            def transposed(i, par):
                pe.wait_ge(b_staged, i + 1)
                if not isinstance(i, int) or i:
                    pe.wait_ge(bt_stored, i)
                for k in range(2):
                    last = nc.tensor.transpose(b_ps[:, k * P:(k + 1) * P], bst[:, k, :], K.ident[:])
                last.then_inc(bt_done, 1)

            def inputs(i, par, t):
                if t == 0:
                    pe.wait_ge(bt_stored, i + 1)
                pe.wait_ge(bu_read, i * 4 + (t + 1))
                r = slice(32 * t, 32 * t + 32)
                for k in range(2):
                    o = (2 * (t % 2) + k) * T
                    last = nc.tensor.matmul(bu_ps[:, o:o + T], bt[r, par, k, :], ust[r, par, :], start=True, stop=True)
                last.then_inc(bu_done, 1)

            def outputs(i, par, t):
                pe.wait_ge(rotated, i * 4 + (t + 5))
                if t == 0:
                    pe.wait_ge(c_staged, i + 1)
                    pe.wait_ge(yb_done, i + 1)
                for n, (mat, cs, w) in enumerate(((0, 0, 0), (2, 1, 1), (1, 0, 1), (1, 1, 0))):
                    last = nc.tensor.matmul(y_ps[32 * t:32 * t + 32, par * T:(par + 1) * T], ct[:, par, mat, t, :],
                                            pq[:, t % 2, cs, w, :], start=n == 0, stop=n == 3)
                last.then_inc(y_done, 1)

            def turn(i, par, last):
                for t in range(4):
                    if t < 2:
                        inputs(i, par, t + 2)
                    elif not last:
                        inputs(i + 1, 1 - par, t - 2)
                    if t == 1 and not last:
                        transposed(i + 1, 1 - par)
                    outputs(i, par, t)

            pe.sem_inc(y_done, 2)
            transposed(0, 0)
            inputs(0, 0, 0)
            inputs(0, 0, 1)
            turns(pe, Steps(pe, v), 0, turn)

        @block.scalar
        def _(act):
            def store(i, par):
                act.wait_ge(bt_done, i + 1)
                act.wait_ge(yb_done, i + 1)
                nc.scalar.activation(ust[:, par, :], u[:, bass.ds(i, 1), :].squeeze(1), ACT.Copy)
                nc.scalar.activation(bt[:, par], b_ps[:, 0:2 * P].rearrange("p (k s) -> p k s", k=2), ACT.Copy).then_inc(bt_stored, 1)

            def turn(i, par, last):
                if not last:
                    store(i + 1, 1 - par)
                act.wait_ge(yb_done, i + 3)
                nc.scalar.activation(g[:, bass.ds(i, 1), :].squeeze(1), yb[:], ACT.Gelu_apprx_tanh).then_inc(g_done, 1)

            act.sem_inc(g_done, 1)
            store(0, 0)
            turns(act, Steps(act, v), 0, turn)
            act.wait_ge(g_done, KT + 1)

        @block.vector
        def _(dve):
            V = nc.vector
            st = Steps(dve, v)

            def stage(i, par):
                if not isinstance(i, int) or i:
                    dve.wait_ge(bt_done, i)
                V.tensor_copy(bst[:].rearrange("p k (t c) -> p k t c", c=32), S.bd[:, :, bass.ds(i * 4, 4), :]).then_inc(b_staged, 1)
                V.tensor_copy(ct[:, par], S.cd[:, :, bass.ds(i * 4, 4), :]).then_inc(c_staged, 1)

            def turn_inputs(i, t):
                b = t % 2
                dve.wait_ge(bu_done, i * 4 + (t + 1))
                dve.wait_ge(rot_done, i * 8 + (2 * t + 2))
                both = bu_ps[:, 2 * b * T:(2 * b + 2) * T].rearrange("p (k t) -> p k t", k=2)
                st.do(V.tensor_tensor(m[:, 0], rot[:, t, 0:1, :].to_broadcast([P, 2, T]), both, ALU.mult))
                V.tensor_tensor(m[:, 1], rot[:, t, 1:2, :].to_broadcast([P, 2, T]), both, ALU.mult).then_inc(bu_read, 1)

            def scan(i, t):
                dve.wait_ge(bu_read, i * 4 + (t + 3))
                st.do(V.tensor_tensor(bu[:, 0, :], m[:, 0, 0, :], m[:, 1, 1, :], ALU.add))
                st.then(V.tensor_tensor(bu[:, 1, :], m[:, 0, 1, :], m[:, 1, 0, :], ALU.subtract))
                dve.wait_ge(rotated, i * 4 + (t + 4))
                mg = S.mag[:, bass.ds(i * 4 + t, 1)].to_broadcast([P, T])
                for k in range(2):
                    st.do(V.tensor_tensor_scan(wv[:, k, :], mg, bu[:, k, :], 0.0, ALU.mult, ALU.add))

            def turn_back(i, t):
                b = t % 2
                st.sync()
                dve.wait_ge(y_done, i * 4 + (t + 1))
                st.do(V.tensor_tensor(pq[:, b, 0], rot[:, t, 0:1, :].to_broadcast([P, 2, T]), wv[:], ALU.mult))
                V.tensor_tensor(pq[:, b, 1], rot[:, t, 1:2, :].to_broadcast([P, 2, T]), wv[:], ALU.mult).then_inc(rotated, 1)

            def finish(i, par):
                dve.wait_ge(y_done, i * 4 + 6)
                dve.wait_ge(g_done, i + 1)
                V.scalar_tensor_tensor(out=yb[:], in0=ust[:, par, :], scalar=K.vec[:, bass.ds(i + dcol, 1)],
                                       in1=y_ps[:, par * T:(par + 1) * T], op0=ALU.mult, op1=ALU.add).then_inc(yb_done, 1)

            def turn(i, par, last, first=False):
                for t in range(4):
                    at = (i, t + 1) if t < 3 else (i + 1, 0)
                    if t < 3 or not last:
                        turn_inputs(*at)
                    turn_back(i, t)
                    if t < 3 or not last:
                        scan(*at)
                    if t == 0:
                        if not first:
                            finish(i - 1, 1 - par)
                        if not last:
                            stage(i + 1, 1 - par)

            dve.sem_inc(rotated, 4)
            dve.sem_inc(yb_done, 2)
            dve.sem_inc(bu_read, 2)
            stage(0, 0)
            turn_inputs(0, 0)
            scan(0, 0)
            turn(0, 0, False, True)
            n0, per = st.n, 24
            with dve.Fori(0, KT // 2 - 1) as i:
                st.turn = i * (2 * per)
                turn(i * 2 + 1, 1, False)
                turn(i * 2 + 2, 0, False)
            assert st.n - n0 == 2 * per, st.n - n0
            st.n, st.turn = n0 + 2 * per * (KT // 2 - 1), 0
            turn(KT - 1, 1, True)
            finish(KT - 1, 1)


def lay_out_ssm(w):
    def states(v):
        v = np.asarray(v)
        return np.moveaxis(v.reshape((NST, P) + v.shape[2:]), 0, 1)
    ldt = np.broadcast_to(w["ssm_log_dt_2"][0][:, None], (64, 64))
    prm = np.stack([states(w["ssm_a_re_2"][0]), states(w["ssm_a_im_2"][0]), states(ldt)], 1)
    bc = np.stack([states(w["ssm_b_re_2"][0]), states(w["ssm_b_im_2"][0]),
                   states(w["ssm_c_re_2"][0].transpose(0, 2, 1)), states(w["ssm_c_im_2"][0].transpose(0, 2, 1))], 1)
    return {"ssm_prm": np.ascontiguousarray(prm), "ssm_bc": np.ascontiguousarray(bc), "ssm_win": _tiles(w["ssm_w_in_2"][0]),
            "ssm_wglu": _tiles(w["ssm_w_glu_2"][0]), "ssm_wout": _tiles(w["ssm_w_out_2"][0])}


class Consts:
    pass


def residual(K, gate):
    def step(st, i, bank, buf):
        xk = K.x[:, bass.ds(i, 1), :].squeeze(1)
        return K.nc.vector.scalar_tensor_tensor(out=xk, in0=bank, scalar=gate[:, bass.ds(i, 1)],
                                                    in1=xk, op0=ALU.mult, op1=ALU.add)
    return None, step, 0


def build(nc, d, out):
    SPENT.clear()
    with ExitStack() as ctx:
        K = Consts()
        K.nc = nc

        def keep(stack, name, shape, dt=F32):
            return stack.enter_context(nc.sbuf_tensor(name, shape, dt))

        K.x = keep(ctx, "x", [P, KT, T])
        K.h = keep(ctx, "h", [P, KT, T])
        K.vec = keep(ctx, "vec", [P, NVEC])
        K.mod = keep(ctx, "modv", [P, MOD_TILES + 16])
        K.ops = keep(ctx, "ops", [P, 4, 16])
        K.gs_mix = keep(ctx, "gs_mix", [P, KT])
        K.gs_ctx = keep(ctx, "gs_ctx", [P, KT])
        K.gs_ffn = keep(ctx, "gs_ffn", [P, KT])
        K.ones = keep(ctx, "ones", [P, P])
        K.ident = keep(ctx, "ident", [P, P])
        K.lb = keep(ctx, "lb", [P, 16])
        K.oml = keep(ctx, "oml", [P, 16])

        with ExitStack() as mix:
            y_hg = keep(mix, "y_hg", [P, HG_H, T])
            y_gla = K.x
            with ExitStack() as scan:
                K.hc = keep(scan, "hc", [P, KT, TC])
                K.segf = keep(scan, "segf", [P, T + TC])
                K.segb = keep(scan, "segb", [P, T + TC])
                K.tri = keep(scan, "tri", [CH, 2, CH])
                K.triu = keep(scan, "triu", [CH, 2, NCH, CH], U32)
                setup_and_modulation(nc, K, d)
                norm_phase(nc, K, "norm1", [(K.x, K.h, T, K.gs_mix, K.mod[:, 0:8]),
                                            (K.hc, K.hc, TC, K.gs_ctx, K.mod[:, MOD_TILES:MOD_TILES + 8])])
                g0, g1 = VEC["hgrn_norm_g"][0], VEC["gla_norm_g"][0]
                heads_phase(nc, K, d, "hgrn", d["w_hg"], HG_H, 1, K.vec[:, g0:g0 + 1], y_hg, 1.0)
                with nc.sbuf_tensor("log_gates", [P, 2 * GLA_H, T + TC], F32) as lg:
                    lora_gates(nc, K, d, lg)
                    heads_phase(nc, K, d, "gla", d["w_gla"], GLA_H, GLA_VT, K.vec[:, g1:g1 + 2], y_gla, 1.0 / 16.0, lg)
            recycle(nc)
            K.slots = WeightSlots(nc, mix, "out_slots")
            with nc.sbuf_tensor("merged", [P, KT, T], F32) as merged:
                with nc.sbuf_tensor("m_h_parts", [P, 2, KT, T], F32R) as hp, nc.sbuf_tensor("m_y_parts", [P, 2, KT, T], F32R) as yp:
                    merge_phase(nc, K, d, "merge_hg", 0, y_hg, hp, yp, merged)
                    merge_phase(nc, K, d, "merge_gla", 1, y_gla, hp, yp, merged)
                linear_phase(nc, K, "wo", lambda n: d["w_out"][n], merged, KT, residual(K, K.mod[:, 16:24]))
        recycle(nc)

        norm_phase(nc, K, "norm2", [(K.x, K.h, T, K.gs_ffn, K.mod[:, 24:32])])
        peer(nc, K, d)
        f = VEC["final_g"][0]
        norm_phase(nc, K, "normf", [(K.x, K.x, T, K.vec[:, f:f + KT], None)])
        recycle(nc)

        K.slots = WeightSlots(nc, ctx, "slots")
        mla(nc, K, d)
        mlp(nc, K, d, 0, lambda n: d["ssm_win"][n])
        recycle(nc)
        ssm(nc, K, d)
        mlp(nc, K, d, 1, None)
        store_out(nc, K.x, out)


def store_out(nc, x, out):
    with Phase(nc, "out") as ph:
        stored = ph.sems("stored")
        block = ph.block()

        @block.sync
        def _(sp):
            sp.dma_start(out.rearrange("(k p) t -> p k t", p=P), x[:, 0:KT, 0:T]).then_inc(stored, 16)
            sp.wait_ge(stored, 16)


def _tiles(w):
    k, m = w.shape
    return np.ascontiguousarray(w.reshape(k // P, P, m // P, P).transpose(2, 1, 0, 3).reshape(m // P, P, k))


def _cols(v):
    return np.asarray(v).reshape(-1, P).T


def lay_out(inp):
    w = {k: np.asarray(v) for k, v in inp.items()}
    a = {}
    a["xT"] = np.ascontiguousarray(w["x"][0].T)
    a["ctxT"] = np.ascontiguousarray(w["ctx"][0].T)
    inv = (np.float32(10000.0) ** (-np.arange(0, 64, 2, dtype=np.float32) / np.float32(64))).astype(np.float32)
    order = {
        "mod_b": np.concatenate([_cols(w["ada_b"][0]), _cols(w["mod_mix_b_2"][0]), _cols(w["mod_ffn_b_2"][0]),
                                 _cols(w["mod_mix_b_2"][1]), _cols(w["mod_ffn_b_2"][1])], 1),
        "norm_mix_g": _cols(w["norm_mix_g"][0]), "lb_logits": _cols(w["hgrn_lb_logits"].reshape(-1)),
        "hgrn_norm_g": _cols(w["hgrn_norm_g"][0]), "gk_b": _cols(w["gla_gk_b"][0].reshape(-1)),
        "gla_norm_g": _cols(w["gla_norm_g"][0]), "norm_ffn_g": _cols(w["norm_ffn_g"][0]), "final_g": _cols(w["final_g"]),
        "q_norm": _cols(w["mla_q_norm_2"][0]), "kv_norm": _cols(w["mla_kv_norm_2"][0]), "ssm_d": _cols(w["ssm_d_2"][0]),
        "b_glu": _cols(w["ssm_b_glu_2"][0]), "mlp_b1": _cols(w["mlp_b1_2"].reshape(-1)), "mlp_b2": _cols(w["mlp_b2_2"].reshape(-1)),
        "ln_mix_g": _cols(w["ln_mix_g_2"].reshape(-1)), "ln_mix_b": _cols(w["ln_mix_b_2"].reshape(-1)),
        "ln_ffn_g": _cols(w["ln_ffn_g_2"].reshape(-1)), "ln_ffn_b": _cols(w["ln_ffn_b_2"].reshape(-1)),
        "inv_freq": np.tile(inv, 4).reshape(P, 1),
        "rope_sign": np.where(np.arange(P) % 64 < 32, -1.0, 1.0).astype(np.float32).reshape(P, 1),
    }
    a["vec"] = np.ascontiguousarray(np.concatenate([order[n] for n, _ in VEC_SIZES], 1))
    a["w_mod"] = np.concatenate([m.T for m in (w["ada_w"][0], w["mod_mix_w_2"][0], w["mod_ffn_w_2"][0],
                                               w["mod_mix_w_2"][1], w["mod_ffn_w_2"][1])]).reshape(MOD_TILES, P, D)
    a["c_rows"] = np.stack([w["c"][0], w["c_ctx"], w["c_2"][0]])
    wi = w["w_in"][0]
    at = np.cumsum([0, 1024, 1024, 1024, 1024, 1024, 512, 512, 1024, 1024, 16, 16, 1024, 1024])
    hq, ff, fb, hi, hg, gq, gk, gv, gg, _, _, mh, mg = [wi[:, at[i]:at[i + 1]] for i in range(13)]
    t = {n: _tiles(x) for n, x in dict(hq=hq, ff=ff, fb=fb, hi=hi, hg=hg, gq=gq, gk=gk, gv=gv, gg=gg, mh=mh, mg=mg).items()}
    a["w_hg"] = np.stack([t["ff"], t["fb"], t["hi"], t["hq"], t["hg"]], 1).reshape(-1, P, D)
    a["w_gla"] = np.stack([t["gk"], t["gv"][0::2], t["gv"][1::2], t["gq"], t["gg"][0::2], t["gg"][1::2]], 1).reshape(-1, P, D)
    a["w_gr"] = np.ascontiguousarray(wi[:, at[9]:at[11]])
    a["gk_w"] = w["gla_gk_w"][0]
    a["w_merge"] = np.stack([np.stack([t["mh"], _tiles(w["w_branch_hgrn"][0])], 1),
                             np.stack([t["mg"], _tiles(w["w_branch_gla"][0])], 1)]).reshape(2, 2 * KT, P, D)
    a["w_out"] = _tiles(w["w_out"][0])
    a.update(lay_out_peer(w))
    a.update(lay_out_mla(w))
    a.update(lay_out_rest(w))
    a.update(lay_out_ssm(w))
    return a


def kernel(**inputs):
    import concourse.bacc as _bacc
    from concourse.bass_utils import run_bass_kernel_spmd as _run

    nc = _bacc.Bacc("TRN2", target_bir_lowering=False, num_devices=1)
    arrays = lay_out(inputs)
    d = {n: nc.dram_tensor(f"in_{n}", a.shape, mybir.dt.from_np(a.dtype), kind="ExternalInput").ap() for n, a in arrays.items()}
    out = nc.dram_tensor("out_0", (D, T), F32, kind="ExternalOutput").ap()
    build(nc, d, out)
    r = _run(nc, [{f"in_{n}": a for n, a in arrays.items()}], core_ids=[0])
    return np.ascontiguousarray(r.results[0]["out_0"].T)[None]
```
